# Optimizing a Trainium2 kernel written in Bass

```python
import jax, jax.numpy as jnp
from jax import lax
import numpy as np
import math

D_MODEL = 1024
BATCH = 1
SEQ = 256
DEPTH = 1

CHUNK = 64
CONV_DIM = D_MODEL
CONV_WIDTH = 31
GLA_HEADS = 4
GLA_DK = D_MODEL // 2
GLA_DV = D_MODEL
GLA_HK = GLA_DK // GLA_HEADS
GLA_HV = GLA_DV // GLA_HEADS
GATE_RANK = 16
GATE_TAU = 16.0
N_GROUPS = 8
EXPERTS_PER_GROUP = 8
N_EXPERTS = N_GROUPS * EXPERTS_PER_GROUP
TOP_K = 2
D_EXPERT = D_MODEL // 2
MOE_BLOCK = 128
LN_EPS = 1e-5
RMS_EPS = 1e-6
DEEPNORM_ALPHA = (2.0 * DEPTH) ** 0.25
DEEPNORM_BETA = (8.0 * DEPTH) ** -0.25
IN_SPLITS = (CONV_DIM, CONV_DIM, GLA_DK, GLA_DK, GLA_DV, GLA_DV, GATE_RANK, D_MODEL, D_MODEL)
D_IN_PROJ = sum(IN_SPLITS)


def layer_norm(x, g, b):
    xf = x.astype(jnp.float32)
    mu = jnp.mean(xf, axis=-1, keepdims=True)
    var = jnp.mean(jnp.square(xf - mu), axis=-1, keepdims=True)
    return ((xf - mu) * lax.rsqrt(var + LN_EPS) * g + b).astype(x.dtype)

def conv_module(a, g, conv_w, conv_b, ln_g, ln_b, w_co, b_co):
    u = a * jax.nn.sigmoid(g)
    u = lax.conv_general_dilated(
        u, conv_w[:, None, :].astype(u.dtype), window_strides=(1,),
        padding=[(CONV_WIDTH - 1, 0)],
        dimension_numbers=("NWC", "WIO", "NWC"),
        feature_group_count=CONV_DIM) + conv_b
    u = jax.nn.silu(layer_norm(u, ln_g, ln_b))
    return u @ w_co + b_co

def gla_branch(q, k, v, r, f_lr, w_gate_up, b_gate_up, norm_g, w_o):
    bsz, seq, _ = q.shape
    n_chunks = seq // CHUNK
    dt = q.dtype
    f32 = jnp.float32
    log_a = jax.nn.log_sigmoid((f_lr @ w_gate_up + b_gate_up).astype(f32)) / GATE_TAU

    def chunked(t, hd):
        return t.astype(f32).reshape(bsz, n_chunks, CHUNK, GLA_HEADS, hd)

    qc = chunked(q, GLA_HK) * (GLA_HK ** -0.5)
    kc = chunked(k, GLA_HK)
    vc = chunked(v, GLA_HV)
    cum = jnp.cumsum(chunked(log_a, GLA_HK), axis=2)
    cum_end = cum[:, :, -1:]
    k_dec = kc * jnp.exp(cum_end - cum)
    chunk_kv = jnp.einsum("bnchk,bnchv->nbhkv", k_dec, vc)
    chunk_decay = jnp.exp(cum_end[:, :, 0]).transpose(1, 0, 2, 3)

    def step(state, inp):
        dec, kv = inp
        state = dec[..., None] * state + kv
        return state, state

    s0 = jnp.zeros((bsz, GLA_HEADS, GLA_HK, GLA_HV), f32)
    _, states = lax.scan(step, s0, (chunk_decay, chunk_kv))
    o = jnp.einsum("bnchk,nbhkv->bnchv", qc, states).reshape(bsz, seq, GLA_HEADS, GLA_HV)
    o = o * lax.rsqrt(jnp.mean(jnp.square(o), axis=-1, keepdims=True) + RMS_EPS) * norm_g
    o = o * jax.nn.silu(r.astype(f32)).reshape(bsz, seq, GLA_HEADS, GLA_HV)
    return o.reshape(bsz, seq, GLA_DV).astype(dt) @ w_o

def hier_moe(x, w_rg, b_rg, w_re, b_re, w1, w3, w2):
    bsz, seq, d = x.shape
    n_tok = bsz * seq
    xt = x.reshape(n_tok, d)
    f32 = jnp.float32
    g_logits = (xt @ w_rg + b_rg).astype(f32)
    g_prob = jax.nn.softmax(g_logits, axis=-1)
    _, g_sel = lax.top_k(g_logits, 1)
    g_w = jnp.take_along_axis(g_prob, g_sel, axis=1)
    e_all = (xt @ w_re + b_re).astype(f32).reshape(n_tok, N_GROUPS, EXPERTS_PER_GROUP)
    e_logits = jnp.take_along_axis(e_all, g_sel[:, :, None], axis=1)[:, 0]
    top_v, top_i = lax.top_k(e_logits, TOP_K)
    weights = g_w * jax.nn.softmax(top_v, axis=-1)
    expert = g_sel * EXPERTS_PER_GROUP + top_i

    n_assign = n_tok * TOP_K
    flat_e = expert.reshape(-1)
    flat_tok = jnp.repeat(jnp.arange(n_tok, dtype=jnp.int32), TOP_K)
    flat_w = weights.reshape(-1)
    order = jnp.argsort(flat_e)
    se, st, sw = flat_e[order], flat_tok[order], flat_w[order]
    counts = jnp.bincount(flat_e, length=N_EXPERTS)
    starts = jnp.cumsum(counts) - counts
    pcounts = (counts + MOE_BLOCK - 1) // MOE_BLOCK * MOE_BLOCK
    pends = jnp.cumsum(pcounts)
    pstarts = pends - pcounts
    dest = pstarts[se] + (jnp.arange(n_assign) - starts[se])
    n_blocks = -(-n_assign // MOE_BLOCK) + N_EXPERTS
    n_slots = n_blocks * MOE_BLOCK
    slot_tok = jnp.zeros((n_slots,), jnp.int32).at[dest].set(st)
    slot_w = jnp.zeros((n_slots,), x.dtype).at[dest].set(sw.astype(x.dtype))
    block_e = jnp.minimum(
        jnp.searchsorted(pends, jnp.arange(n_blocks) * MOE_BLOCK, side="right"), N_EXPERTS - 1)
    xs = xt[slot_tok].reshape(n_blocks, MOE_BLOCK, d)

    def expert_block(args):
        xb, e = args
        hdn = jax.nn.silu(xb @ w1[e]) * (xb @ w3[e])
        return hdn @ w2[e]

    ys = lax.map(expert_block, (xs, block_e)).reshape(n_slots, d) * slot_w[:, None]
    out = jnp.zeros((n_tok, d), x.dtype).at[slot_tok].add(ys)
    return out.reshape(bsz, seq, d)

def first_inputs(seed: int = 0) -> dict:
    key = jax.random.key(seed)
    ks = jax.random.split(key, 26)
    L = DEPTH

    def nrm(k, shape, scale):
        return jax.random.normal(k, shape, jnp.float32) * scale

    return {
        "x": nrm(ks[0], (BATCH, SEQ, D_MODEL), 1.0),
        "w_in": nrm(ks[1], (L, D_MODEL, D_IN_PROJ), D_MODEL ** -0.5),
        "b_in": nrm(ks[2], (L, D_IN_PROJ), 0.02),
        "conv_w": nrm(ks[3], (L, CONV_WIDTH, CONV_DIM), CONV_WIDTH ** -0.5),
        "conv_b": nrm(ks[4], (L, CONV_DIM), 0.02),
        "conv_ln_g": 1.0 + nrm(ks[5], (L, CONV_DIM), 0.05),
        "conv_ln_b": nrm(ks[6], (L, CONV_DIM), 0.02),
        "w_conv_out": nrm(ks[7], (L, CONV_DIM, D_MODEL), CONV_DIM ** -0.5),
        "b_conv_out": nrm(ks[8], (L, D_MODEL), 0.02),
        "w_gate_up": nrm(ks[9], (L, GATE_RANK, GLA_DK), GATE_RANK ** -0.5),
        "b_gate_up": nrm(ks[10], (L, GLA_DK), 0.1),
        "gla_norm_g": 1.0 + nrm(ks[11], (L, GLA_HEADS, GLA_HV), 0.05),
        "w_gla_out": nrm(ks[12], (L, GLA_DV, D_MODEL), GLA_DV ** -0.5),
        "w_out": nrm(ks[13], (L, D_MODEL, D_MODEL), D_MODEL ** -0.5 * DEEPNORM_BETA),
        "b_out": nrm(ks[14], (L, D_MODEL), 0.02),
        "ln1_g": 1.0 + nrm(ks[15], (L, D_MODEL), 0.05),
        "ln1_b": nrm(ks[16], (L, D_MODEL), 0.02),
        "w_router_group": nrm(ks[17], (L, D_MODEL, N_GROUPS), D_MODEL ** -0.5),
        "b_router_group": nrm(ks[18], (L, N_GROUPS), 0.01),
        "w_router_expert": nrm(ks[19], (L, D_MODEL, N_EXPERTS), D_MODEL ** -0.5),
        "b_router_expert": nrm(ks[20], (L, N_EXPERTS), 0.01),
        "w1": nrm(ks[21], (L, N_EXPERTS, D_MODEL, D_EXPERT), D_MODEL ** -0.5),
        "w3": nrm(ks[22], (L, N_EXPERTS, D_MODEL, D_EXPERT), D_MODEL ** -0.5),
        "w2": nrm(ks[23], (L, N_EXPERTS, D_EXPERT, D_MODEL), D_EXPERT ** -0.5 * DEEPNORM_BETA),
        "ln2_g": 1.0 + nrm(ks[24], (L, D_MODEL), 0.05),
        "ln2_b": nrm(ks[25], (L, D_MODEL), 0.02),
    }

def first_block(x, w_in, b_in, conv_w, conv_b, conv_ln_g, conv_ln_b, w_conv_out, b_conv_out,
              w_gate_up, b_gate_up, gla_norm_g, w_gla_out, w_out, b_out, ln1_g, ln1_b,
              w_router_group, b_router_group, w_router_expert, b_router_expert,
              w1, w3, w2, ln2_g, ln2_b):
    split_points = np.cumsum(IN_SPLITS)[:-1].tolist()
    for l in range(DEPTH):
        h = x @ w_in[l] + b_in[l]
        conv_a, conv_g, q, k, v, r, f_lr, gate_a, gate_b = jnp.split(h, split_points, axis=-1)
        y_conv = conv_module(conv_a, conv_g, conv_w[l], conv_b[l], conv_ln_g[l], conv_ln_b[l],
                             w_conv_out[l], b_conv_out[l])
        y_gla = gla_branch(q, k, v, r, f_lr, w_gate_up[l], b_gate_up[l], gla_norm_g[l], w_gla_out[l])
        merged = jax.nn.sigmoid(gate_a) * y_conv + jax.nn.sigmoid(gate_b) * y_gla
        mix = merged @ w_out[l] + b_out[l]
        x = layer_norm(DEEPNORM_ALPHA * x + mix, ln1_g[l], ln1_b[l])
        ffn = hier_moe(x, w_router_group[l], b_router_group[l], w_router_expert[l],
                       b_router_expert[l], w1[l], w3[l], w2[l])
        x = layer_norm(DEEPNORM_ALPHA * x + ffn, ln2_g[l], ln2_b[l])
    return x


PLE_DIM = 256
EPS = 1e-6

LRU_WIDTH = 1024
LRU_BLOCKS = 8
LRU_BLOCK = LRU_WIDTH // LRU_BLOCKS
LRU_CONV = 4
LRU_C = 8.0

N_HEADS = 8
HEAD_DIM = 128
N_KV_HEADS = 2
GROUP = N_HEADS // N_KV_HEADS
ATTN_WIDTH = N_HEADS * HEAD_DIM
KV_WIDTH = N_KV_HEADS * HEAD_DIM
IDX_HEADS = 8
IDX_DIM = 64
TOPK_MAX = 256
Q_BLOCK = 128

N_BUCKETS = 32
MAX_DISTANCE = 128

D_FF = 3072
FFN_CONV = 3

IN_SPLITS_2 = (LRU_WIDTH, LRU_WIDTH, ATTN_WIDTH, KV_WIDTH, KV_WIDTH,
             IDX_HEADS * IDX_DIM, IDX_DIM, IDX_HEADS, D_MODEL, D_MODEL)
IN_WIDTH = sum(IN_SPLITS_2)


def _rmsnorm(x, g):
    x32 = x.astype(jnp.float32)
    y = x32 * lax.rsqrt(jnp.mean(x32 * x32, axis=-1, keepdims=True) + EPS)
    return (y * g.astype(jnp.float32)).astype(x.dtype)

def _split_cols(h):
    parts = []
    start = 0
    for n in IN_SPLITS_2:
        parts.append(h[..., start:start + n])
        start += n
    return parts

def _causal_dwconv(x, w, b):
    width = w.shape[0]
    s = x.shape[1]
    xp = jnp.pad(x, ((0, 0), (width - 1, 0), (0, 0)))
    y = b
    for j in range(width):
        y = y + xp[:, j:j + s] * w[j]
    return y

def _rg_lru(x, wa, ba, wx, bx, lam):
    b, s, _ = x.shape
    xb = x.reshape(b, s, LRU_BLOCKS, LRU_BLOCK)
    r = jax.nn.sigmoid(jnp.einsum('bsnc,ncd->bsnd', xb, wa).reshape(b, s, LRU_WIDTH) + ba)
    i = jax.nn.sigmoid(jnp.einsum('bsnc,ncd->bsnd', xb, wx).reshape(b, s, LRU_WIDTH) + bx)
    log_a = -LRU_C * r.astype(jnp.float32) * jax.nn.softplus(-lam.astype(jnp.float32))
    a = jnp.exp(log_a)
    mult = jnp.sqrt(-jnp.expm1(2.0 * log_a))
    u = mult * (i * x).astype(jnp.float32)

    def combine(left, right):
        a1, b1 = left
        a2, b2 = right
        return a1 * a2, a2 * b1 + b2

    _, h = lax.associative_scan(combine, (a, u), axis=1)
    return h.astype(x.dtype)

def _t5_bucket(dist):
    max_exact = N_BUCKETS // 2
    d_f = jnp.maximum(dist, 1).astype(jnp.float32)
    large = max_exact + (jnp.log(d_f / max_exact) / math.log(MAX_DISTANCE / max_exact)
                         * (N_BUCKETS - max_exact)).astype(jnp.int32)
    large = jnp.minimum(large, N_BUCKETS - 1)
    return jnp.where(dist < max_exact, dist, large)

def _dsa_attention(q, k, v, qi, ki, wi, rel_bias):
    b, s = q.shape[0], q.shape[1]
    n_blk = s // Q_BLOCK
    top_k = min(TOPK_MAX, s // 4)
    key_pos = jnp.arange(s, dtype=jnp.int32)
    q_pos = key_pos.reshape(n_blk, Q_BLOCK)
    ki32 = ki.astype(jnp.float32)

    def blockify(a):
        return jnp.moveaxis(a.reshape((b, n_blk, Q_BLOCK) + a.shape[2:]), 1, 0)

    def one_block(args):
        qb, qib, wib, tpos = args
        dots = jnp.einsum('bthd,bsd->bths', qib.astype(jnp.float32), ki32) * (IDX_DIM ** -0.5)
        score = jnp.einsum('bth,bths->bts', wib.astype(jnp.float32), jax.nn.relu(dots))
        causal = key_pos[None, :] <= tpos[:, None]
        score = jnp.where(causal[None], score, -jnp.inf)
        _, sel = lax.top_k(score, top_k)
        k_sel = jax.vmap(lambda kb, ib: kb[ib])(k, sel)
        v_sel = jax.vmap(lambda vb, ib: vb[ib])(v, sel)
        qg = qb.reshape(b, Q_BLOCK, N_KV_HEADS, GROUP, HEAD_DIM)
        logits = jnp.einsum('btngd,btknd->btngk', qg, k_sel).astype(jnp.float32) * (HEAD_DIM ** -0.5)
        dist = tpos[None, :, None] - sel
        bias = rel_bias[_t5_bucket(jnp.maximum(dist, 0))]
        bias = bias.reshape(b, Q_BLOCK, top_k, N_KV_HEADS, GROUP).transpose(0, 1, 3, 4, 2)
        logits = logits + bias.astype(jnp.float32)
        logits = jnp.where((dist >= 0)[:, :, None, None, :], logits, -jnp.inf)
        probs = jax.nn.softmax(logits, axis=-1).astype(v.dtype)
        o = jnp.einsum('btngk,btknd->btngd', probs, v_sel)
        return o.reshape(b, Q_BLOCK, N_HEADS, HEAD_DIM)

    out = lax.map(one_block, (blockify(q), blockify(qi), blockify(wi), q_pos))
    return jnp.moveaxis(out, 0, 1).reshape(b, s, ATTN_WIDTH)

def second_inputs(seed: int = 0) -> dict:
    key = jax.random.key(seed)
    ks = jax.random.split(key, 32)
    f32 = jnp.float32

    def nrm(k, shape, fan_in):
        return jax.random.normal(k, shape, f32) * (fan_in ** -0.5)

    def gain(k, shape):
        return 1.0 + 0.05 * jax.random.normal(k, shape, f32)

    def small(k, shape):
        return 0.01 * jax.random.normal(k, shape, f32)

    u = jax.random.uniform(ks[10], (DEPTH, LRU_WIDTH), f32, 0.9, 0.999)
    sa = u ** (1.0 / LRU_C)
    lru_lambda = jnp.log(sa) - jnp.log1p(-sa)

    return {
        'x': jax.random.normal(ks[0], (BATCH, SEQ, D_MODEL), f32),
        'p': jax.random.normal(ks[1], (DEPTH, BATCH, SEQ, PLE_DIM), f32),
        'mix_norm': gain(ks[2], (DEPTH, D_MODEL)),
        'w_in': nrm(ks[3], (DEPTH, D_MODEL, IN_WIDTH), D_MODEL),
        'lru_conv_w': nrm(ks[4], (DEPTH, LRU_CONV, LRU_WIDTH), LRU_CONV),
        'lru_conv_b': small(ks[5], (DEPTH, LRU_WIDTH)),
        'lru_wa': nrm(ks[6], (DEPTH, LRU_BLOCKS, LRU_BLOCK, LRU_BLOCK), LRU_BLOCK),
        'lru_ba': small(ks[7], (DEPTH, LRU_WIDTH)),
        'lru_wx': nrm(ks[8], (DEPTH, LRU_BLOCKS, LRU_BLOCK, LRU_BLOCK), LRU_BLOCK),
        'lru_bx': small(ks[9], (DEPTH, LRU_WIDTH)),
        'lru_lambda': lru_lambda,
        'q_norm': gain(ks[11], (DEPTH, HEAD_DIM)),
        'k_norm': gain(ks[12], (DEPTH, HEAD_DIM)),
        'rel_bias': 0.5 * jax.random.normal(ks[13], (N_BUCKETS, N_HEADS), f32),
        'w_lru_br': nrm(ks[14], (DEPTH, LRU_WIDTH, D_MODEL), LRU_WIDTH),
        'w_attn_br': nrm(ks[15], (DEPTH, ATTN_WIDTH, D_MODEL), ATTN_WIDTH),
        'w_out': nrm(ks[16], (DEPTH, D_MODEL, D_MODEL), D_MODEL),
        'ffn_norm': gain(ks[17], (DEPTH, D_MODEL)),
        'w_up': nrm(ks[18], (DEPTH, D_MODEL, 2 * D_FF), D_MODEL),
        'ffn_conv_w': nrm(ks[19], (DEPTH, FFN_CONV, D_FF), FFN_CONV),
        'ffn_conv_b': small(ks[20], (DEPTH, D_FF)),
        'w_down': nrm(ks[21], (DEPTH, D_FF, D_MODEL), D_FF),
        'ple_norm': gain(ks[22], (DEPTH, D_MODEL)),
        'w_ple_gate': nrm(ks[23], (DEPTH, D_MODEL, D_MODEL), D_MODEL),
        'w_ple_proj': nrm(ks[24], (DEPTH, PLE_DIM, D_MODEL), PLE_DIM),
    }

def second_block(x, p, mix_norm, w_in, lru_conv_w, lru_conv_b, lru_wa, lru_ba, lru_wx, lru_bx,
              lru_lambda, q_norm, k_norm, rel_bias, w_lru_br, w_attn_br, w_out, ffn_norm,
              w_up, ffn_conv_w, ffn_conv_b, w_down, ple_norm, w_ple_gate, w_ple_proj):
    b, s, _ = x.shape
    for l in range(DEPTH):
        xn = _rmsnorm(x, mix_norm[l])
        h = xn @ w_in[l]
        lru_x, lru_gate, q, k, v, qi, ki, wi, gate_a, gate_b = _split_cols(h)

        ua = _causal_dwconv(lru_x, lru_conv_w[l], lru_conv_b[l])
        ya = _rg_lru(ua, lru_wa[l], lru_ba[l], lru_wx[l], lru_bx[l], lru_lambda[l])
        ya = (ya * jax.nn.gelu(lru_gate)) @ w_lru_br[l]

        qh = _rmsnorm(q.reshape(b, s, N_HEADS, HEAD_DIM), q_norm[l])
        kh = _rmsnorm(k.reshape(b, s, N_KV_HEADS, HEAD_DIM), k_norm[l])
        vh = v.reshape(b, s, N_KV_HEADS, HEAD_DIM)
        qih = qi.reshape(b, s, IDX_HEADS, IDX_DIM)
        wih = wi * (IDX_HEADS ** -0.5)
        yb = _dsa_attention(qh, kh, vh, qih, ki, wih, rel_bias) @ w_attn_br[l]

        merged = jax.nn.sigmoid(gate_a) * ya + jax.nn.sigmoid(gate_b) * yb
        x = x + merged @ w_out[l]

        xn = _rmsnorm(x, ffn_norm[l])
        up = xn @ w_up[l]
        g_ffn = _causal_dwconv(up[..., :D_FF], ffn_conv_w[l], ffn_conv_b[l])
        x = x + (jax.nn.gelu(g_ffn) * up[..., D_FF:]) @ w_down[l]

        g_ple = jax.nn.sigmoid(_rmsnorm(x, ple_norm[l]) @ w_ple_gate[l])
        x = x + g_ple * (p[l] @ w_ple_proj[l])
    return x


def setup_inputs(seed=0):
    out = dict(first_inputs(seed))
    for name, value in second_inputs(seed + 1).items():
        if name != "x":
            out[name + "_2"] = value
    return out


def reference(
    x, w_in, b_in, conv_w, conv_b, conv_ln_g, conv_ln_b, w_conv_out, b_conv_out, w_gate_up,
    b_gate_up, gla_norm_g, w_gla_out, w_out, b_out, ln1_g, ln1_b, w_router_group,
    b_router_group, w_router_expert, b_router_expert, w1, w3, w2, ln2_g, ln2_b, p_2, mix_norm_2,
    w_in_2, lru_conv_w_2, lru_conv_b_2, lru_wa_2, lru_ba_2, lru_wx_2, lru_bx_2, lru_lambda_2,
    q_norm_2, k_norm_2, rel_bias_2, w_lru_br_2, w_attn_br_2, w_out_2, ffn_norm_2, w_up_2,
    ffn_conv_w_2, ffn_conv_b_2, w_down_2, ple_norm_2, w_ple_gate_2, w_ple_proj_2,
):
    x = first_block(
        x, w_in, b_in, conv_w, conv_b, conv_ln_g, conv_ln_b, w_conv_out, b_conv_out, w_gate_up,
        b_gate_up, gla_norm_g, w_gla_out, w_out, b_out, ln1_g, ln1_b, w_router_group,
        b_router_group, w_router_expert, b_router_expert, w1, w3, w2, ln2_g, ln2_b,
    )
    return second_block(
        x, p_2, mix_norm_2, w_in_2, lru_conv_w_2, lru_conv_b_2, lru_wa_2, lru_ba_2, lru_wx_2,
        lru_bx_2, lru_lambda_2, q_norm_2, k_norm_2, rel_bias_2, w_lru_br_2, w_attn_br_2,
        w_out_2, ffn_norm_2, w_up_2, ffn_conv_w_2, ffn_conv_b_2, w_down_2, ple_norm_2,
        w_ple_gate_2, w_ple_proj_2,
    )


_drawn_inputs = setup_inputs


def setup_inputs(seed=0):
    import zlib

    import numpy as np

    out = dict(_drawn_inputs(seed))
    spreads = {}
    factors = {'b_in': 3.885,
     'conv_b': 3.681,
     'conv_ln_g': 2.86,
     'conv_ln_b': 5.34,
     'b_conv_out': 4.132,
     'b_gate_up': 3.554,
     'gla_norm_g': 3.708,
     'b_router_group': 6.873,
     'b_router_expert': 7.423,
     'lru_conv_b_2': 4.165,
     'lru_ba_2': 64.0,
     'lru_bx_2': 43.147,
     'q_norm_2': 8.0,
     'k_norm_2': 8.0,
     'ffn_conv_b_2': 8.0,
     'ple_norm_2': 7.568}
    for name, (base, spread) in spreads.items():
        noise = np.random.default_rng([zlib.crc32(name.encode()), seed]).standard_normal(out[name].shape)
        drawn = base * np.exp(spread * noise) if base else spread * noise
        out[name] = __import__('jax').numpy.asarray(drawn.astype(out[name].dtype))
    for name, factor in factors.items():
        out[name] = (out[name] * factor).astype(out[name].dtype)
    return out
```

```python
from contextlib import ExitStack

import numpy as np

import concourse.bass as bass
from concourse import mybir

ALU = mybir.AluOpType
ACT = mybir.ActivationFunctionType
F32 = mybir.dt.float32
I32 = mybir.dt.int32
U32 = mybir.dt.uint32
AX_X = mybir.AxisListType.X

P = 128
T = 256
TT = T // P
D = 1024
DC = D // P
UNIT = 4096
RING = 6
ALPHA = 2.0 ** 0.25

CONV_W = 31
CHUNK = 64
NCH = T // CHUNK
H1, HK, HV = 4, 128, 256
RANK = 16
TAU = 16.0

NG, EPG = 8, 8
NE = NG * EPG
SMALL_LOADS = 7
CONSTS = 9
CAP = 32
ROUNDS = T // CAP
META = NE + 2

NH, NKV, HD = 8, 2, 128
QPK = NH // NKV
IH, ID = 8, 64
TOPK = 64
NB, MAXD = 32, 128
LRU_W = 4
FF = 3072
FFC = FF // P
FFN_W = 3
PLE = 256
FILL = -1.0e38
TAKEN = -3.0e38
HIDE = -1.0e30

COLS = {}
_n = 0
for _name, _w in (("b_conv_a", 8), ("b_conv_g", 8), ("b_q", 4), ("b_k", 4), ("b_r", 8), ("b_flr", 1),
                  ("b_ga", 8), ("b_gb", 8), ("conv_w", 8 * CONV_W), ("conv_b", 8), ("cln_g", 8), ("cln_b", 8),
                  ("b_co", 8), ("b_gate", 4), ("gla_g", 8), ("mix_norm", 8), ("lru_w", 8 * LRU_W),
                  ("lru_b", 8), ("lru_ba", 8), ("lru_bx", 8), ("lam", 8), ("q_norm", 1), ("k_norm", 1),
                  ("ffn_norm", 8), ("ffn_w", FFC * FFN_W), ("ffn_b", FFC), ("ple_norm", 8)):
    COLS[_name] = _n
    _n += _w
NCOLS = _n

def _tasks():
    names = []
    names += ["g0", "g1", "a0", "a1", "g2", "g3", "a2", "a3", "k0", "k1", "fl", "z0", "z1"]
    names += [f"v{u}_{t}" for u in range(2) for t in range(2)] + ["q0", "q1", "csum"]
    names += [f"r{j}" for j in range(4)] + ["csq", "kdt0", "kdt1"] + [f"kv{i}" for i in range(8)]
    names += [f"ga{j}" for j in range(4)] + [f"o{h}" for h in range(4)]
    names += [f"gb{j}" for j in range(4)] + ["osum0", "osum1"]
    names += [f"yc{j}" for j in range(4)] + [f"yg{j}" for j in range(4)]
    names += [f"mix{u}_{t}" for u in range(2) for t in range(2)]
    names += [f"x1t{j}" for j in range(4)] + ["lg", "pos"]
    first = list(names)
    n2 = [f"x2t{j}" for j in range(4)] + ["kiwi_k", "kiwi_w", "relb"]
    n2 += [f"lx{j}" for j in range(4)] + [f"lg_{j}" for j in range(4)]
    n2 += ["kk", "vv", "qi0", "qi1"]
    n2 += [f"lr{j}" for j in range(4)] + [f"li{j}" for j in range(4)]
    n2 += ["ksum"]
    n2 += [f"qq{j}" for j in range(4)] + [f"gc{j}" for j in range(4)]
    n2 += [f"dots{t}_{j}" for t in range(2) for j in range(4)]
    n2 += [f"qsum{j}" for j in range(4)]
    n2 += [f"ya{j}" for j in range(4)] + [f"gd{j}" for j in range(4)]
    for t in range(2):
        n2 += [f"log{t}_{j}" for j in range(4)]
    for t in range(2):
        n2 += [f"pt{t}_{s}_{k}" for s in range(t + 1) for k in range(2)] + [f"pv{t}_{k}" for k in range(2)]
    n2 += [f"yb{j}" for j in range(4)] + [f"mo{u}_{t}" for u in range(2) for t in range(2)]
    n2 += [f"x3t{j}" for j in range(4)]
    for i in range(6):
        n2 += [f"fg{i}_0", f"fg{i}_1", f"fu{i}_0", f"fu{i}_1"]
    n2 += [f"dn{u}_{t}" for u in range(2) for t in range(2)]
    n2 += [f"pp{u}_{t}" for u in range(2) for t in range(2)]
    n2 += [f"x4t{j}" for j in range(4)]
    n2 += [f"pg{u}_{t}" for u in range(2) for t in range(2)]
    return first, n2


TASKS1, TASKS2 = _tasks()
TASK = {name: i for i, name in enumerate(TASKS1 + TASKS2)}

UNITS1 = ["g1", "a1", "g3", "a3", "k1", "v0_1", "v1_1", "q1", "r1", "r3", "ga1", "ga3", "gb1", "gb3",
          "yc1", "yc3", "yg1", "yg3", "mix0_1", "mix1_1"]
UNITS2 = (["lx1", "lx3", "lg_1", "lg_3", "vv", "qi1", "li3", "qq1", "qq3", "gc1", "gc3", "ya1", "ya3",
           "gd1", "gd3", "yb1", "yb3", "mo0_1", "mo1_1"]
          + [f"f{x}{i}_1" for i in range(6) for x in "gu"]
          + ["dn0_1"] * 3 + ["dn1_1"] * 3 + ["pp1_1", "pg0_1", "pg1_1"])
EXPERT_SLOT0 = len(UNITS1) % RING


def build(nc, a, out):
    with ExitStack() as ctx:
        def sb(name, shape, dt=F32):
            return ctx.enter_context(nc.sbuf_tensor(name, shape, dt))

        sems = {}

        def S(name):
            if name not in sems:
                sems[name] = ctx.enter_context(nc.semaphore(name))
            return sems[name]

        banks = [ctx.enter_context(nc.psum_tensor(f"bank{i}", [P, 512], F32)) for i in range(8)]
        ring = sb("ring", [P, RING, UNIT])
        slab = sb("slab", [P, 11, 2048])
        rows = sb("rows", [P, 3, D])
        cols = sb("cols", [P, NCOLS])
        w_flr = sb("w_flr", [P, DC, RANK])
        w_route = sb("w_route", [P, DC, NG + NE])
        b_route = sb("b_route", [P, NG + NE])
        ident = sb("ident", [P, P])
        ones = sb("ones", [P, P])
        before = sb("before", [P, P])
        stack = sb("stack", [P, CAP])
        slots = sb("slots", [P, P])
        slots_i = sb("slots_i", [P, P], I32)
        numbers = sb("numbers", [P, NE])
        numbers_i = sb("numbers_i", [P, NE], I32)
        eps_ln = sb("eps_ln", [P, 1])
        eps_rms = sb("eps_rms", [P, 1])
        small = sb("small", [P, 192])
        meta = sb("meta", [P, META, 4])
        g_top = sb("g_top", [P, TT, 8])
        g_idx = sb("g_idx", [P, TT, 8], U32)
        e_top = sb("e_top", [P, TT, 8])
        e_idx = sb("e_idx", [P, TT, 8], U32)
        over = sb("over", [P, 1], I32)
        bias_dram = nc.dram_tensor("bias_scratch", (NH, 512), F32, kind="Internal").ap()

        def col(name, i=0):
            return cols[:, COLS[name] + i:COLS[name] + i + 1]

        def chan(s):
            return slab[:, s, :].rearrange("p (c t) -> p c t", c=DC)

        def tok(s):
            return slab[:, s, :].rearrange("p (t d) -> p t d", t=TT)

        def half(s, h):
            return slab[:, s, 1024 * h:1024 * h + 1024].rearrange("p (c t) -> p c t", c=4)

        xg = slab[:, 1, 0:DC * CAP].rearrange("p (c s) -> p c s", c=DC)
        g_sb = slab[:, 1, 512:1024]
        u_sb = slab[:, 1, 1024:1536]
        silu_sb = slab[:, 1, 1536:1664].rearrange("p (c s) -> p c s", c=4)
        h_sb = slab[:, 1, 1664:1792].rearrange("p (c s) -> p c s", c=4)
        y_sb = tok(2)
        spread = slab[:, 3, 0:512].rearrange("p (a t) -> p a t", a=2)
        sel = slab[:, 3, 512:640].rearrange("p (a t s) -> p a t s", a=2, t=TT)
        selw = slab[:, 3, 1024:1536].rearrange("p (a t s) -> p a t s", a=2, t=TT)
        meta_f = slab[:, 3, 640:648].rearrange("p (a b) -> p a b", a=2)
        zeros = slab[:, 4, 0:512]
        logit = slab[:, 5, 0:TT * 72].rearrange("p (t n) -> p t n", t=TT)
        mask = slab[:, 5, 256:256 + TT * NE].rearrange("p (t n) -> p t n", t=TT)
        mask_a = slab[:, 5, 384:384 + TT * NE].rearrange("p (t n) -> p t n", t=TT)
        mask_b = slab[:, 5, 512:512 + TT * NE].rearrange("p (t n) -> p t n", t=TT)
        picked = slab[:, 5, 640:640 + TT * 64].rearrange("p (t i g) -> p t i g", t=TT, i=EPG)
        e_log = slab[:, 5, 768:768 + TT * 8].rearrange("p (t n) -> p t n", t=TT)
        onehot = slab[:, 5, 784:784 + TT * 8].rearrange("p (t n) -> p t n", t=TT)
        e_exp = slab[:, 5, 800:800 + TT * 8].rearrange("p (t n) -> p t n", t=TT)
        kT = slab[:, 7, 0:512].rearrange("p (h t) -> p h t", h=NKV)
        v2 = slab[:, 7, 512:1024].rearrange("p (t n) -> p t n", t=TT)
        qiT = slab[:, 7, 1024:2048].rearrange("p (c t) -> p c t", c=4)
        kiT = slab[:, 8, 0:256]
        score = slab[:, 8, 256:768].rearrange("p (t s) -> p t s", t=TT)
        work = slab[:, 8, 768:1280].rearrange("p (t s) -> p t s", t=TT)
        k_sq = slab[:, 8, 1280:1792]
        wih = slab[:, 8, 1792:1808].rearrange("p (t h) -> p t h", t=TT)
        best = slab[:, 8, 1808:1816]
        lgt = slab[:, 4, :].rearrange("p (h s) -> p h s", h=NH)
        prob_t = slab[:, 5, :].rearrange("p (s h t) -> p s h t", s=TT, h=NH)
        hT = slab[:, 1:4, :].rearrange("p a (c t) -> p (a c) t", c=DC)
        turn_ = [banks[(TASK["pos"] + 1 + i) % 8] for i in range(8)]
        acc = [turn_[0:2], turn_[2:4]]
        gate_bank, up_bank, y_bank, gather_bank = turn_[4:8]

        def states(n, h):
            i = n * H1 + h
            return slab[:, 8 + i // 8, HV * (i % 8):HV * (i % 8) + HV]

        mean = slab[:, 10, 768:1024]
        slotted = slab[:, 5, 896:1024]

        def indexer_head(j, m):
            return 4 * (j // 2) + j % 2 + 2 * m

        def bank(task):
            return banks[TASK[task] % 8]

        def take_bank(task):
            if TASK[task] >= 8:
                nc.tensor.wait_ge(S(f"bank_read{TASK[task] % 8}"), TASK[task] // 8)
            return bank(task)

        def full(ins, task):
            ins.then_inc(S(f"bank_full{TASK[task] % 8}"), 1)

        def wait_full(eng, task):
            eng.wait_ge(S(f"bank_full{TASK[task] % 8}"), TASK[task] // 8 + 1)
            return bank(task)

        def read(ins, task):
            ins.then_inc(S(f"bank_read{TASK[task] % 8}"), 1)

        def wait_read(eng, *tasks):
            for task in tasks:
                eng.wait_ge(S(f"bank_read{TASK[task] % 8}"), TASK[task] // 8 + 1)

        def expert_slot(q, w):
            return (EXPERT_SLOT0 + 3 * q + w) % RING

        block = ctx.enter_context(nc.Block())

        @block.sync
        def _(sp):
            sp.dma_start(slab[:, 0, :], a["xT"]).then_inc(S("xt_landed"), 16)
            sp.dma_start(cols[:], a["cols"]).then_inc(S("cols_landed"), 16)
            for n, _task in enumerate(UNITS1):
                if n >= RING:
                    wait_full(sp, UNITS1[n - RING])
                sp.dma_start(ring[:, n % RING, :], a["units1"][n]).then_inc(S(f"unit_landed{n % RING}"), 16)

            def expert_unit(e, q, w):
                name = ("w1", "w3", "w2")[w]
                src = a[name][bass.ds(e, 1) if not isinstance(e, int) else slice(e, e + 1)]
                src = src.rearrange("e (p c) n -> p (e c n)", p=P)
                sp.dma_start(ring[:, expert_slot(q, w), :], src).then_inc(S(f"expert_landed{3 * q + w}"), 16)

            used = ("gate_full", "up_full", "y1_full")

            def expert_pair(it, r):
                for q in range(2):
                    for w in range(3):
                        sp.wait_ge(S(used[w]), r * NE + 2 * it + q - 1)
                        expert_unit(2 * it + q, q, w)

            for q in range(2):
                for w in range(3):
                    wait_full(sp, UNITS1[len(UNITS1) - RING + 3 * q + w])
                    expert_unit(q, q, w)
            with sp.Fori(1, NE // 2) as it:
                expert_pair(it, 0)
            wait_read(sp, "pos")
            more = sp.value_load(over[0:1, 0:1], min_val=0, max_val=1)
            with sp.If(more > 0):
                with sp.Fori(1, ROUNDS) as r:
                    with sp.Fori(0, NE // 2) as it:
                        expert_pair(it, r)
                for w in range(3):
                    sp.wait_ge(S(used[w]), ROUNDS * NE)
            for n, _task in enumerate(UNITS2):
                if n < RING:
                    sp.wait_ge(S(used[n % 3]), NE - 1 + n // 3)
                else:
                    wait_full(sp, UNITS2[n - RING])
                s = (EXPERT_SLOT0 + n) % RING
                sp.dma_start(ring[:, s, :], a["units2"][n]).then_inc(S(f"unit_landed{s}"), 16)
            sp.wait_ge(S("out_ready"), TT)
            sp.dma_start(out.rearrange("o (t p) d -> p (o t) d", p=P), tok(10)).then_inc(S("out_stored"), 16)
            sp.wait_ge(S("out_stored"), 16)

        @block.gpsimd
        def _(pool):
            g = nc.gpsimd
            pool.dma_start(w_flr[:], a["w_flr"]).then_inc(S("small_landed"), 16)
            pool.dma_start(slab[0:RANK, 10, 0:512], a["w_gate_up"]).then_inc(S("small_landed"), 16)
            pool.dma_start(rows[:, 0, :], a["b_v"].partition_broadcast(P)).then_inc(S("small_landed"), 16)
            pool.dma_start(rows[:, 1, :], a["b_out"].partition_broadcast(P)).then_inc(S("small_landed"), 16)
            pool.dma_start(rows[:, 2, :], a["ln1_g"].partition_broadcast(P)).then_inc(S("small_landed"), 16)
            pool.dma_start(w_route[:], a["w_route"]).then_inc(S("small_landed"), 16)
            pool.dma_start(b_route[:], a["b_route"].partition_broadcast(P)).then_inc(S("small_landed"), 16)
            g.memset(ident[:], 0.0).then_inc(S("consts_begun"), 1)
            g.memset(before[:], 1.0).then_inc(S("consts_begun"), 1)
            g.memset(stack[:], 0.0).then_inc(S("consts_begun"), 1)
            g.memset(slab[:, 10, 1024:2048], 1.0).then_inc(S("consts_begun"), 1)
            g.iota(slots_i[:].rearrange("p (a b) -> p a b", a=4), pattern=[[0, 4], [1, CAP]], base=0,
                   channel_multiplier=0).then_inc(S("consts_begun"), 1)
            g.iota(numbers_i[:], pattern=[[1, NE]], base=0, channel_multiplier=0).then_inc(S("consts_begun"), 1)
            pool.wait_ge(S("consts_begun"), 6)
            for j in range(4):
                if j:
                    pool.wait_ge(S("stacked"), j)
                g.affine_select(out=stack[:], in_=stack[:], compare_op=ALU.not_equal, fill=1.0, base=-CAP * j,
                                pattern=[[-1, CAP]], channel_multiplier=1).then_inc(S("stacked"), 1)
            g.memset(slab[:, 10, 1024:2048:CHUNK], 0.0).then_inc(S("consts_ready"), 1)
            g.affine_select(out=ident[:], in_=ident[:], compare_op=ALU.not_equal, fill=1.0, base=0,
                            pattern=[[-1, P]], channel_multiplier=1).then_inc(S("consts_ready"), 1)
            g.affine_select(out=before[:], in_=before[:], compare_op=ALU.is_gt, fill=0.0, base=0,
                            pattern=[[1, P]], channel_multiplier=-1).then_inc(S("consts_ready"), 1)
            g.tensor_copy(slots[:], slots_i[:]).then_inc(S("consts_ready"), 1)
            g.tensor_copy(numbers[:], numbers_i[:]).then_inc(S("consts_ready"), 1)
            g.memset(ones[:], 1.0).then_inc(S("consts_ready"), 1)
            g.memset(eps_ln[:], 1e-5).then_inc(S("consts_ready"), 1)
            g.memset(eps_rms[:], 1e-6).then_inc(S("consts_ready"), 1)
            g.memset(meta[:], -1.0).then_inc(S("consts_ready"), 1)
            pool.wait_ge(S("consts_ready"), CONSTS)

            pool.wait_ge(S("conv_tap"), DC * CONV_W)
            pool.dma_start(tok(2), a["x"].rearrange("o (t p) d -> p (o t) d", p=P)).then_inc(S("x_landed"), 16)
            wait_read(pool, "v0_1", "v1_1")
            pool.dma_start(rows[:, 0, :], a["ln1_b"].partition_broadcast(P)).then_inc(S("ln1b_landed"), 16)

            pool.wait_ge(S("x1_ready"), TT)
            pool.dma_start(rows[:, 1, :], a["ln2_g"].partition_broadcast(P)).then_inc(S("ln2_landed"), 16)
            pool.dma_start(rows[:, 2, :], a["ln2_b"].partition_broadcast(P)).then_inc(S("ln2_landed"), 16)
            pool.dma_start(slab[:, 6, 0:DC * 136], a["w_kiwi"]).then_inc(S("small2_landed"), 16)
            pool.dma_start(slab[0:NB, 9, 0:NH], a["rel_bias"]).then_inc(S("small2_landed"), 16)
            pool.dma_start(slab[0:NB, 9, 16:16 + 511], a["buckets"]).then_inc(S("small2_landed"), 16)
            wait_read(pool, "relb")
            pool.dma_start(bias_dram[:, 0:511], slab[0:NH, 9, 1024:1024 + 511]).then_inc(S("relb_stored"), 16)
            pool.wait_ge(S("relb_stored"), 16)

            def load_bias(t):
                src = bass.AP(bias_dram.tensor, bias_dram.offset + P * t, [[1, P], [512, NH], [1, T]])
                pool.dma_start(slab[:, 2, :].rearrange("p (h j) -> p h j", h=NH), src
                               ).then_inc(S("bias_landed"), 16)

            pool.wait_ge(S("ua_used"), 1)
            load_bias(0)
            for t in range(TT):
                pool.wait_ge(S("score_ready"), t + 1)
                g.affine_select(out=work[:, t, 0:P * (t + 1)], in_=score[:, t, 0:P * (t + 1)],
                                compare_op=ALU.is_ge, fill=FILL, base=P * t, pattern=[[-1, P * (t + 1)]],
                                channel_multiplier=1).then_inc(S("work_ready"), 1)
            for t in range(TT):
                pool.wait_ge(S("hide_made"), t + 1)
                g.affine_select(out=score[:, t, 0:P * (t + 1)], in_=score[:, t, 0:P * (t + 1)],
                                compare_op=ALU.is_ge, fill=HIDE, base=P * t, pattern=[[-1, P * (t + 1)]],
                                channel_multiplier=1).then_inc(S("hide_ready"), 1)
            pool.wait_ge(S("logits_ready"), 4)
            load_bias(1)
            wait_read(pool, "yb3")
            pool.dma_start(slab[:, 7, 0:512], a["pT"]).then_inc(S("p_landed"), 16)

        @block.tensor
        def _(pe):
            mm = nc.tensor.matmul
            units = [0, 0]

            def unit(part=0, cols_=512):
                n = units[part]
                units[part] += 1
                if part == 0:
                    s = n % RING
                    pe.wait_ge(S(f"unit_landed{s}"), 16 * (n // RING + 1))
                else:
                    s = (EXPERT_SLOT0 + n) % RING
                    pe.wait_ge(S(f"unit_landed{s}"), 16 * (len(range(s, len(UNITS1), RING)) + n // RING + 1))
                return ring[:, s, :].rearrange("p (c n) -> p c n", n=cols_)

            def chan_major(w, x, tasks, off=0):
                for i, task in enumerate(tasks):
                    o = take_bank(task)
                    for m in range(2):
                        f = off + P * (2 * i + m)
                        for c in range(DC):
                            last = mm(o[:, T * m:T * m + T], w[:, c, f:f + P], x[:, c, :],
                                      start=c == 0, stop=c == DC - 1)
                    full(last, task)

            def token_major(w, x, tasks, n=512, off=0):
                for t, task in enumerate(tasks):
                    o = take_bank(task)
                    for c in range(DC):
                        last = mm(o[:, 0:n], x[:, c, P * t:P * t + P], w[:, c, off:off + n],
                                  start=c == 0, stop=c == DC - 1)
                    full(last, task)

            def turn(src, tasks, ready, done=0):
                for j, task in enumerate(tasks):
                    o = take_bank(task)
                    for m in range(2):
                        for t in range(TT):
                            if j == 0 and m == 0:
                                pe.wait_ge(S(ready), done + t + 1)
                            c = 2 * j + m
                            last = nc.tensor.transpose(o[:, T * m + P * t:T * m + P * t + P],
                                                       src[:, t, P * c:P * c + P], ident[:])
                    full(last, task)

            xT = chan(0)
            pe.wait_ge(S("xt_landed"), 16)
            chan_major(unit(), xT, ["g0", "g1"])
            chan_major(unit(), xT, ["a0", "a1"])
            chan_major(unit(), xT, ["g2", "g3"])
            chan_major(unit(), xT, ["a2", "a3"])
            chan_major(unit(), xT, ["k0", "k1"])
            pe.wait_ge(S("small_landed"), 16 * SMALL_LOADS)
            o = take_bank("fl")
            for c in range(DC):
                last = mm(o[0:RANK, 0:T], w_flr[:, c, :], xT[:, c, :], start=c == 0, stop=c == DC - 1)
            full(last, "fl")
            pe.wait_ge(S("small_landed"), 16 * SMALL_LOADS)
            wait_read(pe, "fl")
            for j in range(2):
                o = take_bank(f"z{j}")
                for m in range(2):
                    f = P * (2 * j + m)
                    last = mm(o[:, T * m:T * m + T], slab[0:RANK, 10, f:f + P], slab[0:RANK, 10, 512:512 + T],
                              start=True, stop=True)
                full(last, f"z{j}")
            token_major(unit(), xT, ["v0_0", "v0_1"])
            token_major(unit(), xT, ["v1_0", "v1_1"])
            chan_major(unit(), xT, ["q0", "q1"])
            pe.wait_ge(S("consts_ready"), CONSTS)
            o = take_bank("csum")
            for c in range(DC):
                if c % 4 == 0:
                    pe.wait_ge(S("conv_tap"), 4 * CONV_W * (c // 4 + 1))
                last = mm(o[:, 0:T], ones[:], chan(3)[:, c, :], start=c == 0, stop=c == DC - 1)
            full(last, "csum")
            chan_major(unit(), xT, ["r0", "r1"])
            chan_major(unit(), xT, ["r2", "r3"])
            o = take_bank("csq")
            pe.wait_ge(S("csq_ready"), 1)
            for c in range(DC):
                last = mm(o[:, 0:T], ones[:], chan(1)[:, c, :], start=c == 0, stop=c == DC - 1)
            full(last, "csq")
            pe.wait_ge(S("consts_ready"), CONSTS)
            pe.wait_ge(S("kdec_ready"), 1)
            for t in range(TT):
                o = take_bank(f"kdt{t}")
                for h in range(H1):
                    last = nc.tensor.transpose(o[:, P * h:P * h + P], half(5, 0)[:, h, P * t:P * t + P], ident[:])
                full(last, f"kdt{t}")
            wait_read(pe, "kdt0", "kdt1", "v0_0", "v0_1", "v1_0", "v1_1")
            for n in range(NCH):
                b = CHUNK * (n % 2)
                for hp in range(2):
                    task = f"kv{2 * n + hp}"
                    o = take_bank(task)
                    for m in range(2):
                        h = 2 * hp + m
                        last = mm(o[:, HV * m:HV * m + HV],
                                  slab[b:b + CHUNK, 5, 1024 + 512 * (n // 2) + P * h:1024 + 512 * (n // 2) + P * h + P],
                                  tok(6)[b:b + CHUNK, n // 2, HV * h:HV * h + HV], start=True, stop=True)
                    full(last, task)
            chan_major(unit(), xT, ["ga0", "ga1"])
            chan_major(unit(), xT, ["ga2", "ga3"])
            wait_read(pe, "q0", "q1")
            wait_read(pe, *[f"kv{i}" for i in range(8)])
            for h in range(H1):
                o = take_bank(f"o{h}")
                for m in range(2):
                    for n in range(NCH):
                        st = states(n, h)[:, P * m:P * m + P]
                        last = mm(o[:, T * m + CHUNK * n:T * m + CHUNK * n + CHUNK], st,
                                  half(7, 0)[:, h, CHUNK * n:CHUNK * n + CHUNK], start=True, stop=True)
                full(last, f"o{h}")
            chan_major(unit(), xT, ["gb0", "gb1"])
            chan_major(unit(), xT, ["gb2", "gb3"])
            for j in range(2):
                pe.wait_ge(S("osq_ready"), 2 * j + 2)
                o = take_bank(f"osum{j}")
                for m in range(2):
                    h = 2 * j + m
                    for k in range(2):
                        last = mm(o[:, T * m:T * m + T], ones[:], chan(4)[:, 2 * h + k, :], start=k == 0, stop=k == 1)
                full(last, f"osum{j}")
            pe.wait_ge(S("conv_act_ready"), 1)
            chan_major(unit(), chan(1), ["yc0", "yc1"])
            chan_major(unit(), chan(1), ["yc2", "yc3"])
            pe.wait_ge(S("gla_ready"), 1)
            chan_major(unit(), chan(10), ["yg0", "yg1"])
            chan_major(unit(), chan(10), ["yg2", "yg3"])
            pe.wait_ge(S("merged_ready"), 4)
            token_major(unit(), chan(5), ["mix0_0", "mix0_1"])
            token_major(unit(), chan(5), ["mix1_0", "mix1_1"])
            turn(tok(0), [f"x1t{j}" for j in range(4)], "x1_ready")
            wait_read(pe, *[f"x1t{j}" for j in range(4)])
            pe.wait_ge(S("small_landed"), 16 * SMALL_LOADS)
            o = take_bank("lg")
            for t in range(TT):
                for c in range(DC):
                    last = mm(o[:, 128 * t:128 * t + 72], chan(1)[:, c, P * t:P * t + P], w_route[:, c, :],
                              start=c == 0, stop=c == DC - 1)
            full(last, "lg")
            pe.wait_ge(S("zeros_ready"), 1)
            wait_read(pe, *TASKS1[-8:-2])
            for t in range(TT):
                for hf in range(2):
                    mm(acc[t][hf][:], zeros[:, 0:P], zeros[:], start=True, stop=False)
            pe.wait_ge(S("mask_ready"), 1)
            pe.wait_ge(S("consts_ready"), CONSTS)
            o = take_bank("pos")
            mm(o[:, 0:64], before[:], mask[:, 0, :], start=True, stop=True)
            mm(o[:, 64:128], before[:], mask[:, 1, :], start=True, stop=False)
            mm(o[:, 64:128], ones[:], mask[:, 0, :], start=False, stop=True)
            mm(o[:, 128:192], ones[:], mask[:, 0, :], start=True, stop=False)
            full(mm(o[:, 128:192], ones[:], mask[:, 1, :], start=False, stop=True), "pos")
            wait_read(pe, "pos", "lg")
            pe.wait_ge(S("x1_ready"), TT)

            def gather(f, par, r):
                pe.wait_ge(S("sel_ready"), (r * META + f + 1) * TT)
                for c in range(DC):
                    for t in range(TT):
                        last = mm(gather_bank[:, CAP * c:CAP * c + CAP], tok(0)[:, t, c::DC], sel[:, par, t, :],
                                  start=t == 0, stop=t == 1)
                last.then_inc(S("xg_full"), 1)

            def combine(par, ends=False, again=False):
                for t in range(TT):
                    for hf in range(2):
                        last = mm(acc[t][hf][:], spread[:, par, P * t:P * t + P],
                                  y_sb[:, par, 512 * hf:512 * hf + 512], start=False, stop=ends,
                                  skip_group_check=again)
                last.then_inc(S("combined"), 1)

            def expert(e, q, it, r):
                n = r * NE + e
                for w, (b, name) in enumerate(((gate_bank, "gate_full"), (up_bank, "up_full"))):
                    pe.wait_ge(S(f"expert_landed{3 * q + w}"), 16 * (r * (NE // 2) + it + 1))
                    if w == 0:
                        pe.wait_ge(S("xg_copied"), r * (NE + 1) + e + 1)
                    else:
                        pe.wait_ge(S("y1_copied"), r * (NE + 1) + e + 1)
                    wt = ring[:, expert_slot(q, w), :].rearrange("p (c n) -> p c n", c=DC)
                    for c in range(DC):
                        j = c % 4
                        last = mm(b[CAP * j:CAP * j + CAP, :], xg[:, c, :], wt[:, c, :],
                                  start=c < 4, stop=c >= 4, tile_position=(0, CAP * j))
                    last.then_inc(S(name), 1)
                gather(e + 1, 1 - q, r)
                pe.wait_ge(S("selw_ready"), (r * META + e + 1) * TT)
                pe.wait_ge(S("y0_copied"), r * (NE + 1) + e + 1)
                for t in range(TT):
                    last = nc.tensor.transpose(y_bank[:, P * t:P * t + P], selw[:, q, t, :], ident[:])
                last.then_inc(S("spread_full"), 1)
                pe.wait_ge(S("g_copied"), n + 1)
                pe.wait_ge(S("u_copied"), n + 1)
                for src, o in ((g_sb, 0), (u_sb, 128)):
                    for m in range(4):
                        last = mm(gate_bank[:, o + CAP * m:o + CAP * m + CAP], src[:, m::4], stack[:],
                                  start=True, stop=True)
                last.then_inc(S("hidden_full"), 1)
                pe.wait_ge(S("spread_copied"), r * (NE + 1) + e + 1)
                combine(1 - q, again=not isinstance(r, int))
                pe.wait_ge(S("h_ready"), n + 1)
                pe.wait_ge(S(f"expert_landed{3 * q + 2}"), 16 * (r * (NE // 2) + it + 1))
                wt = ring[:, expert_slot(q, 2), :].rearrange("p (c n) -> p c n", c=4)
                pe.wait_ge(S("spread_copied"), r * (NE + 1) + e + 2)
                for hf, (b, name) in enumerate(((y_bank, "y0_full"), (up_bank, "y1_full"))):
                    for m in range(4):
                        last = mm(b[CAP * m:CAP * m + CAP, :], h_sb[:, m, :],
                                  wt[:, m, 512 * hf:512 * hf + 512], start=True, stop=True,
                                  tile_position=(0, CAP * m))
                    last.then_inc(S(name), 1)

            def last_combine(r):
                pe.wait_ge(S("y0_copied"), (r + 1) * (NE + 1))
                pe.wait_ge(S("y1_copied"), (r + 1) * (NE + 1))
                pe.wait_ge(S("spread_copied"), (r + 1) * (NE + 1))
                combine(1, ends=True, again=not isinstance(r, int))

            pe.wait_ge(S("consts_ready"), CONSTS)
            gather(0, 0, 0)
            with pe.Fori(0, NE // 2) as it:
                for q in range(2):
                    expert(2 * it + q, q, it, 0)
            last_combine(0)
            more = pe.value_load(over[0:1, 0:1], min_val=0, max_val=1)
            with pe.If(more > 0):
                with pe.Fori(1, ROUNDS) as r:
                    pe.wait_ge(S("xg_copied"), r * (NE + 1))
                    gather(0, 0, r)
                    with pe.Fori(0, NE // 2) as it:
                        for q in range(2):
                            expert(2 * it + q, q, it, r)
                    last_combine(r)
            turn(tok(1), [f"x2t{j}" for j in range(4)], "xn_ready")
            wait_read(pe, *[f"x2t{j}" for j in range(4)])
            xn = chan(0)
            pe.wait_ge(S("small2_landed"), 48)
            kiwi = slab[:, 6, 0:DC * 136].rearrange("p (c n) -> p c n", c=DC)
            o = take_bank("kiwi_k")
            for c in range(DC):
                last = mm(o[:, 0:T], kiwi[:, c, 0:P], xn[:, c, :], start=c == 0, stop=c == DC - 1)
            full(last, "kiwi_k")
            o = take_bank("kiwi_w")
            for t in range(TT):
                for c in range(DC):
                    last = mm(o[:, 8 * t:8 * t + 8], xn[:, c, P * t:P * t + P], kiwi[:, c, P:P + 8],
                              start=c == 0, stop=c == DC - 1)
            full(last, "kiwi_w")
            o = take_bank("relb")
            full(mm(o[0:NH, 0:511], slab[0:NB, 9, 0:NH], slab[0:NB, 9, 16:16 + 511], start=True, stop=True), "relb")
            chan_major(unit(1), xn, ["lx0", "lx1"])
            chan_major(unit(1), xn, ["lx2", "lx3"])
            chan_major(unit(1), xn, ["lg_0", "lg_1"])
            chan_major(unit(1), xn, ["lg_2", "lg_3"])
            w = unit(1)
            chan_major(w, xn, ["kk"])
            o = take_bank("vv")
            for t in range(TT):
                for c in range(DC):
                    last = mm(o[:, T * t:T * t + T], xn[:, c, P * t:P * t + P], w[:, c, 256:512],
                              start=c == 0, stop=c == DC - 1)
            full(last, "vv")
            chan_major(unit(1), xn, ["qi0", "qi1"])
            w = unit(1, 128)
            for x, pre in ((0, "lr"), (1, "li")):
                for j in range(4):
                    o = take_bank(f"{pre}{j}")
                    for m in range(2):
                        c = 2 * j + m
                        if x == 0:
                            pe.wait_ge(S("lru_tap"), 2 * LRU_W * (j + 1))
                        last = mm(o[:, T * m:T * m + T], w[:, 8 * x + c, :], chan(2)[:, c, :], start=True, stop=True)
                    full(last, f"{pre}{j}")
            o = take_bank("ksum")
            pe.wait_ge(S("k_sq_ready"), 1)
            full(mm(o[:, 0:512], ones[:], k_sq, start=True, stop=True), "ksum")
            chan_major(unit(1), xn, ["qq0", "qq1"])
            chan_major(unit(1), xn, ["qq2", "qq3"])
            chan_major(unit(1), xn, ["gc0", "gc1"])
            chan_major(unit(1), xn, ["gc2", "gc3"])
            wait_read(pe, "kiwi_k", "qi0", "qi1")
            for t in range(TT):
                n = P * (t + 1)
                for j in range(4):
                    o = take_bank(f"dots{t}_{j}")
                    for m in range(2):
                        h = indexer_head(j, m)
                        b = ID * (h % 2)
                        last = mm(o[:, T * m:T * m + n], qiT[b:b + ID, h // 2, P * t:P * t + P], kiT[b:b + ID, 0:n],
                                  start=True, stop=True)
                    full(last, f"dots{t}_{j}")
            for j in range(4):
                o = take_bank(f"qsum{j}")
                pe.wait_ge(S("q_sq_ready"), j + 1)
                full(mm(o[:, 0:512], ones[:], slab[:, 6, 512 * j:512 * j + 512], start=True, stop=True), f"qsum{j}")
            pe.wait_ge(S("ya_ready"), 1)
            chan_major(unit(1), chan(1), ["ya0", "ya1"])
            chan_major(unit(1), chan(1), ["ya2", "ya3"])
            chan_major(unit(1), xn, ["gd0", "gd1"])
            chan_major(unit(1), xn, ["gd2", "gd3"])
            pe.wait_ge(S("k_ready"), 1)
            pe.wait_ge(S("q_ready"), 4)
            for t in range(TT):
                n = P * (t + 1)
                for j in range(4):
                    o = take_bank(f"log{t}_{j}")
                    for m in range(2):
                        h = 2 * j + m
                        last = mm(o[:, T * m:T * m + n], chan(9)[:, h, P * t:P * t + P], kT[:, h // QPK, 0:n],
                                  start=True, stop=True)
                    full(last, f"log{t}_{j}")
            for t in range(TT):
                pe.wait_ge(S("probs_ready"), t + 1)
                for s in range(t + 1):
                    for k in range(2):
                        o = take_bank(f"pt{t}_{s}_{k}")
                        for m in range(4):
                            last = nc.tensor.transpose(o[:, P * m:P * m + P], lgt[:, 4 * k + m, P * s:P * s + P],
                                                       ident[:])
                        full(last, f"pt{t}_{s}_{k}")
                wait_read(pe, *[f"pt{t}_{s}_{k}" for s in range(t + 1) for k in range(2)])
                for k in range(2):
                    o = take_bank(f"pv{t}_{k}")
                    for s in range(t + 1):
                        last = mm(o[:, 0:512], v2[:, s, HD * k:HD * k + HD],
                                  prob_t[:, s, 4 * k:4 * k + 4, :].rearrange("p h t -> p (h t)"),
                                  start=s == 0, stop=s == t)
                    full(last, f"pv{t}_{k}")
            wait_read(pe, "pv0_0", "pv0_1", "pv1_0", "pv1_1")
            chan_major(unit(1), chan(6), ["yb0", "yb1"])
            chan_major(unit(1), chan(6), ["yb2", "yb3"])
            pe.wait_ge(S("merged2_ready"), 4)
            token_major(unit(1), chan(3), ["mo0_0", "mo0_1"])
            token_major(unit(1), chan(3), ["mo1_0", "mo1_1"])
            turn(tok(4), [f"x3t{j}" for j in range(4)], "xn_ready", TT)
            wait_read(pe, *[f"x3t{j}" for j in range(4)])
            for i in range(6):
                chan_major(unit(1), xn, [f"fg{i}_0", f"fg{i}_1"])
                chan_major(unit(1), xn, [f"fu{i}_0", f"fu{i}_1"])
            wait_read(pe, "fu5_0", "fu5_1")
            for u in range(2):
                o = [take_bank(f"dn{u}_{t}") for t in range(TT)]
                for k in range(3):
                    w = unit(1)
                    for t in range(TT):
                        for c in range(DC):
                            last = mm(o[t][:], hT[:, DC * k + c, P * t:P * t + P], w[:, c, :],
                                      start=k == 0 and c == 0, stop=k == 2 and c == DC - 1)
                        if k == 2:
                            full(last, f"dn{u}_{t}")
            turn(tok(4), [f"x4t{j}" for j in range(4)], "xn_ready", 2 * TT)
            pe.wait_ge(S("p_landed"), 16)
            w = unit(1, 1024)
            pT = slab[:, 7, 0:512].rearrange("p (c t) -> p c t", c=2)
            for u in range(2):
                for t in range(TT):
                    o = take_bank(f"pp{u}_{t}")
                    for c in range(2):
                        last = mm(o[:], pT[:, c, P * t:P * t + P], w[:, c, 512 * u:512 * u + 512],
                                  start=c == 0, stop=c == 1)
                    full(last, f"pp{u}_{t}")
            wait_read(pe, *[f"x4t{j}" for j in range(4)])
            token_major(unit(1), xn, ["pg0_0", "pg0_1"])
            token_major(unit(1), xn, ["pg1_0", "pg1_1"])

        @block.scalar
        def _(act):
            A = nc.scalar.activation

            def per_chunk(tasks, dst, func, bias=None, scale=1.0, wait=None):
                for i, task in enumerate(tasks):
                    o = wait_full(act, task)
                    for m in range(2):
                        c = 2 * i + m
                        b = col(bias, c) if bias else 0.0
                        ins = A(dst[:, c, :], o[:, T * m:T * m + T], func, bias=b, scale=scale)
                    read(ins, task)

            act.wait_ge(S("cols_landed"), 16)
            per_chunk(["g0", "g1"], chan(1), ACT.Sigmoid, "b_conv_g")
            for i, task in enumerate(["g2", "g3"]):
                o = wait_full(act, task)
                for m in range(2):
                    c = 4 + 2 * i + m
                    ins = A(chan(1)[:, c, :], o[:, T * m:T * m + T], ACT.Sigmoid, bias=col("b_conv_g", c))
                read(ins, task)
            per_chunk(["k0", "k1"], half(4, 0), ACT.Identity, "b_k")
            o = wait_full(act, "fl")
            read(A(slab[0:RANK, 10, 512:512 + T], o[0:RANK, 0:T], ACT.Identity,
                   bias=cols[0:RANK, COLS["b_flr"]:COLS["b_flr"] + 1]), "fl")
            per_chunk(["z0", "z1"], half(5, 0), ACT.Identity, "b_gate")
            la = half(7, 1)
            act.wait_ge(S("negabs_ready"), 1)
            A(la, la, ACT.Exp).then_inc(S("gate_exp"), 1)
            act.wait_ge(S("gate_exp"), 1)
            A(la, la, ACT.Ln, bias=1.0).then_inc(S("gate_ln"), 1)
            per_chunk(["q0", "q1"], half(7, 0), ACT.Identity, "b_q")
            act.wait_ge(S("toend_ready"), 1)
            A(la, la, ACT.Exp, scale=1.0 / TAU).then_inc(S("decay_ready"), 1)
            A(small[:, 0:16].rearrange("p (h n a) -> p h n a", h=H1, a=1), half(4, 1).rearrange("p h (n t) -> p h n t", t=CHUNK)[:, :, :, CHUNK - 1:CHUNK],
              ACT.Exp, scale=1.0 / TAU).then_inc(S("decay_ready"), 1)
            act.wait_ge(S("centered"), DC)
            A(chan(1), chan(3), ACT.Square).then_inc(S("csq_ready"), 1)
            act.wait_ge(S("consts_ready"), CONSTS)
            o = wait_full(act, "csq")
            read(A(slab[:, 1, 0:T], o[:, 0:T], ACT.Sqrt, bias=eps_ln[:], scale=1.0 / D), "csq")
            for c in range(DC):
                act.wait_ge(S("conv_normed"), c + 1)
                ins = A(chan(1)[:, c, :], chan(3)[:, c, :], ACT.Silu, bias=col("cln_b", c), scale=col("cln_g", c))
            ins.then_inc(S("conv_act_ready"), 1)
            act.wait_ge(S("conv_act_ready"), 1)
            per_chunk([f"r{j}" for j in range(4)], chan(3), ACT.Silu, "b_r")
            for i, task in enumerate(["ga0", "ga1", "ga2", "ga3"]):
                if i == 0:
                    wait_full(act, "kv7")
                o = wait_full(act, task)
                for m in range(2):
                    c = 2 * i + m
                    ins = A(chan(5)[:, c, :], o[:, T * m:T * m + T], ACT.Sigmoid, bias=col("b_ga", c))
                read(ins, task)
            for h in range(H1):
                o = wait_full(act, f"o{h}")
                dst = chan(10)[:, 2 * h:2 * h + 2, :].rearrange("p a t -> p (a t)")
                read(A(dst, o[:, 0:512], ACT.Copy, scale=HK ** -0.5), f"o{h}")
                wait_read(act, f"o{h}")
                A(chan(4)[:, 2 * h:2 * h + 2, :].rearrange("p a t -> p (a t)"), dst, ACT.Square
                  ).then_inc(S("osq_ready"), 1)
            per_chunk([f"gb{j}" for j in range(4)], chan(6), ACT.Sigmoid, "b_gb")
            for j in range(2):
                o = wait_full(act, f"osum{j}")
                read(A(slab[:, 7, 1024 + 512 * j:1024 + 512 * j + 512], o[:, 0:512], ACT.Sqrt,
                       bias=eps_rms[:], scale=1.0 / HV), f"osum{j}")
            for t in range(TT):
                act.wait_ge(S("ln_stats"), t + 1)
                A(small[:, 20 + t:21 + t], small[:, 17 + 2 * t:18 + 2 * t], ACT.Sqrt, bias=eps_ln[:]
                  ).then_inc(S("ln_std"), 1)
            for j in range(4):
                o = wait_full(act, f"x1t{j}")
                read(A(slab[:, 1, 512 * j:512 * j + 512], o[:, 0:512], ACT.Copy), f"x1t{j}")
            act.wait_ge(S("gtop_ready"), TT)
            for t in range(TT):
                A(e_exp[:, t, :], logit[:, t, 0:NG], ACT.Exp, bias=small[:, 30 + t:31 + t],
                  accum_out=small[:, 32 + t:33 + t]).then_inc(S("gsum_ready"), 1)
            act.wait_ge(S("ediff_ready"), 1)
            A(small[:, 36:38], small[:, 34:36], ACT.Exp).then_inc(S("ratio_ready"), 1)

            def take_xg(n):
                act.wait_ge(S("xg_full"), n)
                A(slab[:, 1, 0:DC * CAP], gather_bank[:, 0:DC * CAP], ACT.Copy).then_inc(S("xg_copied"), 1)

            def expert(e, q, r):
                n = r * NE + e
                act.wait_ge(S("gate_full"), n + 1)
                A(g_sb, gate_bank[:], ACT.Copy).then_inc(S("g_copied"), 1)
                take_xg(r * (NE + 1) + e + 2)
                act.wait_ge(S("hidden_full"), n + 1)
                A(slab[:, 1, 1536:1664], gate_bank[:, 0:128], ACT.Silu).then_inc(S("silu_ready"), 1)
                act.wait_ge(S("y0_full"), n + 1)
                A(y_sb[:, q, 0:512], y_bank[:], ACT.Copy).then_inc(S("y0_copied"), 1)

            wait_read(act, "lg")
            wait_read(act, "pos")
            act.wait_ge(S("meta_ready"), 1)
            act.wait_ge(S("zeros_ready"), 1)
            A(y_sb[:, 1, 0:512], zeros, ACT.Copy).then_inc(S("y0_copied"), 1)
            take_xg(1)
            with act.Fori(0, NE // 2) as it:
                for q in range(2):
                    expert(2 * it + q, q, 0)
            more = act.value_load(over[0:1, 0:1], min_val=0, max_val=1)
            with act.If(more > 0):
                with act.Fori(1, ROUNDS) as r:
                    act.wait_ge(S("combined"), r * (NE + 1))
                    A(y_sb[:, 1, 0:512], zeros, ACT.Copy).then_inc(S("y0_copied"), 1)
                    take_xg(r * (NE + 1) + 1)
                    with act.Fori(0, NE // 2) as it:
                        for q in range(2):
                            expert(2 * it + q, q, r)
            for t in range(TT):
                act.wait_ge(S("ln_stats"), TT + t + 1)
                A(small[:, 46 + t:47 + t], small[:, 43 + 2 * t:44 + 2 * t], ACT.Sqrt, bias=eps_ln[:]
                  ).then_inc(S("ln_std"), 1)

            def rms_tile(t, dst, done, at):
                A(tok(dst)[:, t, :], tok(10)[:, t, :], ACT.Square, accum_out=small[:, at + t:at + t + 1]
                  ).then_inc(S("rms_sum"), 1)
                act.wait_ge(S("rms_sum"), done + t + 1)
                A(small[:, at + 2 + t:at + 3 + t], small[:, at + t:at + t + 1], ACT.Sqrt, bias=eps_rms[:],
                  scale=1.0 / D).then_inc(S("rms_root"), 1)

            for t in range(TT):
                act.wait_ge(S("x2_ready"), t + 1)
                rms_tile(t, 1, 0, 50)

            def take_turned(tasks, gain):
                for i, task in enumerate(tasks):
                    o = wait_full(act, task)
                    for m in range(2):
                        c = 2 * i + m
                        ins = A(chan(0)[:, c, :], o[:, T * m:T * m + T], ACT.Copy, scale=col(gain, c))
                    read(ins, task)

            take_turned([f"x2t{j}" for j in range(4)], "mix_norm")
            o = wait_full(act, "kiwi_k")
            read(A(kiT, o[:, 0:T], ACT.Copy), "kiwi_k")
            o = wait_full(act, "kiwi_w")
            read(A(slab[:, 8, 1792:1808], o[:, 0:16], ACT.Copy, scale=IH ** -0.5), "kiwi_w")
            o = wait_full(act, "relb")
            read(A(slab[0:NH, 9, 1024:1024 + 511], o[0:NH, 0:511], ACT.Copy), "relb")
            per_chunk([f"lx{j}" for j in range(4)], chan(1), ACT.Copy)
            per_chunk([f"lg_{j}" for j in range(4)], chan(3), ACT.Gelu_apprx_tanh)
            o = wait_full(act, "kk")
            read(A(slab[:, 7, 0:512], o[:, 0:512], ACT.Copy), "kk")
            wait_read(act, "kk")
            A(k_sq, slab[:, 7, 0:512], ACT.Square).then_inc(S("k_sq_ready"), 1)
            o = wait_full(act, "vv")
            read(A(slab[:, 7, 512:1024], o[:, 0:512], ACT.Copy), "vv")
            for j in range(2):
                o = wait_full(act, f"qi{j}")
                read(A(slab[:, 7, 1024 + 512 * j:1536 + 512 * j], o[:, 0:512], ACT.Copy), f"qi{j}")
            act.wait_ge(S("lam_negabs"), 1)
            A(small[:, 80:88], small[:, 72:80], ACT.Exp).then_inc(S("lam_exp"), 1)
            per_chunk([f"lr{j}" for j in range(4)], chan(4), ACT.Sigmoid, "lru_ba")
            per_chunk([f"li{j}" for j in range(4)], chan(5), ACT.Sigmoid, "lru_bx")
            wait_read(act, "lr0", "lr1", "lr2", "lr3")
            act.wait_ge(S("rate_ready"), 1)
            wait_read(act, "kiwi_w", "kiwi_k")
            for c in range(DC):
                ins = A(chan(6)[:, c, :], chan(4)[:, c, :], ACT.Tanh, scale=small[:, 112 + c:113 + c])
            ins.then_inc(S("tanh_ready"), 1)
            for c in range(DC):
                ins = A(chan(4)[:, c, :], chan(4)[:, c, :], ACT.Exp, scale=small[:, 112 + c:113 + c])
            ins.then_inc(S("a_ready"), 1)
            act.wait_ge(S("relb_stored"), 16)
            for j in range(4):
                o = wait_full(act, f"qq{j}")
                read(A(slab[:, 9, 512 * j:512 * j + 512], o[:, 0:512], ACT.Copy), f"qq{j}")
            act.wait_ge(S("mult2_ready"), 1)
            A(slab[:, 6, :], slab[:, 6, :], ACT.Sqrt, scale=-1.0).then_inc(S("mult_ready"), 1)
            o = wait_full(act, "ksum")
            read(A(k_sq, o[:, 0:512], ACT.Sqrt, bias=eps_rms[:], scale=1.0 / HD), "ksum")
            act.wait_ge(S("ya_ready"), 1)
            per_chunk([f"gc{j}" for j in range(4)], chan(3), ACT.Sigmoid)
            for t in range(TT):
                n = P * (t + 1)
                for j in range(4):
                    o = wait_full(act, f"dots{t}_{j}")
                    read(A(slab[:, 4 + t, 512 * j:512 * j + 512].rearrange("p (m s) -> p m s", m=2)[:, :, 0:n],
                           o[:].rearrange("p (m s) -> p m s", m=2)[:, :, 0:n], ACT.Relu, scale=ID ** -0.5),
                         f"dots{t}_{j}")
            for j in range(4):
                wait_read(act, f"qq{j}")
                A(slab[:, 6, 512 * j:512 * j + 512], slab[:, 9, 512 * j:512 * j + 512], ACT.Square
                  ).then_inc(S("q_sq_ready"), 1)
            for j in range(4):
                o = wait_full(act, f"qsum{j}")
                read(A(slab[:, 6, 512 * j:512 * j + 512], o[:, 0:512], ACT.Sqrt, bias=eps_rms[:], scale=1.0 / HD),
                     f"qsum{j}")
            wait_full(act, "ya3")
            per_chunk([f"gd{j}" for j in range(4)], chan(1), ACT.Sigmoid)
            for t in range(TT):
                n = P * (t + 1)
                act.wait_ge(S("rowmax_ready"), t + 1)
                for h in range(NH):
                    ins = A(lgt[:, h, 0:n], lgt[:, h, 0:n], ACT.Exp, bias=small[:, 128 + h:129 + h],
                            accum_out=small[:, 136 + h:137 + h])
                ins.then_inc(S("exp_ready"), 1)
                for s in range(t + 1):
                    for k in range(2):
                        o = wait_full(act, f"pt{t}_{s}_{k}")
                        read(A(prob_t[:, s, 4 * k:4 * k + 4, :].rearrange("p h t -> p (h t)"), o[:, 0:512],
                               ACT.Copy), f"pt{t}_{s}_{k}")
                for k in range(2):
                    o = wait_full(act, f"pv{t}_{k}")
                    read(A(chan(6)[:, 4 * k:4 * k + 4, P * t:P * t + P],
                           o[:].rearrange("p (h t) -> p h t", h=4), ACT.Copy), f"pv{t}_{k}")
            for t in range(TT):
                wait_read(act, f"mo0_{t}", f"mo1_{t}")
                rms_tile(t, 4, TT, 54)
            take_turned([f"x3t{j}" for j in range(4)], "ffn_norm")
            for i in range(6):
                for j in range(2):
                    o = wait_full(act, f"fg{i}_{j}")
                    if i >= 2:
                        act.wait_ge(S("ffn_tap"), 4 * FFN_W * (i - 1))
                    read(A(half(4, i % 2)[:, 2 * j:2 * j + 2, :].rearrange("p a t -> p (a t)"), o[:, 0:512],
                           ACT.Copy), f"fg{i}_{j}")
                act.wait_ge(S("ffn_tap"), 4 * FFN_W * (i + 1))
                A(half(5, i % 2), half(5, i % 2), ACT.Gelu_apprx_tanh).then_inc(S("fgelu_ready"), 1)
            for t in range(TT):
                wait_read(act, f"dn0_{t}", f"dn1_{t}")
                rms_tile(t, 4, 2 * TT, 62)
            take_turned([f"x4t{j}" for j in range(4)], "ple_norm")
            for u in range(2):
                for t in range(TT):
                    o = wait_full(act, f"pg{u}_{t}")
                    read(A(tok(4)[:, t, 512 * u:512 * u + 512], o[:], ACT.Sigmoid), f"pg{u}_{t}")

        @block.vector
        def _(dve):
            v = nc.vector
            stt, ts, tt = v.scalar_tensor_tensor, v.tensor_scalar, v.tensor_tensor

            def glu_input(js):
                for j in js:
                    wait_read(dve, f"g{j}")
                    o = wait_full(dve, f"a{j}")
                    for m in range(2):
                        c = 2 * j + m
                        ins = stt(chan(2)[:, c, :], o[:, T * m:T * m + T], col("b_conv_a", c), chan(1)[:, c, :],
                                  ALU.add, ALU.mult)
                    read(ins, f"a{j}")
                wait_read(dve, *[f"a{j}" for j in js])

            def causal_conv(src, dst, w, width, bias, chunks, done, base, signal=None):
                n = 0
                for j in reversed(range(width)):
                    lag = width - 1 - j
                    for i, (cs, cd, cw) in enumerate(chunks):
                        wc = col(w, width * cw + j)
                        if lag == 0:
                            ins = ts(dst[:, cd, :], src[:, cs, :], wc, col(bias, cw), ALU.mult, ALU.add)
                        else:
                            dve.wait_ge(S(done), base + n - len(chunks) + 1)
                            ins = stt(dst[:, cd, lag:T], src[:, cs, 0:T - lag], wc, dst[:, cd, lag:T],
                                      ALU.mult, ALU.add)
                        n += 1
                        ins.then_inc(S(done), 1)
                dve.wait_ge(S(done), base + n)
                return base + n

            dve.wait_ge(S("cols_landed"), 16)
            glu_input([0, 1])
            n = causal_conv(chan(2), chan(3), "conv_w", CONV_W, "conv_b", [(c, c, c) for c in range(4)],
                            "conv_tap", 0)
            glu_input([2, 3])
            causal_conv(chan(2), chan(3), "conv_w", CONV_W, "conv_b", [(c, c, c) for c in range(4, 8)],
                        "conv_tap", n)
            wait_read(dve, "z0", "z1")
            z, la = half(5, 0), half(7, 1)
            stt(la, z, -1.0, z, ALU.mult, ALU.min).then_inc(S("negabs_ready"), 1)
            dve.wait_ge(S("small_landed"), 16 * SMALL_LOADS)
            for u in range(2):
                for t in range(TT):
                    o = wait_full(dve, f"v{u}_{t}")
                    read(tt(tok(6)[:, t, 512 * u:512 * u + 512], o[:], rows[:, 0, 512 * u:512 * u + 512], ALU.add),
                         f"v{u}_{t}")
            o = wait_full(dve, "csum")
            read(ts(mean, o[:, 0:T], -1.0 / D, None, ALU.mult), "csum")
            wait_read(dve, "csum")
            for c in range(DC):
                tt(chan(3)[:, c, :], chan(3)[:, c, :], mean, ALU.add).then_inc(S("centered"), 1)
            dve.wait_ge(S("gate_ln"), 1)
            stt(z, z, 0.0, la, ALU.min, ALU.subtract).then_inc(S("loga_ready"), 1)
            dve.wait_ge(S("loga_ready"), 1)
            dve.wait_ge(S("consts_ready"), CONSTS)
            v.tensor_tensor_scan(slab[:, 4, 1024:2048], slab[:, 10, 1024:2048], slab[:, 5, 0:1024], 0.0,
                                 ALU.mult, ALU.add).then_inc(S("cum_ready"), 1)
            dve.wait_ge(S("cum_ready"), 1)
            cum = slab[:, 4, 1024:2048].rearrange("p (n t) -> p n t", t=CHUNK)
            tt(slab[:, 7, 1024:2048].rearrange("p (n t) -> p n t", t=CHUNK),
               cum[:, :, CHUNK - 1:CHUNK].broadcast_to([P, 16, CHUNK]), cum, ALU.subtract
               ).then_inc(S("toend_ready"), 1)
            dve.wait_ge(S("decay_ready"), 1)
            wait_read(dve, "k0", "k1")
            tt(half(5, 0), half(4, 0), la, ALU.mult).then_inc(S("kdec_ready"), 1)
            wait_read(dve, "csq")
            v.reciprocal(mean, slab[:, 1, 0:T]).then_inc(S("conv_rstd"), 1)
            dve.wait_ge(S("conv_rstd"), 1)
            for c in range(DC):
                tt(chan(3)[:, c, :], chan(3)[:, c, :], mean, ALU.mult).then_inc(S("conv_normed"), 1)
            for t in range(TT):
                o = wait_full(dve, f"kdt{t}")
                read(v.tensor_copy(slab[:, 5, 1024 + 512 * t:1536 + 512 * t], o[:]), f"kdt{t}")
            dve.wait_ge(S("decay_ready"), 2)
            for n in range(NCH):
                for hp in range(2):
                    o = wait_full(dve, f"kv{2 * n + hp}")
                    if n:
                        wait_read(dve, f"kv{2 * n - 2 + hp}")
                    for m in range(2):
                        h = 2 * hp + m
                        if n == 0:
                            ins = v.tensor_copy(states(n, h), o[:, HV * m:HV * m + HV])
                        else:
                            ins = stt(states(n, h), states(n - 1, h), small[:, 4 * h + n:4 * h + n + 1],
                                      o[:, HV * m:HV * m + HV], ALU.mult, ALU.add)
                    read(ins, f"kv{2 * n + hp}")
            for j in range(2):
                wait_read(dve, f"osum{j}")
            v.reciprocal(slab[:, 7, 1024:2048], slab[:, 7, 1024:2048]).then_inc(S("o_rstd"), 1)
            dve.wait_ge(S("o_rstd"), 1)
            for c in range(DC):
                ins = stt(chan(10)[:, c, :], chan(10)[:, c, :], col("gla_g", c), half(7, 1)[:, c // 2, :],
                          ALU.mult, ALU.mult)
            ins.then_inc(S("o_normed"), 1)
            dve.wait_ge(S("o_normed"), 1)
            wait_read(dve, "r0", "r1", "r2", "r3")
            tt(slab[:, 10, :], slab[:, 10, :], slab[:, 3, :], ALU.mult).then_inc(S("gla_ready"), 1)
            wait_read(dve, "ga0", "ga1", "ga2", "ga3", "gb0", "gb1", "gb2", "gb3")
            for j in range(4):
                o = wait_full(dve, f"yc{j}")
                for m in range(2):
                    c = 2 * j + m
                    ins = stt(chan(5)[:, c, :], o[:, T * m:T * m + T], col("b_co", c), chan(5)[:, c, :],
                              ALU.add, ALU.mult)
                read(ins, f"yc{j}")
            for j in range(4):
                o = wait_full(dve, f"yg{j}")
                gb = slab[:, 6, 512 * j:512 * j + 512]
                mj = slab[:, 5, 512 * j:512 * j + 512]
                read(tt(gb, o[:], gb, ALU.mult), f"yg{j}")
                wait_read(dve, f"yg{j}", f"yc{j}")
                tt(mj, mj, gb, ALU.add).then_inc(S("merged_ready"), 1)
            dve.wait_ge(S("x_landed"), 16)
            dve.wait_ge(S("small_landed"), 16 * SMALL_LOADS)
            x = tok(2)
            for t in range(TT):
                stt(x[:, t, :], x[:, t, :], ALPHA, rows[:, 1, :], ALU.mult, ALU.add).then_inc(S("x_scaled"), 1)
            dve.wait_ge(S("x_scaled"), TT)
            for u in range(2):
                for t in range(TT):
                    o = wait_full(dve, f"mix{u}_{t}")
                    xs = x[:, t, 512 * u:512 * u + 512]
                    read(tt(xs, xs, o[:], ALU.add), f"mix{u}_{t}")

            def layer_norm(src, dst, t, g, b, at, std_at, done):
                k = done + t
                st = small[:, 160 + 12 * t:172 + 12 * t].rearrange("p (a b) -> p a b", a=2)
                for u in range(2):
                    v.bn_stats(st[:, u, :], src[:, t, 512 * u:512 * u + 512]).then_inc(S("ln_bn"), 1)
                dve.wait_ge(S("ln_bn"), 2 * k + 2)
                v.bn_aggr(small[:, at + 2 * t:at + 2 * t + 2], st).then_inc(S("ln_stats"), 1)
                dve.wait_ge(S("ln_std"), k + 1)
                rs = small[:, std_at + 2 + t:std_at + 3 + t]
                v.reciprocal(rs, small[:, std_at + t:std_at + t + 1]).then_inc(S("ln_rstd"), 1)
                dve.wait_ge(S("ln_rstd"), k + 1)
                ts(dst[:, t, :], src[:, t, :], small[:, at + 2 * t:at + 2 * t + 1], rs, ALU.subtract, ALU.mult
                   ).then_inc(S("ln_a"), 1)
                dve.wait_ge(S("ln_a"), k + 1)
                tt(dst[:, t, :], dst[:, t, :], g, ALU.mult).then_inc(S("ln_b"), 1)
                dve.wait_ge(S("ln_b"), k + 1)
                return tt(dst[:, t, :], dst[:, t, :], b, ALU.add)

            dve.wait_ge(S("small_landed"), 16 * SMALL_LOADS)
            dve.wait_ge(S("ln1b_landed"), 16)
            for t in range(TT):
                wait_read(dve, f"mix0_{t}", f"mix1_{t}")
                layer_norm(x, tok(0), t, rows[:, 2, :], rows[:, 0, :], 16, 20, 0).then_inc(S("x1_ready"), 1)
            dve.wait_ge(S("x1_ready"), TT)
            v.memset(zeros, 0.0).then_inc(S("zeros_ready"), 1)
            dve.wait_ge(S("small_landed"), 16 * SMALL_LOADS)
            o = wait_full(dve, "lg")
            for t in range(TT):
                ins = tt(logit[:, t, :], o[:, 128 * t:128 * t + 72], b_route[:], ALU.add)
            read(ins, "lg")
            wait_read(dve, "lg")
            dve.wait_ge(S("consts_ready"), CONSTS)
            for t in range(TT):
                v.max(g_top[:, t, :], logit[:, t, 0:NG]).then_inc(S("route_step"), 1)
            dve.wait_ge(S("route_step"), 2)
            for t in range(TT):
                v.max_index(g_idx[:, t, :], g_top[:, t, :], logit[:, t, 0:NG]).then_inc(S("route_step"), 1)
            for t in range(TT):
                ts(small[:, 30 + t:31 + t], g_top[:, t, 0:1], -1.0, None, ALU.mult).then_inc(S("gtop_ready"), 1)
            dve.wait_ge(S("route_step"), 4)
            gi = small[:, 38:40]
            v.tensor_copy(gi, g_idx[:, :, 0:1].rearrange("p t a -> p (t a)")).then_inc(S("route_step"), 1)
            dve.wait_ge(S("route_step"), 5)
            for t in range(TT):
                ts(onehot[:, t, :], numbers[:, 0:NG], gi[:, t:t + 1], None, ALU.is_equal).then_inc(S("route_step"), 1)
            dve.wait_ge(S("route_step"), 7)
            for t in range(TT):
                tt(picked[:, t, :, :], logit[:, t, NG:].rearrange("p (g i) -> p i g", g=NG),
                   onehot[:, t:t + 1, :].broadcast_to([P, EPG, NG]), ALU.mult).then_inc(S("route_step"), 1)
            dve.wait_ge(S("route_step"), 9)
            for t in range(TT):
                v.tensor_reduce(e_log[:, t, :], picked[:, t, :, :], AX_X, ALU.add).then_inc(S("route_step"), 1)
            dve.wait_ge(S("route_step"), 11)
            for t in range(TT):
                v.max(e_top[:, t, :], e_log[:, t, :]).then_inc(S("route_step"), 1)
            dve.wait_ge(S("route_step"), 13)
            for t in range(TT):
                v.max_index(e_idx[:, t, :], e_top[:, t, :], e_log[:, t, :]).then_inc(S("route_step"), 1)
            tt(small[:, 34:36], e_top[:, :, 1:2].rearrange("p t a -> p (t a)"),
               e_top[:, :, 0:1].rearrange("p t a -> p (t a)"), ALU.subtract).then_inc(S("ediff_ready"), 1)
            dve.wait_ge(S("route_step"), 15)
            ef = small[:, 156:160]
            v.tensor_copy(ef.rearrange("p (t a) -> p t a", t=TT), e_idx[:, :, 0:2]).then_inc(S("route_step"), 1)
            dve.wait_ge(S("route_step"), 16)
            for t in range(TT):
                stt(small[:, 184 + 2 * t:186 + 2 * t], gi[:, t:t + 1].broadcast_to([P, 2]), float(EPG),
                    ef[:, 2 * t:2 * t + 2], ALU.mult, ALU.add).then_inc(S("route_step"), 1)
            dve.wait_ge(S("route_step"), 18)
            for t in range(TT):
                ts(mask_a[:, t, :], numbers[:], small[:, 184 + 2 * t:185 + 2 * t], None, ALU.is_equal
                   ).then_inc(S("route_step"), 1)
                ts(mask_b[:, t, :], numbers[:], small[:, 185 + 2 * t:186 + 2 * t], None, ALU.is_equal
                   ).then_inc(S("route_step"), 1)
            dve.wait_ge(S("route_step"), 22)
            tt(mask, mask_a, mask_b, ALU.add).then_inc(S("mask_ready"), 1)
            dve.wait_ge(S("ratio_ready"), 1)
            dve.wait_ge(S("gsum_ready"), TT)
            den, w0, w1 = small[:, 188:190], small[:, 190:192], small[:, 24:26]
            stt(den, small[:, 36:38], 1.0, small[:, 32:34], ALU.add, ALU.mult).then_inc(S("route_step"), 1)
            dve.wait_ge(S("route_step"), 23)
            v.reciprocal(w0, den).then_inc(S("route_step"), 1)
            dve.wait_ge(S("route_step"), 24)
            tt(w1, w0, small[:, 36:38], ALU.mult).then_inc(S("route_step"), 1)
            dve.wait_ge(S("route_step"), 25)
            dve.wait_ge(S("consts_ready"), CONSTS)
            for t in range(TT):
                ts(mask_a[:, t, :], mask_a[:, t, :], w0[:, t:t + 1], None, ALU.mult).then_inc(S("route_step"), 1)
            dve.wait_ge(S("route_step"), 27)
            for t in range(TT):
                wt = meta[:, 0:NE, 2 + t:3 + t].rearrange("p n a -> p (n a)")
                stt(wt, mask_b[:, t, :], w1[:, t:t + 1], mask_a[:, t, :], ALU.mult, ALU.add
                    ).then_inc(S("route_step"), 1)
            o = wait_full(dve, "pos")
            stt(slotted, o[:, 0:128], 1.0, mask.rearrange("p t n -> p (t n)"), ALU.add, ALU.mult
                ).then_inc(S("route_step"), 1)
            v.tensor_reduce(small[:, 26:27], o[:, 128:192], AX_X, ALU.max).then_inc(S("route_step"), 1)
            dve.wait_ge(S("route_step"), 31)
            read(ts(over[:], small[:, 26:27], float(CAP), None, ALU.is_gt), "pos")
            v.memset(spread[:, 1, :], 0.0).then_inc(S("spread_copied"), 1)
            v.memset(y_sb[:, 1, 512:1024], 0.0).then_inc(S("y1_copied"), 1)
            dve.wait_ge(S("route_step"), 31)
            ts(meta[:, 0:NE, 0:2].rearrange("p n t -> p t n"), slotted.rearrange("p (t n) -> p t n", t=TT),
               -1.0, None, ALU.add).then_inc(S("meta_ready"), 1)

            def select(f, par, r):
                m = meta[:, bass.ds(f, 1), :] if not isinstance(f, int) else meta[:, f:f + 1, :]
                v.tensor_copy(meta_f[:, par, :], m.rearrange("p a b -> p (a b)")).then_inc(S("metaf_ready"), 1)
                dve.wait_ge(S("metaf_ready"), r * META + f + 1)
                for t in range(TT):
                    ts(sel[:, par, t, :], slots[:, 0:CAP], meta_f[:, par, t:t + 1], None,
                       ALU.is_equal).then_inc(S("sel_ready"), 1)
                for t in range(TT):
                    ts(selw[:, par, t, :], slots[:], meta_f[:, par, t:t + 1], meta_f[:, par, 2 + t:3 + t],
                       ALU.is_equal, ALU.mult).then_inc(S("selw_ready"), 1)

            def expert(e, q, r):
                n = r * NE + e
                dve.wait_ge(S("up_full"), n + 1)
                v.tensor_copy(u_sb, up_bank[:]).then_inc(S("u_copied"), 1)
                dve.wait_ge(S("spread_full"), n + 1)
                v.tensor_copy(spread[:, q, :], y_bank[:, 0:256]).then_inc(S("spread_copied"), 1)
                dve.wait_ge(S("silu_ready"), n + 1)
                tt(slab[:, 1, 1664:1792], slab[:, 1, 1536:1664], gate_bank[:, 128:256], ALU.mult
                   ).then_inc(S("h_ready"), 1)
                dve.wait_ge(S("y1_full"), n + 1)
                v.tensor_copy(y_sb[:, q, 512:1024], up_bank[:]).then_inc(S("y1_copied"), 1)
                select(e + 2, q, r)

            dve.wait_ge(S("meta_ready"), 1)
            dve.wait_ge(S("consts_ready"), CONSTS)
            for f in range(2):
                select(f, f, 0)
            with dve.Fori(0, NE // 2) as it:
                for q in range(2):
                    expert(2 * it + q, q, 0)
            more = dve.value_load(over[0:1, 0:1], min_val=0, max_val=1)
            with dve.If(more > 0):
                with dve.Fori(1, ROUNDS) as r:
                    dve.wait_ge(S("combined"), r * (NE + 1))
                    ts(meta[:, :, 0:TT], meta[:, :, 0:TT], -float(CAP), None, ALU.add).then_inc(S("meta_moved"), 1)
                    dve.wait_ge(S("meta_moved"), r)
                    for f in range(2):
                        select(f, f, r)
                    v.memset(spread[:, 1, :], 0.0).then_inc(S("spread_copied"), 1)
                    v.memset(y_sb[:, 1, 512:1024], 0.0).then_inc(S("y1_copied"), 1)
                    with dve.Fori(0, NE // 2) as it:
                        for q in range(2):
                            expert(2 * it + q, q, r)
                dve.wait_ge(S("combined"), ROUNDS * (NE + 1))
            dve.wait_ge(S("combined"), NE + 1)
            dve.wait_ge(S("ln2_landed"), 32)
            for t in range(TT):
                for hf in range(2):
                    d = tok(10)[:, t, 512 * hf:512 * hf + 512]
                    stt(d, tok(0)[:, t, 512 * hf:512 * hf + 512], ALPHA, acc[t][hf][:], ALU.mult, ALU.add
                        ).then_inc(S("moe_out"), 1)
                dve.wait_ge(S("moe_out"), 2 * t + 2)
                layer_norm(tok(10), tok(10), t, rows[:, 1, :], rows[:, 2, :], 42, 46, TT
                           ).then_inc(S("x2_ready"), 1)

            def rms_apply(dst, done, at):
                for t in range(TT):
                    dve.wait_ge(S("rms_root"), done + t + 1)
                    rs = small[:, at + 2 + t:at + 3 + t]
                    v.reciprocal(rs, rs).then_inc(S("rms_inverse"), 1)
                    dve.wait_ge(S("rms_inverse"), done + t + 1)
                    ts(tok(dst)[:, t, :], tok(10)[:, t, :], rs, None, ALU.mult).then_inc(S("xn_ready"), 1)

            rms_apply(1, 0, 50)
            lam = cols[:, COLS["lam"]:COLS["lam"] + 8]
            stt(small[:, 72:80], lam, -1.0, lam, ALU.mult, ALU.min).then_inc(S("lam_negabs"), 1)
            dve.wait_ge(S("lam_exp"), 1)
            e_, d_, s_, s2, pl = (small[:, 80 + 8 * i:88 + 8 * i] for i in range(5))
            ts(d_, e_, 2.0, None, ALU.add).then_inc(S("rate_step"), 1)
            dve.wait_ge(S("rate_step"), 1)
            v.reciprocal(d_, d_).then_inc(S("rate_step"), 1)
            dve.wait_ge(S("rate_step"), 2)
            tt(s_, e_, d_, ALU.mult).then_inc(S("rate_step"), 1)
            dve.wait_ge(S("rate_step"), 3)
            tt(s2, s_, s_, ALU.mult).then_inc(S("rate_step"), 1)
            dve.wait_ge(S("rate_step"), 4)
            ts(pl, s2, 1.0 / 17, 1.0 / 15, ALU.mult, ALU.add).then_inc(S("rate_step"), 1)
            n = 5
            for k in (13, 11, 9, 7, 5, 3, 1):
                dve.wait_ge(S("rate_step"), n)
                tt(pl, pl, s2, ALU.mult).then_inc(S("rate_step"), 1)
                dve.wait_ge(S("rate_step"), n + 1)
                ts(pl, pl, 1.0 / k, None, ALU.add).then_inc(S("rate_step"), 1)
                n += 2
            dve.wait_ge(S("rate_step"), n)
            tt(pl, pl, s_, ALU.mult).then_inc(S("rate_step"), 1)
            ts(d_, lam, -1.0, 0.0, ALU.mult, ALU.max).then_inc(S("rate_step"), 1)
            dve.wait_ge(S("rate_step"), n + 2)
            stt(pl, pl, 2.0, d_, ALU.mult, ALU.add).then_inc(S("rate_step"), 1)
            dve.wait_ge(S("rate_step"), n + 3)
            ts(pl, pl, -8.0, None, ALU.mult).then_inc(S("rate_ready"), 1)
            for j in range(4):
                wait_read(dve, f"lx{j}")
                causal_conv(chan(1), chan(2), "lru_w", LRU_W, "lru_b", [(2 * j + m,) * 3 for m in range(2)],
                            "lru_tap", 2 * LRU_W * j)
            wait_read(dve, "li0", "li1", "li2", "li3")
            tt(slab[:, 5, :], slab[:, 5, :], slab[:, 2, :], ALU.mult).then_inc(S("ua_used"), 1)
            dve.wait_ge(S("a_ready"), 1)
            tt(slab[:, 1, :], slab[:, 4, :], slab[:, 4, :], ALU.mult).then_inc(S("asq"), 1)
            dve.wait_ge(S("asq"), 1)
            stt(slab[:, 6, :], slab[:, 1, :], 1.0, slab[:, 6, :], ALU.add, ALU.mult).then_inc(S("mult2_ready"), 1)
            dve.wait_ge(S("asq"), 1)
            v.memset(chan(4)[:, :, 0:1], 0.0).then_inc(S("a_cut"), 1)
            dve.wait_ge(S("mult_ready"), 1)
            dve.wait_ge(S("ua_used"), 1)
            tt(slab[:, 5, :], slab[:, 5, :], slab[:, 6, :], ALU.mult).then_inc(S("u_ready"), 1)
            dve.wait_ge(S("u_ready"), 1)
            dve.wait_ge(S("a_cut"), 1)
            v.tensor_tensor_scan(slab[:, 1, :], slab[:, 4, :], slab[:, 5, :], 0.0, ALU.mult, ALU.add
                                 ).then_inc(S("lru_done"), 1)
            dve.wait_ge(S("lru_done"), 1)
            wait_read(dve, "lg_0", "lg_1", "lg_2", "lg_3")
            tt(slab[:, 1, :], slab[:, 1, :], slab[:, 3, :], ALU.mult).then_inc(S("ya_ready"), 1)
            wait_read(dve, "ksum")
            v.reciprocal(k_sq, k_sq).then_inc(S("k_rstd"), 1)
            dve.wait_ge(S("k_rstd"), 1)
            stt(slab[:, 7, 0:512], slab[:, 7, 0:512], col("k_norm"), k_sq, ALU.mult, ALU.mult
                ).then_inc(S("k_ready"), 1)
            wait_read(dve, "kiwi_w")
            steps = 0
            for t in range(TT):
                n = P * (t + 1)
                rel = slab[:, 4 + t, :].rearrange("p (h s) -> p h s", h=IH)
                for h in range(IH):
                    if h % 2 == 0:
                        wait_read(dve, f"dots{t}_{h // 2}")
                    w = indexer_head(h // 2, h % 2)
                    sc = score[:, t, 0:n]
                    if h == 0:
                        ins = ts(sc, rel[:, h, 0:n], wih[:, t, w:w + 1], None, ALU.mult)
                    else:
                        dve.wait_ge(S("score_step"), steps)
                        ins = stt(sc, rel[:, h, 0:n], wih[:, t, w:w + 1], sc, ALU.mult, ALU.add)
                    if h < IH - 1:
                        ins.then_inc(S("score_step"), 1)
                        steps += 1
                    else:
                        ins.then_inc(S("score_ready"), 1)
            for j in range(4):
                wait_read(dve, f"qsum{j}")
                r6 = slab[:, 6, 512 * j:512 * j + 512]
                q9 = slab[:, 9, 512 * j:512 * j + 512]
                v.reciprocal(r6, r6).then_inc(S("q_rstd"), 1)
                dve.wait_ge(S("q_rstd"), j + 1)
                stt(q9, q9, col("q_norm"), r6, ALU.mult, ALU.mult).then_inc(S("q_ready"), 1)
            steps = 0
            for t in range(TT):
                n = P * (t + 1)
                w_ = work[:, t, 0:n]
                dve.wait_ge(S("work_ready"), t + 1)
                for i in range(TOPK // 8):
                    if steps:
                        dve.wait_ge(S("top_step"), steps)
                    v.max(best, w_).then_inc(S("top_step"), 1)
                    dve.wait_ge(S("top_step"), steps + 1)
                    v.match_replace(w_, best, w_, TAKEN).then_inc(S("top_step"), 1)
                    steps += 2
                dve.wait_ge(S("top_step"), steps)
                ts(score[:, t, 0:n], w_, 2.0 * FILL, HIDE, ALU.is_gt, ALU.mult).then_inc(S("hide_made"), 1)
            wait_read(dve, "gc0", "gc1", "gc2", "gc3")
            for j in range(4):
                o = wait_full(dve, f"ya{j}")
                m3 = slab[:, 3, 512 * j:512 * j + 512]
                read(tt(m3, o[:], m3, ALU.mult), f"ya{j}")
            for t in range(TT):
                n = P * (t + 1)
                dve.wait_ge(S("bias_landed"), 16 * (t + 1))
                dve.wait_ge(S("hide_ready"), t + 1)
                if t:
                    for k in range(2):
                        wait_full(dve, f"pt0_0_{k}")
                for j in range(4):
                    o = wait_full(dve, f"log{t}_{j}")
                    dst = lgt[:, 2 * j:2 * j + 2, 0:n]
                    bias = slab[:, 2, 512 * j:512 * j + 512].rearrange("p (m s) -> p m s", m=2)[:, :, ::-1][:, :, 0:n]
                    read(stt(dst, o[:].rearrange("p (m s) -> p m s", m=2)[:, :, 0:n], HD ** -0.5, bias,
                             ALU.mult, ALU.add), f"log{t}_{j}")
                    wait_read(dve, f"log{t}_{j}")
                    tt(dst, dst, score[:, t:t + 1, 0:n].broadcast_to([P, 2, n]), ALU.add
                       ).then_inc(S("logits_ready"), 1)
                dve.wait_ge(S("logits_ready"), 4 * (t + 1))
                v.tensor_reduce(small[:, 128:136], lgt[:, :, 0:n], AX_X, ALU.max).then_inc(S("rowmax"), 1)
                dve.wait_ge(S("rowmax"), t + 1)
                ts(small[:, 128:136], small[:, 128:136], -1.0, None, ALU.mult).then_inc(S("rowmax_ready"), 1)
                dve.wait_ge(S("exp_ready"), t + 1)
                v.reciprocal(small[:, 136:144], small[:, 136:144]).then_inc(S("rowsum"), 1)
                dve.wait_ge(S("rowsum"), t + 1)
                tt(lgt[:, :, 0:n], lgt[:, :, 0:n],
                   small[:, 136:144].rearrange("p (h a) -> p h a", a=1).broadcast_to([P, NH, n]), ALU.mult
                   ).then_inc(S("probs_ready"), 1)
            wait_read(dve, "gd0", "gd1", "gd2", "gd3")
            for j in range(4):
                o = wait_full(dve, f"yb{j}")
                g1 = slab[:, 1, 512 * j:512 * j + 512]
                m3 = slab[:, 3, 512 * j:512 * j + 512]
                read(tt(g1, o[:], g1, ALU.mult), f"yb{j}")
                wait_read(dve, f"yb{j}", f"ya{j}")
                tt(m3, m3, g1, ALU.add).then_inc(S("merged2_ready"), 1)

            def residual(pre):
                for u in range(2):
                    for t in range(TT):
                        o = wait_full(dve, f"{pre}{u}_{t}")
                        xs = tok(10)[:, t, 512 * u:512 * u + 512]
                        read(tt(xs, xs, o[:], ALU.add), f"{pre}{u}_{t}")

            residual("mo")
            rms_apply(4, TT, 54)
            for i in range(6):
                wait_read(dve, f"fg{i}_0", f"fg{i}_1")
                if i == 0:
                    wait_read(dve, "x3t3")
                if i >= 2:
                    wait_read(dve, f"fu{i - 2}_0", f"fu{i - 2}_1")
                causal_conv(half(4, i % 2), half(5, i % 2), "ffn_w", FFN_W, "ffn_b",
                            [(c, c, 4 * i + c) for c in range(4)], "ffn_tap", 4 * FFN_W * i)
                dve.wait_ge(S("fgelu_ready"), i + 1)
                for j in range(2):
                    o = wait_full(dve, f"fu{i}_{j}")
                    c = 4 * i + 2 * j
                    read(tt(hT[:, c:c + 2, :].rearrange("p a t -> p (a t)"), o[:],
                            half(5, i % 2)[:, 2 * j:2 * j + 2, :].rearrange("p a t -> p (a t)"), ALU.mult),
                         f"fu{i}_{j}")
            residual("dn")
            rms_apply(4, 2 * TT, 62)
            for u in range(2):
                for t in range(TT):
                    o = wait_full(dve, f"pp{u}_{t}")
                    read(v.tensor_copy(tok(5)[:, t, 512 * u:512 * u + 512], o[:]), f"pp{u}_{t}")
            for u in range(2):
                for t in range(TT):
                    wait_read(dve, f"pg{u}_{t}", f"pp{u}_{t}")
                    gate = tok(4)[:, t, 512 * u:512 * u + 512]
                    tt(gate, gate, tok(5)[:, t, 512 * u:512 * u + 512], ALU.mult).then_inc(S("ple_step"), 1)
                    dve.wait_ge(S("ple_step"), 2 * u + t + 1)
                    xs = tok(10)[:, t, 512 * u:512 * u + 512]
                    ins = tt(xs, xs, gate, ALU.add)
                    if u:
                        ins.then_inc(S("out_ready"), 1)


def _bucket_rows():
    dist = np.maximum(np.arange(511) - (T - 1), 0)
    exact = NB // 2
    far = exact + (np.log(np.maximum(dist, 1).astype(np.float32) / exact) / np.float32(np.log(MAXD / exact))
                   * (NB - exact)).astype(np.int32)
    bucket = np.where(dist < exact, dist, np.minimum(far, NB - 1))
    return (np.arange(NB)[:, None] == bucket[None, :]).astype(np.float32)


def _unit(w):
    return w.reshape(-1, P, w.shape[1]).transpose(1, 0, 2).reshape(P, -1)


def _layout(i):
    f = {k: np.asarray(v) for k, v in i.items()}
    w_in, b_in = f["w_in"][0], f["b_in"][0]
    at = np.cumsum([0, D, D, 512, 512, D, D, RANK, D, D])
    ca, cg, q, k, vv, r, fl, ga, gb = (w_in[:, at[j]:at[j + 1]] for j in range(9))
    bca, bcg, bq, bk, bv, br, bfl, bga, bgb = (b_in[at[j]:at[j + 1]] for j in range(9))

    def two(w):
        return [w[:, 0:512], w[:, 512:1024]]

    first = [cg[:, :512], ca[:, :512], cg[:, 512:], ca[:, 512:], k] + two(vv) + [q] + two(r) + two(ga) + two(gb)
    first += two(f["w_conv_out"][0]) + two(f["w_gla_out"][0]) + two(f["w_out"][0])
    units1 = np.stack([_unit(w) for w in first])

    w2 = f["w_in_2"][0]
    at = np.cumsum([0, D, D, D, 256, 256, 512, 64, 8, D, D])
    lx, lg, q2, k2, v2, qi, ki, wi, gc, gd = (w2[:, at[j]:at[j + 1]] for j in range(10))
    up = f["w_up_2"][0]
    down = f["w_down_2"][0]
    second = two(lx) + two(lg) + [np.concatenate([k2, v2], 1), qi]
    units2 = [_unit(w) for w in second]
    units2.append(np.concatenate([f["lru_wa_2"][0], f["lru_wx_2"][0]]).transpose(1, 0, 2).reshape(P, -1))
    units2 += [_unit(w) for w in two(q2) + two(gc) + two(f["w_lru_br_2"][0]) + two(gd) + two(f["w_attn_br_2"][0])
               + two(f["w_out_2"][0])]
    for j in range(6):
        units2 += [_unit(up[:, 512 * j:512 * j + 512]), _unit(up[:, FF + 512 * j:FF + 512 * j + 512])]
    for u in range(2):
        for j in range(3):
            units2.append(_unit(down[D * j:D * j + D, 512 * u:512 * u + 512]))
    units2.append(_unit(f["w_ple_proj_2"][0]))
    units2 += [_unit(w) for w in two(f["w_ple_gate_2"][0])]
    full2 = np.zeros((len(units2), P, UNIT), np.float32)
    for j, w in enumerate(units2):
        full2[j, :, :w.shape[1]] = w

    def per_channel(x):
        return x.reshape(-1, P).T

    cols = np.zeros((P, NCOLS), np.float32)

    def put(name, x):
        cols[:x.shape[0], COLS[name]:COLS[name] + x.shape[1]] = x

    for name, x in (("b_conv_a", bca), ("b_conv_g", bcg), ("b_q", bq), ("b_k", bk), ("b_r", br), ("b_ga", bga),
                    ("b_gb", bgb), ("conv_b", f["conv_b"]), ("cln_g", f["conv_ln_g"]), ("cln_b", f["conv_ln_b"]),
                    ("b_co", f["b_conv_out"]), ("b_gate", f["b_gate_up"]), ("gla_g", f["gla_norm_g"]),
                    ("mix_norm", f["mix_norm_2"]), ("lru_b", f["lru_conv_b_2"]), ("lru_ba", f["lru_ba_2"]),
                    ("lru_bx", f["lru_bx_2"]), ("lam", f["lru_lambda_2"]), ("q_norm", f["q_norm_2"]),
                    ("k_norm", f["k_norm_2"]), ("ffn_norm", f["ffn_norm_2"]), ("ffn_b", f["ffn_conv_b_2"]),
                    ("ple_norm", f["ple_norm_2"])):
        put(name, per_channel(x))
    put("b_flr", bfl[:, None])
    for name, x in (("conv_w", f["conv_w"]), ("lru_w", f["lru_conv_w_2"]), ("ffn_w", f["ffn_conv_w_2"])):
        put(name, x[0].reshape(x.shape[1], -1, P).transpose(2, 1, 0).reshape(P, -1))

    route = np.concatenate([f["w_router_group"][0], f["w_router_expert"][0]], 1)
    return {
        "xT": np.ascontiguousarray(_unit(f["x"][0].T)), "x": f["x"],
        "cols": cols, "units1": units1, "units2": full2,
        "w1": f["w1"][0], "w3": f["w3"][0], "w2": f["w2"][0],
        "w_flr": np.ascontiguousarray(_unit(fl).reshape(P, DC, RANK)), "w_gate_up": f["w_gate_up"][0],
        "b_v": bv, "b_out": f["b_out"][0], "ln1_g": f["ln1_g"][0], "ln1_b": f["ln1_b"][0],
        "ln2_g": f["ln2_g"][0], "ln2_b": f["ln2_b"][0],
        "w_route": np.ascontiguousarray(_unit(route).reshape(P, DC, NG + NE)),
        "b_route": np.concatenate([f["b_router_group"][0], f["b_router_expert"][0]]),
        "w_kiwi": np.ascontiguousarray(_unit(np.concatenate([ki, ki, wi], 1))),
        "rel_bias": f["rel_bias_2"], "buckets": _bucket_rows(),
        "pT": np.ascontiguousarray(_unit(f["p_2"][0, 0].T)),
    }


def kernel(**inputs):
    import concourse.bacc as bacc
    from concourse.bass_utils import run_bass_kernel_spmd

    nc = bacc.Bacc("TRN2", target_bir_lowering=False, num_devices=1)
    arrays, aps = {}, {}
    for name, x in _layout(inputs).items():
        x = np.ascontiguousarray(x)
        arrays[f"in_{name}"] = x
        aps[name] = nc.dram_tensor(f"in_{name}", x.shape, mybir.dt.from_np(x.dtype), kind="ExternalInput").ap()
    out = nc.dram_tensor("out", (1, T, D), F32, kind="ExternalOutput").ap()
    build(nc, aps, out)
    return run_bass_kernel_spmd(nc, [arrays], core_ids=[0]).results[0]["out"]
```

```python
from contextlib import ExitStack

import numpy as np

import concourse.bass as bass
from concourse import mybir

ALU = mybir.AluOpType
ACT = mybir.ActivationFunctionType
F32 = mybir.dt.float32
F32R = mybir.dt.float32r
I32 = mybir.dt.int32
U32 = mybir.dt.uint32
AX_X = mybir.AxisListType.X

P = 128
T = 256
TT = T // P
D = 1024
DC = D // P
UNIT = 4096
RING = 6
V_LAGS = (4, 12)
STREAM = 4
ALPHA = 2.0 ** 0.25

CONV_W = 31
CHUNK = 64
NCH = T // CHUNK
H1, HK, HV = 4, 128, 256
RANK = 16
TAU = 16.0

NG, EPG = 8, 8
NE = NG * EPG
SMALL_LOADS = 7
CONSTS = 9
CAP = 32
ROUNDS = T // CAP
META = NE + 2

NH, NKV, HD = 8, 2, 128
QPK = NH // NKV
IH, ID = 8, 64
TOPK = 64
NB, MAXD = 32, 128
LRU_W = 4
FF = 3072
FFC = FF // P
FFN_W = 3
PLE = 256
FILL = -1.0e38
TAKEN = -3.0e38
HIDE = -1.0e30

COLS = {}
_n = 0
for _name, _w in (("b_conv_a", 8), ("b_conv_g", 8), ("b_q", 4), ("b_k", 4), ("b_r", 8), ("b_flr", 1),
                  ("b_ga", 8), ("b_gb", 8), ("conv_w", 8 * CONV_W), ("conv_b", 8), ("cln_g", 8), ("cln_b", 8),
                  ("b_co", 8), ("b_gate", 4), ("gla_g", 8), ("mix_norm", 8), ("lru_w", 8 * LRU_W),
                  ("lru_b", 8), ("lru_ba", 8), ("lru_bx", 8), ("lam", 8), ("q_norm", 1), ("k_norm", 1),
                  ("ffn_norm", 8), ("ffn_w", FFC * FFN_W), ("ffn_b", FFC), ("ple_norm", 8)):
    COLS[_name] = _n
    _n += _w
NCOLS = _n

def _tasks():
    names = []
    names += ["g0", "g1", "a0", "a1", "g2", "g3", "a2", "a3", "k0", "k1", "fl", "z0", "z1"]
    names += [f"v{u}_{t}" for u in range(2) for t in range(2)] + ["q0", "q1"]
    names += [f"r{j}" for j in range(4)] + [f"ga{j}" for j in range(4)]
    names += ["csum", "kdt0", "kdt1"] + [f"kv{i}" for i in range(8)] + ["gb0", "gb1", "csq"]
    names += [f"o{h}" for h in range(4)] + ["gb2", "gb3", "osum0", "osum1"]
    names += [f"yc{j}" for j in range(4)] + [f"yg{j}" for j in range(4)]
    names += [f"mix{u}_{t}" for u in range(2) for t in range(2)]
    names += [f"x1t{j}" for j in range(4)] + ["lg", "pos"]
    first = list(names)
    n2 = [f"x2t{j}" for j in range(4)] + ["kiwi_k", "kiwi_w", "relb"]
    n2 += [f"lx{j}" for j in range(4)] + [f"lg_{j}" for j in range(4)]
    n2 += ["kk", "vv", "qi0", "qi1"]
    n2 += [f"lr{j}" for j in range(4)] + [f"li{j}" for j in range(4)]
    n2 += ["ksum"]
    n2 += [f"qq{j}" for j in range(4)] + [f"gc{j}" for j in range(4)]
    n2 += [f"dots{t}_{j}" for t in range(2) for j in range(4)]
    n2 += [f"qsum{j}" for j in range(4)]
    n2 += [f"ya{j}" for j in range(4)] + [f"gd{j}" for j in range(4)]
    for t in range(2):
        n2 += [f"log{t}_{j}" for j in range(4)]
    for t in range(2):
        n2 += [f"pt{t}_{s}_{k}" for s in range(t + 1) for k in range(2)] + [f"pv{t}_{k}" for k in range(2)]
    n2 += [f"yb{j}" for j in range(4)] + [f"mo{u}_{t}" for u in range(2) for t in range(2)]
    n2 += [f"x3t{j}" for j in range(4)]
    for i in range(6):
        n2 += [f"fg{i}_0", f"fg{i}_1", f"fu{i}_0", f"fu{i}_1"]
    n2 += [f"dn{u}_{t}" for u in range(2) for t in range(2)]
    n2 += [f"pp{u}_{t}" for u in range(2) for t in range(2)]
    n2 += [f"x4t{j}" for j in range(4)]
    n2 += [f"pg{u}_{t}" for u in range(2) for t in range(2)]
    return first, n2


TASKS1, TASKS2 = _tasks()
TASK = {name: i for i, name in enumerate(TASKS1 + TASKS2)}

UNITS1 = ["g1", "a1", "g3", "a3", "k1", "v0_1", "v1_1", "q1", "r1", "r3", "ga1", "ga3", "gb1", "gb3",
          "yc1", "yc3", "yg1", "yg3", "mix0_1", "mix1_1"]
UNITS2 = (["lx1", "lx3", "lg_1", "lg_3", "vv", "qi1", "li3", "qq1", "qq3", "gc1", "gc3", "ya1", "ya3",
           "gd1", "gd3", "yb1", "yb3", "mo0_1", "mo1_1"]
          + [f"f{x}{i}_1" for i in range(6) for x in "gu"]
          + ["dn0_1/1", "dn0_1/2", "dn0_1", "dn1_1/1", "dn1_1/2", "dn1_1", "pp1_1", "pg0_1", "pg1_1"])
UNITS = (UNITS1, UNITS2)
SPLIT = (UNITS1[2:], [n for n in UNITS2 if n not in ("li3", "ya1", "ya3", "pp1_1")])
assert len(UNITS1) % STREAM == 0 and len(SPLIT[0]) % 2 == 0


def by_rows(name):
    return name[:2] in ("v0", "v1", "dn", "pg", "mo") or name[:3] == "mix"


def build(nc, a, out):
    with ExitStack() as ctx:
        def sb(name, shape, dt=F32):
            return ctx.enter_context(nc.sbuf_tensor(name, shape, dt))

        sems = {}

        def S(name):
            if name not in sems:
                sems[name] = ctx.enter_context(nc.semaphore(name))
            return sems[name]

        banks = [ctx.enter_context(nc.psum_tensor(f"bank{i}", [P, 512], F32)) for i in range(8)]
        shapes = {"ring": [P, RING, UNIT], "slab": [P, 11, 2048], "rows": [P, 3, D]}
        with ExitStack() as names:
            parts = {name: names.enter_context(nc.sbuf_tensor(f"{name}_parts", shape, F32R))
                     for name, shape in shapes.items()}
        ring, slab, rows = (sb(name, shape) for name, shape in shapes.items())
        cols = sb("cols", [P, NCOLS])
        w_flr = sb("w_flr", [P, DC, RANK])
        w_route = sb("w_route", [P, DC, NG + NE])
        b_route = sb("b_route", [P, NG + NE])
        ident = sb("ident", [P, P])
        ones = sb("ones", [P, P])
        before = sb("before", [P, P])
        stack = sb("stack", [P, CAP])
        slots = sb("slots", [P, P])
        slots_i = sb("slots_i", [P, P], I32)
        numbers = sb("numbers", [P, NE])
        numbers_i = sb("numbers_i", [P, NE], I32)
        eps_ln = sb("eps_ln", [P, 1])
        eps_rms = sb("eps_rms", [P, 1])
        small = sb("small", [P, 192])
        meta = sb("meta", [P, META, 4])
        g_top = sb("g_top", [P, TT, 8])
        g_idx = sb("g_idx", [P, TT, 8], U32)
        e_top = sb("e_top", [P, TT, 8])
        e_idx = sb("e_idx", [P, TT, 8], U32)
        over = sb("over", [P, 1], I32)
        bias_dram = nc.dram_tensor("bias_scratch", (NH, 512), F32, kind="Internal").ap()

        def col(name, i=0):
            return cols[:, COLS[name] + i:COLS[name] + i + 1]

        def chan(s):
            return slab[:, s, :].rearrange("p (c t) -> p c t", c=DC)

        def tok(s):
            return slab[:, s, :].rearrange("p (t d) -> p t d", t=TT)

        def half(s, h):
            return slab[:, s, 1024 * h:1024 * h + 1024].rearrange("p (c t) -> p c t", c=4)

        xg = slab[:, 1, 0:DC * CAP].rearrange("p (c s) -> p c s", c=DC)
        g_sb = slab[:, 1, 512:1024]
        u_sb = slab[:, 1, 1024:1536]
        silu_sb = slab[:, 1, 1536:1664].rearrange("p (c s) -> p c s", c=4)
        h_sb = slab[:, 1, 1664:1792].rearrange("p (c s) -> p c s", c=4)
        y_sb = tok(2)
        spread = slab[:, 3, 0:512].rearrange("p (a t) -> p a t", a=2)
        sel = slab[:, 3, 512:640].rearrange("p (a t s) -> p a t s", a=2, t=TT)
        selw = slab[:, 3, 1024:1536].rearrange("p (a t s) -> p a t s", a=2, t=TT)
        meta_f = slab[:, 3, 640:648].rearrange("p (a b) -> p a b", a=2)
        zeros = slab[:, 4, 0:512]
        logit = slab[:, 5, 0:TT * 72].rearrange("p (t n) -> p t n", t=TT)
        mask = slab[:, 5, 256:256 + TT * NE].rearrange("p (t n) -> p t n", t=TT)
        mask_a = slab[:, 5, 384:384 + TT * NE].rearrange("p (t n) -> p t n", t=TT)
        mask_b = slab[:, 5, 512:512 + TT * NE].rearrange("p (t n) -> p t n", t=TT)
        picked = slab[:, 5, 640:640 + TT * 64].rearrange("p (t i g) -> p t i g", t=TT, i=EPG)
        e_log = slab[:, 5, 768:768 + TT * 8].rearrange("p (t n) -> p t n", t=TT)
        onehot = slab[:, 5, 784:784 + TT * 8].rearrange("p (t n) -> p t n", t=TT)
        e_exp = slab[:, 5, 800:800 + TT * 8].rearrange("p (t n) -> p t n", t=TT)
        kT = slab[:, 7, 0:512].rearrange("p (h t) -> p h t", h=NKV)
        v2 = slab[:, 7, 512:1024].rearrange("p (t n) -> p t n", t=TT)
        qiT = slab[:, 7, 1024:2048].rearrange("p (c t) -> p c t", c=4)
        kiT = slab[:, 8, 0:256]
        score = slab[:, 8, 256:768].rearrange("p (t s) -> p t s", t=TT)
        work = slab[:, 8, 768:1280].rearrange("p (t s) -> p t s", t=TT)
        k_sq = slab[:, 8, 1280:1792]
        wih = slab[:, 8, 1792:1808].rearrange("p (t h) -> p t h", t=TT)
        best = slab[:, 8, 1808:1816]
        lgt = slab[:, 4, :].rearrange("p (h s) -> p h s", h=NH)
        prob_t = slab[:, 5, :].rearrange("p (s h t) -> p s h t", s=TT, h=NH)
        hT = slab[:, 1:4, :].rearrange("p a (c t) -> p (a c) t", c=DC)
        turn_ = [banks[(TASK["pos"] + 1 + i) % 8] for i in range(8)]
        acc = [turn_[0:2], turn_[2:4]]
        gate_bank, up_bank, y_bank, gather_bank = turn_[4:8]

        def states(n, h):
            s, at = ((10, 1024), (4, 0), (4, 1024), (7, 1024))[n]
            return slab[:, s, at + HV * h:at + HV * h + HV]

        mean = slab[:, 10, 768:1024]
        conv_root = slab[:, 10, 0:T]
        slotted = slab[:, 5, 896:1024]

        def indexer_head(j, m):
            return 4 * (j // 2) + j % 2 + 2 * m

        def bank(task):
            return banks[TASK[task] % 8]

        def take_bank(task):
            if TASK[task] >= 8:
                nc.tensor.wait_ge(S(f"bank_read{TASK[task] % 8}"), TASK[task] // 8)
            return bank(task)

        def full(ins, task):
            ins.then_inc(S(f"bank_full{TASK[task] % 8}"), 1)

        def wait_full(eng, task):
            eng.wait_ge(S(f"bank_full{TASK[task] % 8}"), TASK[task] // 8 + 1)
            return bank(task)

        def read(ins, task):
            ins.then_inc(S(f"bank_read{TASK[task] % 8}"), 1)

        def wait_read(eng, *tasks):
            for task in tasks:
                eng.wait_ge(S(f"bank_read{TASK[task] % 8}"), TASK[task] // 8 + 1)

        def expert_slot(q, w):
            return 3 * q + w

        def wait_used(eng, name):
            if "/" in name:
                eng.wait_ge(S("down_used"), 2 * int(name[2]) + int(name[-1]))
            else:
                wait_full(eng, name)

        def wait_landed(eng, part, name):
            n = UNITS[part].index(name)
            eng.wait_ge(S(f"unit_landed{n % STREAM}"), 16 * (part * (len(UNITS1) // STREAM) + n // STREAM + 1))

        def split_count(part, name):
            return 2 * (part * len(SPLIT[0]) + SPLIT[part].index(name))

        def halves(part, name):
            slot_, high = ring[:, UNITS[part].index(name) % STREAM, :], ring[:, STREAM + SPLIT[part].index(name) % 2, :]
            if by_rows(name):
                return [tuple(x[:, 2048 * h:2048 * h + 2048] for x in (slot_, high)) for h in range(2)]
            return [tuple(x.rearrange("p (c n) -> p c n", c=DC)[:, :, 256 * h:256 * h + 256] for x in (slot_, high))
                    for h in range(2)]

        def r32(ap):
            return bass.AP(parts[ap.tensor.name], ap.offset, ap.ap)

        xt_parts = (chan(8), chan(9))
        conv_parts = (chan(4), chan(3))
        gla_parts = (chan(5), chan(10))
        merged_parts = (chan(8), chan(1))
        xn_parts = (chan(0), rows[:, 0:2, :].rearrange("p a (c t) -> p (a c) t", c=4))
        att_parts = (chan(9), chan(6))
        merged2_parts = (chan(7), chan(3))
        hid_parts = (hT, slab[:, 6:9, :].rearrange("p a (c t) -> p (a c) t", c=DC))

        block = ctx.enter_context(nc.Block())

        @block.sync
        def _(sp):
            sp.dma_start(slab[:, 0, :], a["xT"]).then_inc(S("xt_landed"), 16)
            for n, name in enumerate(UNITS1):
                if n >= STREAM:
                    wait_used(sp, UNITS1[n - STREAM])
                if name == "yg1":
                    wait_full(sp, "csq")
                    sp.dma_start(tok(2), a["x"].rearrange("o (t p) d -> p (o t) d", p=P)).then_inc(S("x_landed"), 16)
                    wait_read(sp, "v0_1", "v1_1")
                    sp.dma_start(rows[:, 0, :], a["ln1_b"].partition_broadcast(P)).then_inc(S("ln1b_landed"), 16)
                sp.dma_start(ring[:, n % STREAM, :], a["units1"][n]).then_inc(S(f"unit_landed{n % STREAM}"), 16)
                if n == 0:
                    sp.dma_start(cols[:], a["cols"]).then_inc(S("cols_landed"), 16)

            def expert_unit(e, q, w):
                name = ("w1", "w3", "w2")[w]
                src = a[name][bass.ds(e, 1) if not isinstance(e, int) else slice(e, e + 1)]
                src = src.rearrange("e (p c) n -> p (e c n)", p=P)
                sp.dma_start(ring[:, expert_slot(q, w), :], src).then_inc(S(f"expert_landed{3 * q + w}"), 16)

            used = ("gate_full", "up_full", "y1_full")

            def expert_pair(it, r):
                for q in range(2):
                    for w in range(3):
                        sp.wait_ge(S(used[w]), r * NE + 2 * it + q - 1)
                        expert_unit(2 * it + q, q, w)

            for q in range(2):
                for w in range(3):
                    s = expert_slot(q, w)
                    wait_used(sp, UNITS1[s - STREAM] if s < STREAM else SPLIT[0][s - RING])
                    expert_unit(q, q, w)
            with sp.Fori(1, NE // 2) as it:
                expert_pair(it, 0)
            wait_read(sp, "pos")
            more = sp.value_load(over[0:1, 0:1], min_val=0, max_val=1)
            with sp.If(more > 0):
                with sp.Fori(1, ROUNDS) as r:
                    with sp.Fori(0, NE // 2) as it:
                        expert_pair(it, r)
                for w in range(3):
                    sp.wait_ge(S(used[w]), ROUNDS * NE)
            for n, _task in enumerate(UNITS2):
                if n < STREAM:
                    sp.wait_ge(S(used[n % 3]), NE - 1 + n // 3)
                else:
                    wait_used(sp, UNITS2[n - STREAM])
                s = n % STREAM
                sp.dma_start(ring[:, s, :], a["units2"][n]).then_inc(S(f"unit_landed{s}"), 16)
            sp.wait_ge(S("out_ready"), TT)
            sp.dma_start(out.rearrange("o (t p) d -> p (o t) d", p=P), tok(10)).then_inc(S("out_stored"), 16)
            sp.wait_ge(S("out_stored"), 16)

        @block.gpsimd
        def _(pool):
            g = nc.gpsimd
            pool.dma_start(w_flr[:], a["w_flr"]).then_inc(S("small_landed"), 16)
            pool.dma_start(slab[0:RANK, 10, 0:512], a["w_gate_up"]).then_inc(S("small_landed"), 16)
            pool.dma_start(rows[:, 0, :], a["b_v"].partition_broadcast(P)).then_inc(S("small_landed"), 16)
            pool.dma_start(rows[:, 1, :], a["b_out"].partition_broadcast(P)).then_inc(S("small_landed"), 16)
            pool.dma_start(rows[:, 2, :], a["ln1_g"].partition_broadcast(P)).then_inc(S("small_landed"), 16)
            pool.dma_start(w_route[:], a["w_route"]).then_inc(S("small_landed"), 16)
            pool.dma_start(b_route[:], a["b_route"].partition_broadcast(P)).then_inc(S("small_landed"), 16)
            g.memset(ident[:], 0.0).then_inc(S("consts_begun"), 1)
            g.memset(before[:], 1.0).then_inc(S("consts_begun"), 1)
            g.memset(stack[:], 0.0).then_inc(S("consts_begun"), 1)
            g.memset(slab[:, 10, 1024:2048], 1.0).then_inc(S("consts_begun"), 1)
            g.iota(slots_i[:].rearrange("p (a b) -> p a b", a=4), pattern=[[0, 4], [1, CAP]], base=0,
                   channel_multiplier=0).then_inc(S("consts_begun"), 1)
            g.iota(numbers_i[:], pattern=[[1, NE]], base=0, channel_multiplier=0).then_inc(S("consts_begun"), 1)
            pool.wait_ge(S("consts_begun"), 6)
            for j in range(4):
                if j:
                    pool.wait_ge(S("stacked"), j)
                g.affine_select(out=stack[:], in_=stack[:], compare_op=ALU.not_equal, fill=1.0, base=-CAP * j,
                                pattern=[[-1, CAP]], channel_multiplier=1).then_inc(S("stacked"), 1)
            g.memset(slab[:, 10, 1024:2048:CHUNK], 0.0).then_inc(S("consts_ready"), 1)
            g.affine_select(out=ident[:], in_=ident[:], compare_op=ALU.not_equal, fill=1.0, base=0,
                            pattern=[[-1, P]], channel_multiplier=1).then_inc(S("consts_ready"), 1)
            g.affine_select(out=before[:], in_=before[:], compare_op=ALU.is_gt, fill=0.0, base=0,
                            pattern=[[1, P]], channel_multiplier=-1).then_inc(S("consts_ready"), 1)
            g.tensor_copy(slots[:], slots_i[:]).then_inc(S("consts_ready"), 1)
            g.tensor_copy(numbers[:], numbers_i[:]).then_inc(S("consts_ready"), 1)
            g.memset(ones[:], 1.0).then_inc(S("consts_ready"), 1)
            g.memset(eps_ln[:], 1e-5).then_inc(S("consts_ready"), 1)
            g.memset(eps_rms[:], 1e-6).then_inc(S("consts_ready"), 1)
            g.memset(meta[:], -1.0).then_inc(S("consts_ready"), 1)
            pool.wait_ge(S("consts_ready"), CONSTS)

            def weights_low(part, *names):
                for name in names:
                    for h, (w, high) in enumerate(halves(part, name)):
                        pool.wait_ge(S("high_ready"), split_count(part, name) + h + 1)
                        g.tensor_tensor(r32(w), w, r32(high), ALU.subtract).then_inc(S("low_ready"), 1)

            weights_low(0, *SPLIT[0])
            pool.wait_ge(S("x1_ready"), TT)
            pool.dma_start(rows[:, 1, :], a["ln2_g"].partition_broadcast(P)).then_inc(S("ln2_landed"), 16)
            pool.dma_start(rows[:, 2, :], a["ln2_b"].partition_broadcast(P)).then_inc(S("ln2_landed"), 16)
            pool.dma_start(slab[:, 6, 0:DC * 136], a["w_kiwi"]).then_inc(S("small2_landed"), 16)
            pool.dma_start(slab[0:NB, 9, 0:NH], a["rel_bias"]).then_inc(S("small2_landed"), 16)
            pool.dma_start(slab[0:NB, 9, 16:16 + 511], a["buckets"]).then_inc(S("small2_landed"), 16)
            weights_low(1, "lx1", "lx3")
            pool.wait_ge(S("x2_ready"), TT)
            pool.dma_start(rows[:, 2, 0:512], a["pT"]).then_inc(S("p_landed"), 16)
            weights_low(1, "lg_1", "lg_3", "vv", "qi1", "qq1", "qq3", "gc1", "gc3")
            for t in range(TT):
                pool.wait_ge(S("score_ready"), t + 1)
                g.affine_select(out=work[:, t, 0:P * (t + 1)], in_=score[:, t, 0:P * (t + 1)],
                                compare_op=ALU.is_ge, fill=FILL, base=P * t, pattern=[[-1, P * (t + 1)]],
                                channel_multiplier=1).then_inc(S("work_ready"), 1)
            weights_low(1, "gd1", "gd3")
            for t in range(TT):
                pool.wait_ge(S("hide_made"), t + 1)
                g.affine_select(out=score[:, t, 0:P * (t + 1)], in_=score[:, t, 0:P * (t + 1)],
                                compare_op=ALU.is_ge, fill=HIDE, base=P * t, pattern=[[-1, P * (t + 1)]],
                                channel_multiplier=1).then_inc(S("hide_ready"), 1)
            weights_low(1, *SPLIT[1][SPLIT[1].index("yb1"):])

        @block.tensor
        def _(pe):
            mm = nc.tensor.matmul
            units = [0, 0]

            def unit(part=0, cols_=512):
                name = UNITS[part][units[part]]
                s = units[part] % STREAM
                units[part] += 1
                w = ring[:, s, :].rearrange("p (c n) -> p c n", n=cols_)
                if name not in SPLIT[part]:
                    wait_landed(pe, part, name)
                    return w
                high = ring[:, STREAM + SPLIT[part].index(name) % 2, :].rearrange("p (c n) -> p c n", n=cols_)
                return high, w, split_count(part, name)

            def products(out_, w, x, swap, wcol, xcol, half_, start=True, stop=True):
                def one(wp, xp, first, last):
                    l, r = (xp, wp) if swap else (wp, xp)
                    return mm(out_, l, r, start=start and first, stop=stop and last)

                if not isinstance(w, tuple):
                    for c in range(DC):
                        ins = one(w[:, c, wcol], x[:, c, xcol], c == 0, c == DC - 1)
                    return ins
                high, low, count = w
                for c in range(DC):
                    if half_ is not None and c == 0:
                        pe.wait_ge(S("high_ready"), count + half_ + 1)
                    elif half_ is None and c % 4 == 0:
                        pe.wait_ge(S("high_ready"), count + c // 4 + 1)
                    one(r32(high[:, c, wcol]), r32(x[0][:, c, xcol]), c == 0, False)
                    one(r32(high[:, c, wcol]), r32(x[1][:, c, xcol]), False, False)
                for c in range(DC):
                    if half_ is not None and c == 0:
                        pe.wait_ge(S("low_ready"), count + half_ + 1)
                    elif half_ is None and c % 4 == 0:
                        pe.wait_ge(S("low_ready"), count + c // 4 + 1)
                    ins = one(r32(low[:, c, wcol]), r32(x[0][:, c, xcol]), False, c == DC - 1)
                return ins

            def chan_major(w, x, tasks):
                for i, task in enumerate(tasks):
                    o = take_bank(task)
                    for m in range(2):
                        f = P * (2 * i + m)
                        last = products(o[:, T * m:T * m + T], w, x, False, slice(f, f + P), slice(0, T), i)
                    full(last, task)

            def token_major(w, x, tasks):
                for t, task in enumerate(tasks):
                    o = take_bank(task)
                    full(products(o[:], w, x, True, slice(0, 512), slice(P * t, P * t + P), None), task)

            def turn(src, tasks, ready, done=0):
                for j, task in enumerate(tasks):
                    o = take_bank(task)
                    for m in range(2):
                        for t in range(TT):
                            if j == 0 and m == 0:
                                pe.wait_ge(S(ready), done + t + 1)
                            c = 2 * j + m
                            last = nc.tensor.transpose(o[:, T * m + P * t:T * m + P * t + P],
                                                       src[:, t, P * c:P * c + P], ident[:])
                    full(last, task)

            xT = chan(0)
            pe.wait_ge(S("xt_landed"), 16)
            chan_major(unit(), xT, ["g0", "g1"])
            chan_major(unit(), xT, ["a0", "a1"])
            xTs = xt_parts
            pe.wait_ge(S("xt_high"), 1)
            pe.wait_ge(S("xt_low"), 1)
            chan_major(unit(), xTs, ["g2", "g3"])
            chan_major(unit(), xTs, ["a2", "a3"])
            chan_major(unit(), xTs, ["k0", "k1"])
            pe.wait_ge(S("small_landed"), 16 * SMALL_LOADS)
            o = take_bank("fl")
            for c in range(DC):
                last = mm(o[0:RANK, 0:T], w_flr[:, c, :], xT[:, c, :], start=c == 0, stop=c == DC - 1)
            full(last, "fl")
            pe.wait_ge(S("small_landed"), 16 * SMALL_LOADS)
            wait_read(pe, "fl")
            for j in range(2):
                o = take_bank(f"z{j}")
                for m in range(2):
                    f = P * (2 * j + m)
                    last = mm(o[:, T * m:T * m + T], slab[0:RANK, 10, f:f + P], slab[0:RANK, 10, 512:512 + T],
                              start=True, stop=True)
                full(last, f"z{j}")
            token_major(unit(), xTs, ["v0_0", "v0_1"])
            token_major(unit(), xTs, ["v1_0", "v1_1"])
            chan_major(unit(), xTs, ["q0", "q1"])
            chan_major(unit(), xTs, ["r0", "r1"])
            chan_major(unit(), xTs, ["r2", "r3"])
            chan_major(unit(), xTs, ["ga0", "ga1"])
            chan_major(unit(), xTs, ["ga2", "ga3"])
            pe.wait_ge(S("consts_ready"), CONSTS)
            o = take_bank("csum")
            for c in range(DC):
                if c % 4 == 0:
                    pe.wait_ge(S("conv_tap"), 4 * CONV_W * (c // 4 + 1))
                last = mm(o[:, 0:T], ones[:], chan(3)[:, c, :], start=c == 0, stop=c == DC - 1)
            full(last, "csum")
            pe.wait_ge(S("consts_ready"), CONSTS)
            pe.wait_ge(S("kdec_ready"), 1)
            for t in range(TT):
                o = take_bank(f"kdt{t}")
                for h in range(H1):
                    last = nc.tensor.transpose(o[:, P * h:P * h + P], half(5, 0)[:, h, P * t:P * t + P], ident[:])
                full(last, f"kdt{t}")
            wait_read(pe, "kdt0", "kdt1", "v0_0", "v0_1", "v1_0", "v1_1")
            for n in range(NCH):
                b = CHUNK * (n % 2)
                for hp in range(2):
                    task = f"kv{2 * n + hp}"
                    o = take_bank(task)
                    for m in range(2):
                        h = 2 * hp + m
                        last = mm(o[:, HV * m:HV * m + HV],
                                  slab[b:b + CHUNK, 5, 1024 + 512 * (n // 2) + P * h:1024 + 512 * (n // 2) + P * h + P],
                                  tok(6)[b:b + CHUNK, n // 2, HV * h:HV * h + HV], start=True, stop=True)
                    full(last, task)
            chan_major(unit(), xTs, ["gb0", "gb1"])
            o = take_bank("csq")
            pe.wait_ge(S("csq_ready"), 1)
            for c in range(DC):
                last = mm(o[:, 0:T], ones[:], chan(2)[:, c, :], start=c == 0, stop=c == DC - 1)
            full(last, "csq")
            wait_read(pe, "q0", "q1")
            wait_read(pe, *[f"kv{i}" for i in range(8)])
            for h in range(H1):
                o = take_bank(f"o{h}")
                for m in range(2):
                    for n in range(NCH):
                        st = states(n, h)[:, P * m:P * m + P]
                        last = mm(o[:, T * m + CHUNK * n:T * m + CHUNK * n + CHUNK], st,
                                  half(7, 0)[:, h, CHUNK * n:CHUNK * n + CHUNK], start=True, stop=True)
                full(last, f"o{h}")
            chan_major(unit(), xTs, ["gb2", "gb3"])
            for j in range(2):
                pe.wait_ge(S("osq_ready"), 2 * j + 2)
                o = take_bank(f"osum{j}")
                for m in range(2):
                    h = 2 * j + m
                    for k in range(2):
                        last = mm(o[:, T * m:T * m + T], ones[:], chan(5)[:, 2 * h + k, :], start=k == 0, stop=k == 1)
                full(last, f"osum{j}")
            pe.wait_ge(S("conv_low"), 1)
            chan_major(unit(), conv_parts, ["yc0", "yc1"])
            chan_major(unit(), conv_parts, ["yc2", "yc3"])
            pe.wait_ge(S("gla_low"), 1)
            chan_major(unit(), gla_parts, ["yg0", "yg1"])
            chan_major(unit(), gla_parts, ["yg2", "yg3"])
            pe.wait_ge(S("merged_low"), 4)
            token_major(unit(), merged_parts, ["mix0_0", "mix0_1"])
            token_major(unit(), merged_parts, ["mix1_0", "mix1_1"])
            turn(tok(0), [f"x1t{j}" for j in range(4)], "x1_ready")
            wait_read(pe, *[f"x1t{j}" for j in range(4)])
            pe.wait_ge(S("small_landed"), 16 * SMALL_LOADS)
            o = take_bank("lg")
            for t in range(TT):
                for c in range(DC):
                    last = mm(o[:, 128 * t:128 * t + 72], chan(1)[:, c, P * t:P * t + P], w_route[:, c, :],
                              start=c == 0, stop=c == DC - 1)
            full(last, "lg")
            pe.wait_ge(S("zeros_ready"), 1)
            wait_read(pe, *TASKS1[-8:-2])
            for t in range(TT):
                for hf in range(2):
                    mm(acc[t][hf][:], zeros[:, 0:P], zeros[:], start=True, stop=False)
            pe.wait_ge(S("mask_ready"), 1)
            pe.wait_ge(S("consts_ready"), CONSTS)
            o = take_bank("pos")
            mm(o[:, 0:64], before[:], mask[:, 0, :], start=True, stop=True)
            mm(o[:, 64:128], before[:], mask[:, 1, :], start=True, stop=False)
            mm(o[:, 64:128], ones[:], mask[:, 0, :], start=False, stop=True)
            mm(o[:, 128:192], ones[:], mask[:, 0, :], start=True, stop=False)
            full(mm(o[:, 128:192], ones[:], mask[:, 1, :], start=False, stop=True), "pos")
            wait_read(pe, "pos", "lg")
            pe.wait_ge(S("x1_ready"), TT)

            def gather(f, par, r):
                pe.wait_ge(S("sel_ready"), (r * META + f + 1) * TT)
                for c in range(DC):
                    for t in range(TT):
                        last = mm(gather_bank[:, CAP * c:CAP * c + CAP], tok(0)[:, t, c::DC], sel[:, par, t, :],
                                  start=t == 0, stop=t == 1)
                last.then_inc(S("xg_full"), 1)

            def combine(par, ends=False, again=False):
                for t in range(TT):
                    for hf in range(2):
                        last = mm(acc[t][hf][:], spread[:, par, P * t:P * t + P],
                                  y_sb[:, par, 512 * hf:512 * hf + 512], start=False, stop=ends,
                                  skip_group_check=again)
                last.then_inc(S("combined"), 1)

            def expert(e, q, it, r):
                n = r * NE + e
                for w, (b, name) in enumerate(((gate_bank, "gate_full"), (up_bank, "up_full"))):
                    pe.wait_ge(S(f"expert_landed{3 * q + w}"), 16 * (r * (NE // 2) + it + 1))
                    if w == 0:
                        pe.wait_ge(S("xg_copied"), r * (NE + 1) + e + 1)
                    else:
                        pe.wait_ge(S("y1_copied"), r * (NE + 1) + e + 1)
                    wt = ring[:, expert_slot(q, w), :].rearrange("p (c n) -> p c n", c=DC)
                    for c in range(DC):
                        j = c % 4
                        last = mm(b[CAP * j:CAP * j + CAP, :], xg[:, c, :], wt[:, c, :],
                                  start=c < 4, stop=c >= 4, tile_position=(0, CAP * j))
                    last.then_inc(S(name), 1)
                gather(e + 1, 1 - q, r)
                pe.wait_ge(S("selw_ready"), (r * META + e + 1) * TT)
                pe.wait_ge(S("y0_copied"), r * (NE + 1) + e + 1)
                for t in range(TT):
                    last = nc.tensor.transpose(y_bank[:, P * t:P * t + P], selw[:, q, t, :], ident[:])
                last.then_inc(S("spread_full"), 1)
                pe.wait_ge(S("g_copied"), n + 1)
                pe.wait_ge(S("u_copied"), n + 1)
                for src, o in ((g_sb, 0), (u_sb, 128)):
                    for m in range(4):
                        last = mm(gate_bank[:, o + CAP * m:o + CAP * m + CAP], src[:, m::4], stack[:],
                                  start=True, stop=True)
                last.then_inc(S("hidden_full"), 1)
                pe.wait_ge(S("spread_copied"), r * (NE + 1) + e + 1)
                combine(1 - q, again=not isinstance(r, int))
                pe.wait_ge(S("h_ready"), n + 1)
                pe.wait_ge(S(f"expert_landed{3 * q + 2}"), 16 * (r * (NE // 2) + it + 1))
                wt = ring[:, expert_slot(q, 2), :].rearrange("p (c n) -> p c n", c=4)
                pe.wait_ge(S("spread_copied"), r * (NE + 1) + e + 2)
                for hf, (b, name) in enumerate(((y_bank, "y0_full"), (up_bank, "y1_full"))):
                    for m in range(4):
                        last = mm(b[CAP * m:CAP * m + CAP, :], h_sb[:, m, :],
                                  wt[:, m, 512 * hf:512 * hf + 512], start=True, stop=True,
                                  tile_position=(0, CAP * m))
                    last.then_inc(S(name), 1)

            def last_combine(r):
                pe.wait_ge(S("y0_copied"), (r + 1) * (NE + 1))
                pe.wait_ge(S("y1_copied"), (r + 1) * (NE + 1))
                pe.wait_ge(S("spread_copied"), (r + 1) * (NE + 1))
                combine(1, ends=True, again=not isinstance(r, int))

            pe.wait_ge(S("consts_ready"), CONSTS)
            gather(0, 0, 0)
            with pe.Fori(0, NE // 2) as it:
                for q in range(2):
                    expert(2 * it + q, q, it, 0)
            last_combine(0)
            more = pe.value_load(over[0:1, 0:1], min_val=0, max_val=1)
            with pe.If(more > 0):
                with pe.Fori(1, ROUNDS) as r:
                    pe.wait_ge(S("xg_copied"), r * (NE + 1))
                    gather(0, 0, r)
                    with pe.Fori(0, NE // 2) as it:
                        for q in range(2):
                            expert(2 * it + q, q, it, r)
                    last_combine(r)
            turn(tok(1), [f"x2t{j}" for j in range(4)], "xn_ready")
            wait_read(pe, *[f"x2t{j}" for j in range(4)])
            xn = xn_parts
            pe.wait_ge(S("small2_landed"), 48)
            kiwi = slab[:, 6, 0:DC * 136].rearrange("p (c n) -> p c n", c=DC)
            o = take_bank("kiwi_k")
            for c in range(DC):
                for i, x in enumerate(xn):
                    last = mm(o[:, 0:T], kiwi[:, c, 0:P], r32(x[:, c, :]).bitcast(F32), start=c + i == 0, stop=c + i == DC)
            full(last, "kiwi_k")
            o = take_bank("kiwi_w")
            for t in range(TT):
                for c in range(DC):
                    for i, x in enumerate(xn):
                        last = mm(o[:, 8 * t:8 * t + 8], r32(x[:, c, P * t:P * t + P]).bitcast(F32), kiwi[:, c, P:P + 8],
                                  start=c + i == 0, stop=c + i == DC)
            full(last, "kiwi_w")
            o = take_bank("relb")
            full(mm(o[0:NH, 0:511], slab[0:NB, 9, 0:NH], slab[0:NB, 9, 16:16 + 511], start=True, stop=True), "relb")
            chan_major(unit(1), xn, ["lx0", "lx1"])
            chan_major(unit(1), xn, ["lx2", "lx3"])
            chan_major(unit(1), xn, ["lg_0", "lg_1"])
            chan_major(unit(1), xn, ["lg_2", "lg_3"])
            w = unit(1)
            chan_major(w, xn, ["kk"])
            o = take_bank("vv")
            for t in range(TT):
                last = products(o[:, T * t:T * t + T], w, xn, True, slice(256, 512), slice(P * t, P * t + P), 1)
            full(last, "vv")
            chan_major(unit(1), xn, ["qi0", "qi1"])
            w = unit(1, 128)
            for x, pre in ((0, "lr"), (1, "li")):
                for j in range(4):
                    o = take_bank(f"{pre}{j}")
                    for m in range(2):
                        c = 2 * j + m
                        if x == 0:
                            pe.wait_ge(S("lru_tap"), 2 * LRU_W * (j + 1))
                        last = mm(o[:, T * m:T * m + T], w[:, 8 * x + c, :], chan(2)[:, c, :], start=True, stop=True)
                    full(last, f"{pre}{j}")
            o = take_bank("ksum")
            pe.wait_ge(S("k_sq_ready"), 1)
            full(mm(o[:, 0:512], ones[:], k_sq, start=True, stop=True), "ksum")
            chan_major(unit(1), xn, ["qq0", "qq1"])
            chan_major(unit(1), xn, ["qq2", "qq3"])
            chan_major(unit(1), xn, ["gc0", "gc1"])
            chan_major(unit(1), xn, ["gc2", "gc3"])
            wait_read(pe, "kiwi_k", "qi0", "qi1")
            for t in range(TT):
                n = P * (t + 1)
                for j in range(4):
                    o = take_bank(f"dots{t}_{j}")
                    for m in range(2):
                        h = indexer_head(j, m)
                        b = ID * (h % 2)
                        last = mm(o[:, T * m:T * m + n], qiT[b:b + ID, h // 2, P * t:P * t + P], kiT[b:b + ID, 0:n],
                                  start=True, stop=True)
                    full(last, f"dots{t}_{j}")
            for j in range(4):
                o = take_bank(f"qsum{j}")
                pe.wait_ge(S("q_sq_ready"), j + 1)
                full(mm(o[:, 0:512], ones[:], slab[:, 6, 512 * j:512 * j + 512], start=True, stop=True), f"qsum{j}")
            pe.wait_ge(S("ya_ready"), 1)
            chan_major(unit(1), chan(1), ["ya0", "ya1"])
            chan_major(unit(1), chan(1), ["ya2", "ya3"])
            chan_major(unit(1), xn, ["gd0", "gd1"])
            chan_major(unit(1), xn, ["gd2", "gd3"])
            pe.wait_ge(S("k_ready"), 1)
            pe.wait_ge(S("q_ready"), 4)
            for t in range(TT):
                n = P * (t + 1)
                for j in range(4):
                    o = take_bank(f"log{t}_{j}")
                    for m in range(2):
                        h = 2 * j + m
                        last = mm(o[:, T * m:T * m + n], chan(9)[:, h, P * t:P * t + P], kT[:, h // QPK, 0:n],
                                  start=True, stop=True)
                    full(last, f"log{t}_{j}")
            for t in range(TT):
                pe.wait_ge(S("probs_ready"), t + 1)
                for s in range(t + 1):
                    for k in range(2):
                        o = take_bank(f"pt{t}_{s}_{k}")
                        for m in range(4):
                            last = nc.tensor.transpose(o[:, P * m:P * m + P], lgt[:, 4 * k + m, P * s:P * s + P],
                                                       ident[:])
                        full(last, f"pt{t}_{s}_{k}")
                wait_read(pe, *[f"pt{t}_{s}_{k}" for s in range(t + 1) for k in range(2)])
                for k in range(2):
                    o = take_bank(f"pv{t}_{k}")
                    for s in range(t + 1):
                        last = mm(o[:, 0:512], v2[:, s, HD * k:HD * k + HD],
                                  prob_t[:, s, 4 * k:4 * k + 4, :].rearrange("p h t -> p (h t)"),
                                  start=s == 0, stop=s == t)
                    full(last, f"pv{t}_{k}")
            wait_read(pe, "pv0_0", "pv0_1", "pv1_0", "pv1_1")
            pe.wait_ge(S("att_low"), 1)
            chan_major(unit(1), att_parts, ["yb0", "yb1"])
            chan_major(unit(1), att_parts, ["yb2", "yb3"])
            pe.wait_ge(S("merged2_low"), 4)
            token_major(unit(1), merged2_parts, ["mo0_0", "mo0_1"])
            token_major(unit(1), merged2_parts, ["mo1_0", "mo1_1"])
            turn(tok(4), [f"x3t{j}" for j in range(4)], "xn_ready", TT)
            wait_read(pe, *[f"x3t{j}" for j in range(4)])
            for i in range(6):
                chan_major(unit(1), xn, [f"fg{i}_0", f"fg{i}_1"])
                chan_major(unit(1), xn, [f"fu{i}_0", f"fu{i}_1"])
            for u in range(2):
                o = [take_bank(f"dn{u}_{t}") for t in range(TT)]
                for k in range(3):
                    if u == 0:
                        pe.wait_ge(S("hid_low"), 2 * k + 2)
                    w = unit(1)
                    x = [part[:, DC * k:DC * k + DC, :] for part in hid_parts]
                    for t in range(TT):
                        last = products(o[t][:], w, x, True, slice(0, 512), slice(P * t, P * t + P), None,
                                        start=k == 0, stop=k == 2)
                        if k == 2:
                            full(last, f"dn{u}_{t}")
                    if k < 2:
                        last.then_inc(S("down_used"), 1)
            turn(tok(4), [f"x4t{j}" for j in range(4)], "xn_ready", 2 * TT)
            pe.wait_ge(S("p_landed"), 16)
            w = unit(1, 1024)
            pT = rows[:, 2, 0:512].rearrange("p (c t) -> p c t", c=2)
            for u in range(2):
                for t in range(TT):
                    o = take_bank(f"pp{u}_{t}")
                    for c in range(2):
                        last = mm(o[:], pT[:, c, P * t:P * t + P], w[:, c, 512 * u:512 * u + 512],
                                  start=c == 0, stop=c == 1)
                    full(last, f"pp{u}_{t}")
            wait_read(pe, *[f"x4t{j}" for j in range(4)])
            token_major(unit(1), xn, ["pg0_0", "pg0_1"])
            token_major(unit(1), xn, ["pg1_0", "pg1_1"])

        @block.scalar
        def _(act):
            A = nc.scalar.activation

            def per_chunk(tasks, dst, func, bias=None, scale=1.0, first=0):
                for i, task in enumerate(tasks):
                    o = wait_full(act, task)
                    for m in range(2):
                        c = first + 2 * i + m
                        b = col(bias, c) if bias else 0.0
                        ins = A(dst[:, c, :], o[:, T * m:T * m + T], func, bias=b, scale=scale)
                    read(ins, task)

            def weights_high(part, *names):
                for name in names:
                    k = SPLIT[part].index(name)
                    wait_landed(act, part, name)
                    if k >= 2:
                        wait_used(act, SPLIT[part][k - 2])
                    for w, high in halves(part, name):
                        A(r32(high), w, ACT.Copy).then_inc(S("high_ready"), 1)

            act.wait_ge(S("xt_landed"), 16)
            A(r32(slab[:, 8, :]), slab[:, 0, :], ACT.Copy).then_inc(S("xt_high"), 1)
            weights_high(0, "g3")
            act.wait_ge(S("cols_landed"), 16)
            per_chunk(["g0", "g1"], chan(1), ACT.Sigmoid, "b_conv_g")
            weights_high(0, "a3")
            per_chunk(["g2", "g3"], chan(1), ACT.Sigmoid, "b_conv_g", first=4)
            weights_high(0, "k1", "v0_1")
            per_chunk(["k0", "k1"], half(4, 0), ACT.Identity, "b_k")
            o = wait_full(act, "fl")
            read(A(slab[0:RANK, 10, 512:512 + T], o[0:RANK, 0:T], ACT.Identity,
                   bias=cols[0:RANK, COLS["b_flr"]:COLS["b_flr"] + 1]), "fl")
            weights_high(0, "v1_1")
            per_chunk(["z0", "z1"], half(5, 0), ACT.Identity, "b_gate")
            la = half(7, 1)
            act.wait_ge(S("negabs_ready"), 1)
            A(la, la, ACT.Exp).then_inc(S("gate_exp"), 1)
            act.wait_ge(S("gate_exp"), 1)
            A(la, la, ACT.Ln, bias=1.0).then_inc(S("gate_ln"), 1)
            weights_high(0, "q1", "r1")
            act.wait_ge(S("toend_ready"), 1)
            A(la, la, ACT.Exp, scale=1.0 / TAU).then_inc(S("decay_ready"), 1)
            A(small[:, 0:16].rearrange("p (h n a) -> p h n a", h=H1, a=1), half(4, 1).rearrange("p h (n t) -> p h n t", t=CHUNK)[:, :, :, CHUNK - 1:CHUNK],
              ACT.Exp, scale=1.0 / TAU).then_inc(S("decay_ready"), 1)
            per_chunk(["q0", "q1"], half(7, 0), ACT.Identity, "b_q")
            weights_high(0, "r3")
            wait_full(act, "fl")
            per_chunk(["r0", "r1"], chan(0), ACT.Silu, "b_r")
            weights_high(0, "ga1")
            per_chunk(["r2", "r3"], chan(0), ACT.Silu, "b_r", first=4)
            weights_high(0, "ga3")
            wait_read(act, "a0", "a1", "a2", "a3")
            per_chunk(["ga0", "ga1"], chan(1), ACT.Sigmoid, "b_ga")
            weights_high(0, "gb1")
            per_chunk(["ga2", "ga3"], chan(1), ACT.Sigmoid, "b_ga", first=4)
            weights_high(0, "gb3")
            act.wait_ge(S("centered"), DC)
            A(chan(2), chan(3), ACT.Square).then_inc(S("csq_ready"), 1)
            wait_full(act, "kv7")
            per_chunk(["gb0", "gb1"], chan(6), ACT.Sigmoid, "b_gb")
            act.wait_ge(S("consts_ready"), CONSTS)
            o = wait_full(act, "csq")
            read(A(conv_root, o[:, 0:T], ACT.Sqrt, bias=eps_ln[:], scale=1.0 / D), "csq")
            weights_high(0, "yc1")
            act.wait_ge(S("conv_normed"), DC)
            for h in range(H1):
                if h == 2:
                    wait_full(act, "o3")
                o = wait_full(act, f"o{h}")
                dst = chan(10)[:, 2 * h:2 * h + 2, :].rearrange("p a t -> p (a t)")
                read(A(dst, o[:, 0:512], ACT.Copy, scale=HK ** -0.5), f"o{h}")
                wait_read(act, f"o{h}")
                A(chan(5)[:, 2 * h:2 * h + 2, :].rearrange("p a t -> p (a t)"), dst, ACT.Square
                  ).then_inc(S("osq_ready"), 1)
            for c in range(DC):
                act.wait_ge(S("conv_normed"), c + 1)
                ins = A(chan(3)[:, c, :], chan(3)[:, c, :], ACT.Silu, bias=col("cln_b", c), scale=col("cln_g", c))
            ins.then_inc(S("conv_act_ready"), 1)
            act.wait_ge(S("conv_act_ready"), 1)
            A(r32(slab[:, 4, :]), slab[:, 3, :], ACT.Copy).then_inc(S("conv_high"), 1)
            per_chunk(["gb2", "gb3"], chan(6), ACT.Sigmoid, "b_gb", first=4)
            weights_high(0, "yc3")
            for j in range(2):
                o = wait_full(act, f"osum{j}")
                read(A(slab[:, 7, 1024 + 512 * j:1024 + 512 * j + 512], o[:, 0:512], ACT.Sqrt,
                       bias=eps_rms[:], scale=1.0 / HV), f"osum{j}")
            act.wait_ge(S("gla_ready"), 1)
            A(r32(slab[:, 5, :]), slab[:, 10, :], ACT.Copy).then_inc(S("gla_high"), 1)
            weights_high(0, "yg1", "yg3", "mix0_1")
            wait_full(act, "gb3")
            for j in range(4):
                act.wait_ge(S("merged_ready"), j + 1)
                A(r32(slab[:, 8, 512 * j:512 * j + 512]), slab[:, 1, 512 * j:512 * j + 512], ACT.Copy
                  ).then_inc(S("merged_high"), 1)
                if j == 0:
                    weights_high(0, "mix1_1")
            for t in range(TT):
                act.wait_ge(S("ln_stats"), t + 1)
                A(small[:, 20 + t:21 + t], small[:, 17 + 2 * t:18 + 2 * t], ACT.Sqrt, bias=eps_ln[:]
                  ).then_inc(S("ln_std"), 1)
            for j in range(4):
                o = wait_full(act, f"x1t{j}")
                read(A(slab[:, 1, 512 * j:512 * j + 512], o[:, 0:512], ACT.Copy), f"x1t{j}")
            act.wait_ge(S("gtop_ready"), TT)
            for t in range(TT):
                A(e_exp[:, t, :], logit[:, t, 0:NG], ACT.Exp, bias=small[:, 30 + t:31 + t],
                  accum_out=small[:, 32 + t:33 + t]).then_inc(S("gsum_ready"), 1)
            act.wait_ge(S("ediff_ready"), 1)
            A(small[:, 36:38], small[:, 34:36], ACT.Exp).then_inc(S("ratio_ready"), 1)

            def take_xg(n):
                act.wait_ge(S("xg_full"), n)
                A(slab[:, 1, 0:DC * CAP], gather_bank[:, 0:DC * CAP], ACT.Copy).then_inc(S("xg_copied"), 1)

            def expert(e, q, r):
                n = r * NE + e
                act.wait_ge(S("gate_full"), n + 1)
                A(g_sb, gate_bank[:], ACT.Copy).then_inc(S("g_copied"), 1)
                take_xg(r * (NE + 1) + e + 2)
                act.wait_ge(S("hidden_full"), n + 1)
                A(slab[:, 1, 1536:1664], gate_bank[:, 0:128], ACT.Silu).then_inc(S("silu_ready"), 1)
                act.wait_ge(S("y0_full"), n + 1)
                A(y_sb[:, q, 0:512], y_bank[:], ACT.Copy).then_inc(S("y0_copied"), 1)

            wait_read(act, "lg")
            wait_read(act, "pos")
            act.wait_ge(S("meta_ready"), 1)
            act.wait_ge(S("zeros_ready"), 1)
            A(y_sb[:, 1, 0:512], zeros, ACT.Copy).then_inc(S("y0_copied"), 1)
            take_xg(1)
            with act.Fori(0, NE // 2) as it:
                for q in range(2):
                    expert(2 * it + q, q, 0)
            more = act.value_load(over[0:1, 0:1], min_val=0, max_val=1)
            with act.If(more > 0):
                with act.Fori(1, ROUNDS) as r:
                    act.wait_ge(S("combined"), r * (NE + 1))
                    A(y_sb[:, 1, 0:512], zeros, ACT.Copy).then_inc(S("y0_copied"), 1)
                    take_xg(r * (NE + 1) + 1)
                    with act.Fori(0, NE // 2) as it:
                        for q in range(2):
                            expert(2 * it + q, q, r)
                act.wait_ge(S("y1_full"), ROUNDS * NE)
            act.wait_ge(S("up_full"), NE)
            act.wait_ge(S("y1_full"), NE)
            weights_high(1, "lx1")
            for t in range(TT):
                act.wait_ge(S("ln_stats"), TT + t + 1)
                A(small[:, 46 + t:47 + t], small[:, 43 + 2 * t:44 + 2 * t], ACT.Sqrt, bias=eps_ln[:]
                  ).then_inc(S("ln_std"), 1)

            def rms_tile(t, dst, done, at):
                A(tok(dst)[:, t, :], tok(10)[:, t, :], ACT.Square, accum_out=small[:, at + t:at + t + 1]
                  ).then_inc(S("rms_sum"), 1)
                act.wait_ge(S("rms_sum"), done + t + 1)
                A(small[:, at + 2 + t:at + 3 + t], small[:, at + t:at + t + 1], ACT.Sqrt, bias=eps_rms[:],
                  scale=1.0 / D).then_inc(S("rms_root"), 1)

            for t in range(TT):
                act.wait_ge(S("x2_ready"), t + 1)
                rms_tile(t, 1, 0, 50)

            def take_turned(tasks, gain):
                for i, task in enumerate(tasks):
                    o = wait_full(act, task)
                    for m in range(2):
                        c = 2 * i + m
                        ins = A(r32(chan(0)[:, c, :]), o[:, T * m:T * m + T], ACT.Copy, scale=col(gain, c))
                    ins.then_inc(S("xn_high"), 1)

            take_turned([f"x2t{j}" for j in range(4)], "mix_norm")
            weights_high(1, "lx3")
            o = wait_full(act, "kiwi_k")
            read(A(kiT, o[:, 0:T], ACT.Copy), "kiwi_k")
            o = wait_full(act, "kiwi_w")
            read(A(slab[:, 8, 1792:1808], o[:, 0:16], ACT.Copy, scale=IH ** -0.5), "kiwi_w")
            o = wait_full(act, "relb")
            read(A(slab[0:NH, 9, 1024:1024 + 511], o[0:NH, 0:511], ACT.Copy), "relb")
            wait_read(act, "relb")
            act.dma_start(bias_dram[:, 0:511], slab[0:NH, 9, 1024:1024 + 511]).then_inc(S("relb_stored"), 16)

            def load_bias(t):
                src = bass.AP(bias_dram.tensor, bias_dram.offset + P * t, [[1, P], [512, NH], [1, T]])
                act.dma_start(slab[:, 2, :].rearrange("p (h j) -> p h j", h=NH), src
                              ).then_inc(S("bias_landed"), 16)

            per_chunk(["lx0", "lx1"], chan(1), ACT.Copy)
            weights_high(1, "lg_1")
            per_chunk(["lx2", "lx3"], chan(1), ACT.Copy, first=4)
            weights_high(1, "lg_3")
            per_chunk(["lg_0", "lg_1"], chan(3), ACT.Gelu_apprx_tanh)
            weights_high(1, "vv")
            per_chunk(["lg_2", "lg_3"], chan(3), ACT.Gelu_apprx_tanh, first=4)
            weights_high(1, "qi1")
            o = wait_full(act, "kk")
            read(A(slab[:, 7, 0:512], o[:, 0:512], ACT.Copy), "kk")
            wait_read(act, "kk")
            A(k_sq, slab[:, 7, 0:512], ACT.Square).then_inc(S("k_sq_ready"), 1)
            o = wait_full(act, "vv")
            read(A(slab[:, 7, 512:1024], o[:, 0:512], ACT.Copy), "vv")
            weights_high(1, "qq1")
            for j in range(2):
                o = wait_full(act, f"qi{j}")
                read(A(slab[:, 7, 1024 + 512 * j:1536 + 512 * j], o[:, 0:512], ACT.Copy), f"qi{j}")
            weights_high(1, "qq3")
            act.wait_ge(S("lam_negabs"), 1)
            A(small[:, 80:88], small[:, 72:80], ACT.Exp).then_inc(S("lam_exp"), 1)
            per_chunk([f"lr{j}" for j in range(4)], chan(4), ACT.Sigmoid, "lru_ba")
            per_chunk([f"li{j}" for j in range(4)], chan(5), ACT.Sigmoid, "lru_bx")
            wait_read(act, "lr0", "lr1", "lr2", "lr3")
            act.wait_ge(S("rate_ready"), 1)
            wait_read(act, "kiwi_w", "kiwi_k")
            for c in range(DC):
                ins = A(chan(6)[:, c, :], chan(4)[:, c, :], ACT.Tanh, scale=small[:, 112 + c:113 + c])
            ins.then_inc(S("tanh_ready"), 1)
            for c in range(DC):
                ins = A(chan(4)[:, c, :], chan(4)[:, c, :], ACT.Exp, scale=small[:, 112 + c:113 + c])
            ins.then_inc(S("a_ready"), 1)
            act.wait_ge(S("relb_stored"), 16)
            for j in range(4):
                o = wait_full(act, f"qq{j}")
                read(A(slab[:, 9, 512 * j:512 * j + 512], o[:, 0:512], ACT.Copy), f"qq{j}")
                if j % 2:
                    weights_high(1, ("gc1", "gc3")[j // 2])
            act.wait_ge(S("ua_used"), 1)
            load_bias(0)
            act.wait_ge(S("mult2_ready"), 1)
            A(slab[:, 6, :], slab[:, 6, :], ACT.Sqrt, scale=-1.0).then_inc(S("mult_ready"), 1)
            o = wait_full(act, "ksum")
            read(A(k_sq, o[:, 0:512], ACT.Sqrt, bias=eps_rms[:], scale=1.0 / HD), "ksum")
            act.wait_ge(S("ya_ready"), 1)
            per_chunk([f"gc{j}" for j in range(4)], chan(3), ACT.Sigmoid)
            weights_high(1, "gd1", "gd3")
            for t in range(TT):
                n = P * (t + 1)
                for j in range(4):
                    o = wait_full(act, f"dots{t}_{j}")
                    read(A(slab[:, 4 + t, 512 * j:512 * j + 512].rearrange("p (m s) -> p m s", m=2)[:, :, 0:n],
                           o[:].rearrange("p (m s) -> p m s", m=2)[:, :, 0:n], ACT.Relu, scale=ID ** -0.5),
                         f"dots{t}_{j}")
            for j in range(4):
                wait_read(act, f"qq{j}")
                A(slab[:, 6, 512 * j:512 * j + 512], slab[:, 9, 512 * j:512 * j + 512], ACT.Square
                  ).then_inc(S("q_sq_ready"), 1)
            for j in range(4):
                o = wait_full(act, f"qsum{j}")
                read(A(slab[:, 6, 512 * j:512 * j + 512], o[:, 0:512], ACT.Sqrt, bias=eps_rms[:], scale=1.0 / HD),
                     f"qsum{j}")
            wait_full(act, "ya3")
            per_chunk([f"gd{j}" for j in range(4)], chan(1), ACT.Sigmoid)
            weights_high(1, "yb1", "yb3")
            for t in range(TT):
                n = P * (t + 1)
                act.wait_ge(S("rowmax_ready"), t + 1)
                if t == 0:
                    load_bias(1)
                for h in range(NH):
                    ins = A(lgt[:, h, 0:n], lgt[:, h, 0:n], ACT.Exp, bias=small[:, 128 + h:129 + h],
                            accum_out=small[:, 136 + h:137 + h])
                ins.then_inc(S("exp_ready"), 1)
                for s in range(t + 1):
                    for k in range(2):
                        o = wait_full(act, f"pt{t}_{s}_{k}")
                        read(A(prob_t[:, s, 4 * k:4 * k + 4, :].rearrange("p h t -> p (h t)"), o[:, 0:512],
                               ACT.Copy), f"pt{t}_{s}_{k}")
                for k in range(2):
                    o = wait_full(act, f"pv{t}_{k}")
                    read(A(chan(6)[:, 4 * k:4 * k + 4, P * t:P * t + P],
                           o[:].rearrange("p (h t) -> p h t", h=4), ACT.Copy), f"pv{t}_{k}")
            wait_read(act, "pv0_0", "pv0_1", "pv1_0", "pv1_1")
            A(r32(slab[:, 9, :]), slab[:, 6, :], ACT.Copy).then_inc(S("att_high"), 1)
            wait_full(act, "yb1")
            weights_high(1, "mo0_1")
            for j in range(4):
                act.wait_ge(S("merged2_ready"), j + 1)
                A(r32(slab[:, 7, 512 * j:512 * j + 512]), slab[:, 3, 512 * j:512 * j + 512], ACT.Copy
                  ).then_inc(S("merged2_high"), 1)
                if j == 0:
                    weights_high(1, "mo1_1")
            weights_high(1, "fg0_1")
            for t in range(TT):
                wait_read(act, f"mo0_{t}", f"mo1_{t}")
                rms_tile(t, 4, TT, 54)
            take_turned([f"x3t{j}" for j in range(4)], "ffn_norm")
            weights_high(1, "fu0_1")
            down = ["dn0_1/1", "dn0_1/2", "dn0_1", "dn1_1/1", "dn1_1/2", "dn1_1"]
            for i in range(6):
                for j in range(2):
                    o = wait_full(act, f"fg{i}_{j}")
                    if i >= 2:
                        act.wait_ge(S("ffn_tap"), 4 * FFN_W * (i - 1))
                    read(A(half(4, i % 2)[:, 2 * j:2 * j + 2, :].rearrange("p a t -> p (a t)"), o[:, 0:512],
                           ACT.Copy), f"fg{i}_{j}")
                weights_high(1, f"fg{i + 1}_1" if i < 5 else down[0])
                act.wait_ge(S("ffn_tap"), 4 * FFN_W * (i + 1))
                A(half(5, i % 2), half(5, i % 2), ACT.Gelu_apprx_tanh).then_inc(S("fgelu_ready"), 1)
                weights_high(1, f"fu{i + 1}_1" if i < 5 else down[1])
                wait_read(act, f"fu{i}_0", f"fu{i}_1")
                A(r32(hT[:, 4 * i:4 * i + 4, :]), half(5, i % 2), ACT.Copy).then_inc(S("hid_high"), 1)
            weights_high(1, *down[2:])
            weights_high(1, "pg0_1", "pg1_1")
            for t in range(TT):
                wait_read(act, f"dn0_{t}", f"dn1_{t}")
                rms_tile(t, 4, 2 * TT, 62)
            take_turned([f"x4t{j}" for j in range(4)], "ple_norm")
            for u in range(2):
                for t in range(TT):
                    o = wait_full(act, f"pg{u}_{t}")
                    read(A(tok(4)[:, t, 512 * u:512 * u + 512], o[:], ACT.Sigmoid), f"pg{u}_{t}")

        @block.vector
        def _(dve):
            v = nc.vector
            stt, ts, tt = v.scalar_tensor_tensor, v.tensor_scalar, v.tensor_tensor

            def glu_input(js):
                for j in js:
                    wait_read(dve, f"g{j}")
                    o = wait_full(dve, f"a{j}")
                    for m in range(2):
                        c = 2 * j + m
                        ins = stt(chan(2)[:, c, :], o[:, T * m:T * m + T], col("b_conv_a", c), chan(1)[:, c, :],
                                  ALU.add, ALU.mult)
                    read(ins, f"a{j}")
                wait_read(dve, *[f"a{j}" for j in js])

            def causal_conv(src, dst, w, width, bias, chunks, done, base, between=None):
                n = 0
                for j in reversed(range(width)):
                    lag = width - 1 - j
                    for i, (cs, cd, cw) in enumerate(chunks):
                        wc = col(w, width * cw + j)
                        if lag == 0:
                            ins = ts(dst[:, cd, :], src[:, cs, :], wc, col(bias, cw), ALU.mult, ALU.add)
                        else:
                            dve.wait_ge(S(done), base + n - len(chunks) + 1)
                            ins = stt(dst[:, cd, lag:T], src[:, cs, 0:T - lag], wc, dst[:, cd, lag:T],
                                      ALU.mult, ALU.add)
                        n += 1
                        ins.then_inc(S(done), 1)
                    if between and lag in between:
                        between[lag]()
                dve.wait_ge(S(done), base + n)
                return base + n

            def low_part(full_, high, low):
                return tt(r32(low), full_, r32(high), ALU.subtract)

            dve.wait_ge(S("xt_high"), 1)
            low_part(slab[:, 0, :], slab[:, 8, :], slab[:, 9, :]).then_inc(S("xt_low"), 1)

            def take_v(u):
                dve.wait_ge(S("small_landed"), 16 * SMALL_LOADS)
                for t in range(TT):
                    o = wait_full(dve, f"v{u}_{t}")
                    read(tt(tok(6)[:, t, 512 * u:512 * u + 512], o[:], rows[:, 0, 512 * u:512 * u + 512], ALU.add),
                         f"v{u}_{t}")

            dve.wait_ge(S("cols_landed"), 16)
            glu_input([0, 1])
            n = causal_conv(chan(2), chan(3), "conv_w", CONV_W, "conv_b", [(c, c, c) for c in range(4)],
                            "conv_tap", 0)
            wait_read(dve, "z0", "z1")
            z, la = half(5, 0), half(7, 1)
            stt(la, z, -1.0, z, ALU.mult, ALU.min).then_inc(S("negabs_ready"), 1)
            glu_input([2, 3])
            dve.wait_ge(S("gate_ln"), 1)
            stt(z, z, 0.0, la, ALU.min, ALU.subtract).then_inc(S("loga_ready"), 1)
            dve.wait_ge(S("loga_ready"), 1)
            dve.wait_ge(S("consts_ready"), CONSTS)
            v.tensor_tensor_scan(slab[:, 4, 1024:2048], slab[:, 10, 1024:2048], slab[:, 5, 0:1024], 0.0,
                                 ALU.mult, ALU.add).then_inc(S("cum_ready"), 1)
            dve.wait_ge(S("cum_ready"), 1)
            cum = slab[:, 4, 1024:2048].rearrange("p (n t) -> p n t", t=CHUNK)
            tt(slab[:, 7, 1024:2048].rearrange("p (n t) -> p n t", t=CHUNK),
               cum[:, :, CHUNK - 1:CHUNK].broadcast_to([P, 16, CHUNK]), cum, ALU.subtract
               ).then_inc(S("toend_ready"), 1)
            causal_conv(chan(2), chan(3), "conv_w", CONV_W, "conv_b", [(c, c, c) for c in range(4, 8)],
                        "conv_tap", n, between={V_LAGS[0]: lambda: take_v(0), V_LAGS[1]: lambda: take_v(1)})
            dve.wait_ge(S("decay_ready"), 1)
            wait_read(dve, "k0", "k1")
            tt(half(5, 0), half(4, 0), la, ALU.mult).then_inc(S("kdec_ready"), 1)
            o = wait_full(dve, "csum")
            read(ts(mean, o[:, 0:T], -1.0 / D, None, ALU.mult), "csum")
            for t in range(TT):
                o = wait_full(dve, f"kdt{t}")
                read(v.tensor_copy(slab[:, 5, 1024 + 512 * t:1536 + 512 * t], o[:]), f"kdt{t}")
            wait_read(dve, "csum")
            for c in range(DC):
                tt(chan(3)[:, c, :], chan(3)[:, c, :], mean, ALU.add).then_inc(S("centered"), 1)
            dve.wait_ge(S("decay_ready"), 2)
            for n in range(NCH):
                for hp in range(2):
                    o = wait_full(dve, f"kv{2 * n + hp}")
                    if n:
                        wait_read(dve, f"kv{2 * n - 2 + hp}")
                    for m in range(2):
                        h = 2 * hp + m
                        if n == 0:
                            ins = v.tensor_copy(states(n, h), o[:, HV * m:HV * m + HV])
                        else:
                            ins = stt(states(n, h), states(n - 1, h), small[:, 4 * h + n:4 * h + n + 1],
                                      o[:, HV * m:HV * m + HV], ALU.mult, ALU.add)
                    read(ins, f"kv{2 * n + hp}")
            wait_read(dve, "csq")
            v.reciprocal(mean, conv_root).then_inc(S("conv_rstd"), 1)
            dve.wait_ge(S("conv_rstd"), 1)
            for c in range(DC):
                tt(chan(3)[:, c, :], chan(3)[:, c, :], mean, ALU.mult).then_inc(S("conv_normed"), 1)
            dve.wait_ge(S("conv_high"), 1)
            low_part(slab[:, 3, :], slab[:, 4, :], slab[:, 3, :]).then_inc(S("conv_low"), 1)
            for j in range(2):
                wait_read(dve, f"osum{j}")
            v.reciprocal(slab[:, 7, 1024:2048], slab[:, 7, 1024:2048]).then_inc(S("o_rstd"), 1)
            dve.wait_ge(S("o_rstd"), 1)
            for c in range(DC):
                ins = stt(chan(10)[:, c, :], chan(10)[:, c, :], col("gla_g", c), half(7, 1)[:, c // 2, :],
                          ALU.mult, ALU.mult)
            ins.then_inc(S("o_normed"), 1)
            dve.wait_ge(S("o_normed"), 1)
            wait_read(dve, "r0", "r1", "r2", "r3")
            tt(slab[:, 10, :], slab[:, 10, :], slab[:, 0, :], ALU.mult).then_inc(S("gla_ready"), 1)
            dve.wait_ge(S("gla_high"), 1)
            low_part(slab[:, 10, :], slab[:, 5, :], slab[:, 10, :]).then_inc(S("gla_low"), 1)
            wait_read(dve, "ga0", "ga1", "ga2", "ga3", "gb0", "gb1", "gb2", "gb3")
            for j in range(4):
                o = wait_full(dve, f"yc{j}")
                for m in range(2):
                    c = 2 * j + m
                    ins = stt(chan(1)[:, c, :], o[:, T * m:T * m + T], col("b_co", c), chan(1)[:, c, :],
                              ALU.add, ALU.mult)
                read(ins, f"yc{j}")
            for j in range(4):
                o = wait_full(dve, f"yg{j}")
                gb = slab[:, 6, 512 * j:512 * j + 512]
                mj = slab[:, 1, 512 * j:512 * j + 512]
                read(tt(gb, o[:], gb, ALU.mult), f"yg{j}")
                wait_read(dve, f"yg{j}", f"yc{j}")
                tt(mj, mj, gb, ALU.add).then_inc(S("merged_ready"), 1)
                dve.wait_ge(S("merged_high"), j + 1)
                low_part(mj, slab[:, 8, 512 * j:512 * j + 512], mj).then_inc(S("merged_low"), 1)
            dve.wait_ge(S("x_landed"), 16)
            dve.wait_ge(S("small_landed"), 16 * SMALL_LOADS)
            x = tok(2)
            for t in range(TT):
                stt(x[:, t, :], x[:, t, :], ALPHA, rows[:, 1, :], ALU.mult, ALU.add).then_inc(S("x_scaled"), 1)
            dve.wait_ge(S("x_scaled"), TT)
            for u in range(2):
                for t in range(TT):
                    o = wait_full(dve, f"mix{u}_{t}")
                    xs = x[:, t, 512 * u:512 * u + 512]
                    read(tt(xs, xs, o[:], ALU.add), f"mix{u}_{t}")

            def layer_norm(src, dst, t, g, b, at, std_at, done):
                k = done + t
                st = small[:, 160 + 12 * t:172 + 12 * t].rearrange("p (a b) -> p a b", a=2)
                for u in range(2):
                    v.bn_stats(st[:, u, :], src[:, t, 512 * u:512 * u + 512]).then_inc(S("ln_bn"), 1)
                dve.wait_ge(S("ln_bn"), 2 * k + 2)
                v.bn_aggr(small[:, at + 2 * t:at + 2 * t + 2], st).then_inc(S("ln_stats"), 1)
                dve.wait_ge(S("ln_std"), k + 1)
                rs = small[:, std_at + 2 + t:std_at + 3 + t]
                v.reciprocal(rs, small[:, std_at + t:std_at + t + 1]).then_inc(S("ln_rstd"), 1)
                dve.wait_ge(S("ln_rstd"), k + 1)
                ts(dst[:, t, :], src[:, t, :], small[:, at + 2 * t:at + 2 * t + 1], rs, ALU.subtract, ALU.mult
                   ).then_inc(S("ln_a"), 1)
                dve.wait_ge(S("ln_a"), k + 1)
                tt(dst[:, t, :], dst[:, t, :], g, ALU.mult).then_inc(S("ln_b"), 1)
                dve.wait_ge(S("ln_b"), k + 1)
                return tt(dst[:, t, :], dst[:, t, :], b, ALU.add)

            dve.wait_ge(S("small_landed"), 16 * SMALL_LOADS)
            dve.wait_ge(S("ln1b_landed"), 16)
            for t in range(TT):
                wait_read(dve, f"mix0_{t}", f"mix1_{t}")
                layer_norm(x, tok(0), t, rows[:, 2, :], rows[:, 0, :], 16, 20, 0).then_inc(S("x1_ready"), 1)
            dve.wait_ge(S("x1_ready"), TT)
            v.memset(zeros, 0.0).then_inc(S("zeros_ready"), 1)
            dve.wait_ge(S("small_landed"), 16 * SMALL_LOADS)
            o = wait_full(dve, "lg")
            for t in range(TT):
                ins = tt(logit[:, t, :], o[:, 128 * t:128 * t + 72], b_route[:], ALU.add)
            read(ins, "lg")
            wait_read(dve, "lg")
            dve.wait_ge(S("consts_ready"), CONSTS)
            for t in range(TT):
                v.max(g_top[:, t, :], logit[:, t, 0:NG]).then_inc(S("route_step"), 1)
            dve.wait_ge(S("route_step"), 2)
            for t in range(TT):
                v.max_index(g_idx[:, t, :], g_top[:, t, :], logit[:, t, 0:NG]).then_inc(S("route_step"), 1)
            for t in range(TT):
                ts(small[:, 30 + t:31 + t], g_top[:, t, 0:1], -1.0, None, ALU.mult).then_inc(S("gtop_ready"), 1)
            dve.wait_ge(S("route_step"), 4)
            gi = small[:, 38:40]
            v.tensor_copy(gi, g_idx[:, :, 0:1].rearrange("p t a -> p (t a)")).then_inc(S("route_step"), 1)
            dve.wait_ge(S("route_step"), 5)
            for t in range(TT):
                ts(onehot[:, t, :], numbers[:, 0:NG], gi[:, t:t + 1], None, ALU.is_equal).then_inc(S("route_step"), 1)
            dve.wait_ge(S("route_step"), 7)
            for t in range(TT):
                tt(picked[:, t, :, :], logit[:, t, NG:].rearrange("p (g i) -> p i g", g=NG),
                   onehot[:, t:t + 1, :].broadcast_to([P, EPG, NG]), ALU.mult).then_inc(S("route_step"), 1)
            dve.wait_ge(S("route_step"), 9)
            for t in range(TT):
                v.tensor_reduce(e_log[:, t, :], picked[:, t, :, :], AX_X, ALU.add).then_inc(S("route_step"), 1)
            dve.wait_ge(S("route_step"), 11)
            for t in range(TT):
                v.max(e_top[:, t, :], e_log[:, t, :]).then_inc(S("route_step"), 1)
            dve.wait_ge(S("route_step"), 13)
            for t in range(TT):
                v.max_index(e_idx[:, t, :], e_top[:, t, :], e_log[:, t, :]).then_inc(S("route_step"), 1)
            tt(small[:, 34:36], e_top[:, :, 1:2].rearrange("p t a -> p (t a)"),
               e_top[:, :, 0:1].rearrange("p t a -> p (t a)"), ALU.subtract).then_inc(S("ediff_ready"), 1)
            dve.wait_ge(S("route_step"), 15)
            ef = small[:, 156:160]
            v.tensor_copy(ef.rearrange("p (t a) -> p t a", t=TT), e_idx[:, :, 0:2]).then_inc(S("route_step"), 1)
            dve.wait_ge(S("route_step"), 16)
            for t in range(TT):
                stt(small[:, 184 + 2 * t:186 + 2 * t], gi[:, t:t + 1].broadcast_to([P, 2]), float(EPG),
                    ef[:, 2 * t:2 * t + 2], ALU.mult, ALU.add).then_inc(S("route_step"), 1)
            dve.wait_ge(S("route_step"), 18)
            for t in range(TT):
                ts(mask_a[:, t, :], numbers[:], small[:, 184 + 2 * t:185 + 2 * t], None, ALU.is_equal
                   ).then_inc(S("route_step"), 1)
                ts(mask_b[:, t, :], numbers[:], small[:, 185 + 2 * t:186 + 2 * t], None, ALU.is_equal
                   ).then_inc(S("route_step"), 1)
            dve.wait_ge(S("route_step"), 22)
            tt(mask, mask_a, mask_b, ALU.add).then_inc(S("mask_ready"), 1)
            dve.wait_ge(S("ratio_ready"), 1)
            dve.wait_ge(S("gsum_ready"), TT)
            den, w0, w1 = small[:, 188:190], small[:, 190:192], small[:, 24:26]
            stt(den, small[:, 36:38], 1.0, small[:, 32:34], ALU.add, ALU.mult).then_inc(S("route_step"), 1)
            dve.wait_ge(S("route_step"), 23)
            v.reciprocal(w0, den).then_inc(S("route_step"), 1)
            dve.wait_ge(S("route_step"), 24)
            tt(w1, w0, small[:, 36:38], ALU.mult).then_inc(S("route_step"), 1)
            dve.wait_ge(S("route_step"), 25)
            dve.wait_ge(S("consts_ready"), CONSTS)
            for t in range(TT):
                ts(mask_a[:, t, :], mask_a[:, t, :], w0[:, t:t + 1], None, ALU.mult).then_inc(S("route_step"), 1)
            dve.wait_ge(S("route_step"), 27)
            for t in range(TT):
                wt = meta[:, 0:NE, 2 + t:3 + t].rearrange("p n a -> p (n a)")
                stt(wt, mask_b[:, t, :], w1[:, t:t + 1], mask_a[:, t, :], ALU.mult, ALU.add
                    ).then_inc(S("route_step"), 1)
            o = wait_full(dve, "pos")
            stt(slotted, o[:, 0:128], 1.0, mask.rearrange("p t n -> p (t n)"), ALU.add, ALU.mult
                ).then_inc(S("route_step"), 1)
            v.tensor_reduce(small[:, 26:27], o[:, 128:192], AX_X, ALU.max).then_inc(S("route_step"), 1)
            dve.wait_ge(S("route_step"), 31)
            read(ts(over[:], small[:, 26:27], float(CAP), None, ALU.is_gt), "pos")
            v.memset(spread[:, 1, :], 0.0).then_inc(S("spread_copied"), 1)
            v.memset(y_sb[:, 1, 512:1024], 0.0).then_inc(S("y1_copied"), 1)
            dve.wait_ge(S("route_step"), 31)
            ts(meta[:, 0:NE, 0:2].rearrange("p n t -> p t n"), slotted.rearrange("p (t n) -> p t n", t=TT),
               -1.0, None, ALU.add).then_inc(S("meta_ready"), 1)

            def select(f, par, r):
                m = meta[:, bass.ds(f, 1), :] if not isinstance(f, int) else meta[:, f:f + 1, :]
                v.tensor_copy(meta_f[:, par, :], m.rearrange("p a b -> p (a b)")).then_inc(S("metaf_ready"), 1)
                dve.wait_ge(S("metaf_ready"), r * META + f + 1)
                for t in range(TT):
                    ts(sel[:, par, t, :], slots[:, 0:CAP], meta_f[:, par, t:t + 1], None,
                       ALU.is_equal).then_inc(S("sel_ready"), 1)
                for t in range(TT):
                    ts(selw[:, par, t, :], slots[:], meta_f[:, par, t:t + 1], meta_f[:, par, 2 + t:3 + t],
                       ALU.is_equal, ALU.mult).then_inc(S("selw_ready"), 1)

            def expert(e, q, r):
                n = r * NE + e
                dve.wait_ge(S("up_full"), n + 1)
                v.tensor_copy(u_sb, up_bank[:]).then_inc(S("u_copied"), 1)
                dve.wait_ge(S("spread_full"), n + 1)
                v.tensor_copy(spread[:, q, :], y_bank[:, 0:256]).then_inc(S("spread_copied"), 1)
                dve.wait_ge(S("silu_ready"), n + 1)
                tt(slab[:, 1, 1664:1792], slab[:, 1, 1536:1664], gate_bank[:, 128:256], ALU.mult
                   ).then_inc(S("h_ready"), 1)
                dve.wait_ge(S("y1_full"), n + 1)
                v.tensor_copy(y_sb[:, q, 512:1024], up_bank[:]).then_inc(S("y1_copied"), 1)
                select(e + 2, q, r)

            dve.wait_ge(S("meta_ready"), 1)
            dve.wait_ge(S("consts_ready"), CONSTS)
            for f in range(2):
                select(f, f, 0)
            with dve.Fori(0, NE // 2) as it:
                for q in range(2):
                    expert(2 * it + q, q, 0)
            more = dve.value_load(over[0:1, 0:1], min_val=0, max_val=1)
            with dve.If(more > 0):
                with dve.Fori(1, ROUNDS) as r:
                    dve.wait_ge(S("combined"), r * (NE + 1))
                    ts(meta[:, :, 0:TT], meta[:, :, 0:TT], -float(CAP), None, ALU.add).then_inc(S("meta_moved"), 1)
                    dve.wait_ge(S("meta_moved"), r)
                    for f in range(2):
                        select(f, f, r)
                    v.memset(spread[:, 1, :], 0.0).then_inc(S("spread_copied"), 1)
                    v.memset(y_sb[:, 1, 512:1024], 0.0).then_inc(S("y1_copied"), 1)
                    with dve.Fori(0, NE // 2) as it:
                        for q in range(2):
                            expert(2 * it + q, q, r)
                dve.wait_ge(S("combined"), ROUNDS * (NE + 1))
            dve.wait_ge(S("combined"), NE + 1)
            dve.wait_ge(S("ln2_landed"), 32)
            for t in range(TT):
                for hf in range(2):
                    d = tok(10)[:, t, 512 * hf:512 * hf + 512]
                    stt(d, tok(0)[:, t, 512 * hf:512 * hf + 512], ALPHA, acc[t][hf][:], ALU.mult, ALU.add
                        ).then_inc(S("moe_out"), 1)
                dve.wait_ge(S("moe_out"), 2 * t + 2)
                layer_norm(tok(10), tok(10), t, rows[:, 1, :], rows[:, 2, :], 42, 46, TT
                           ).then_inc(S("x2_ready"), 1)

            def rms_apply(dst, done, at):
                for t in range(TT):
                    dve.wait_ge(S("rms_root"), done + t + 1)
                    rs = small[:, at + 2 + t:at + 3 + t]
                    v.reciprocal(rs, rs).then_inc(S("rms_inverse"), 1)
                    dve.wait_ge(S("rms_inverse"), done + t + 1)
                    ts(tok(dst)[:, t, :], tok(10)[:, t, :], rs, None, ALU.mult).then_inc(S("xn_ready"), 1)

            def low_turned(tasks, gain, done):
                for i, task in enumerate(tasks):
                    o = wait_full(dve, task)
                    dve.wait_ge(S("xn_high"), done + i + 1)
                    for m in range(2):
                        c = 2 * i + m
                        ins = stt(r32(xn_parts[1][:, c, :]), o[:, T * m:T * m + T], col(gain, c),
                                  r32(xn_parts[0][:, c, :]), ALU.mult, ALU.subtract)
                    read(ins, task)

            rms_apply(1, 0, 50)
            low_turned([f"x2t{j}" for j in range(4)], "mix_norm", 0)
            lam = cols[:, COLS["lam"]:COLS["lam"] + 8]
            stt(small[:, 72:80], lam, -1.0, lam, ALU.mult, ALU.min).then_inc(S("lam_negabs"), 1)
            dve.wait_ge(S("lam_exp"), 1)
            e_, d_, s_, s2, pl = (small[:, 80 + 8 * i:88 + 8 * i] for i in range(5))
            ts(d_, e_, 2.0, None, ALU.add).then_inc(S("rate_step"), 1)
            dve.wait_ge(S("rate_step"), 1)
            v.reciprocal(d_, d_).then_inc(S("rate_step"), 1)
            dve.wait_ge(S("rate_step"), 2)
            tt(s_, e_, d_, ALU.mult).then_inc(S("rate_step"), 1)
            dve.wait_ge(S("rate_step"), 3)
            tt(s2, s_, s_, ALU.mult).then_inc(S("rate_step"), 1)
            dve.wait_ge(S("rate_step"), 4)
            ts(pl, s2, 1.0 / 17, 1.0 / 15, ALU.mult, ALU.add).then_inc(S("rate_step"), 1)
            n = 5
            for k in (13, 11, 9, 7, 5, 3, 1):
                dve.wait_ge(S("rate_step"), n)
                tt(pl, pl, s2, ALU.mult).then_inc(S("rate_step"), 1)
                dve.wait_ge(S("rate_step"), n + 1)
                ts(pl, pl, 1.0 / k, None, ALU.add).then_inc(S("rate_step"), 1)
                n += 2
            dve.wait_ge(S("rate_step"), n)
            tt(pl, pl, s_, ALU.mult).then_inc(S("rate_step"), 1)
            ts(d_, lam, -1.0, 0.0, ALU.mult, ALU.max).then_inc(S("rate_step"), 1)
            dve.wait_ge(S("rate_step"), n + 2)
            stt(pl, pl, 2.0, d_, ALU.mult, ALU.add).then_inc(S("rate_step"), 1)
            dve.wait_ge(S("rate_step"), n + 3)
            ts(pl, pl, -8.0, None, ALU.mult).then_inc(S("rate_ready"), 1)
            for j in range(4):
                wait_read(dve, f"lx{j}")
                causal_conv(chan(1), chan(2), "lru_w", LRU_W, "lru_b", [(2 * j + m,) * 3 for m in range(2)],
                            "lru_tap", 2 * LRU_W * j)
            wait_read(dve, "li0", "li1", "li2", "li3")
            tt(slab[:, 5, :], slab[:, 5, :], slab[:, 2, :], ALU.mult).then_inc(S("ua_used"), 1)
            dve.wait_ge(S("a_ready"), 1)
            tt(slab[:, 1, :], slab[:, 4, :], slab[:, 4, :], ALU.mult).then_inc(S("asq"), 1)
            dve.wait_ge(S("asq"), 1)
            stt(slab[:, 6, :], slab[:, 1, :], 1.0, slab[:, 6, :], ALU.add, ALU.mult).then_inc(S("mult2_ready"), 1)
            dve.wait_ge(S("asq"), 1)
            v.memset(chan(4)[:, :, 0:1], 0.0).then_inc(S("a_cut"), 1)
            dve.wait_ge(S("mult_ready"), 1)
            dve.wait_ge(S("ua_used"), 1)
            tt(slab[:, 5, :], slab[:, 5, :], slab[:, 6, :], ALU.mult).then_inc(S("u_ready"), 1)
            dve.wait_ge(S("u_ready"), 1)
            dve.wait_ge(S("a_cut"), 1)
            v.tensor_tensor_scan(slab[:, 1, :], slab[:, 4, :], slab[:, 5, :], 0.0, ALU.mult, ALU.add
                                 ).then_inc(S("lru_done"), 1)
            dve.wait_ge(S("lru_done"), 1)
            wait_read(dve, "lg_0", "lg_1", "lg_2", "lg_3")
            tt(slab[:, 1, :], slab[:, 1, :], slab[:, 3, :], ALU.mult).then_inc(S("ya_ready"), 1)
            wait_read(dve, "ksum")
            v.reciprocal(k_sq, k_sq).then_inc(S("k_rstd"), 1)
            dve.wait_ge(S("k_rstd"), 1)
            stt(slab[:, 7, 0:512], slab[:, 7, 0:512], col("k_norm"), k_sq, ALU.mult, ALU.mult
                ).then_inc(S("k_ready"), 1)
            wait_read(dve, "kiwi_w")
            steps = 0
            for t in range(TT):
                n = P * (t + 1)
                rel = slab[:, 4 + t, :].rearrange("p (h s) -> p h s", h=IH)
                for h in range(IH):
                    if h % 2 == 0:
                        wait_read(dve, f"dots{t}_{h // 2}")
                    w = indexer_head(h // 2, h % 2)
                    sc = score[:, t, 0:n]
                    if h == 0:
                        ins = ts(sc, rel[:, h, 0:n], wih[:, t, w:w + 1], None, ALU.mult)
                    else:
                        dve.wait_ge(S("score_step"), steps)
                        ins = stt(sc, rel[:, h, 0:n], wih[:, t, w:w + 1], sc, ALU.mult, ALU.add)
                    if h < IH - 1:
                        ins.then_inc(S("score_step"), 1)
                        steps += 1
                    else:
                        ins.then_inc(S("score_ready"), 1)
            for j in range(4):
                wait_read(dve, f"qsum{j}")
                r6 = slab[:, 6, 512 * j:512 * j + 512]
                q9 = slab[:, 9, 512 * j:512 * j + 512]
                v.reciprocal(r6, r6).then_inc(S("q_rstd"), 1)
                dve.wait_ge(S("q_rstd"), j + 1)
                stt(q9, q9, col("q_norm"), r6, ALU.mult, ALU.mult).then_inc(S("q_ready"), 1)
            steps = 0
            for t in range(TT):
                n = P * (t + 1)
                w_ = work[:, t, 0:n]
                dve.wait_ge(S("work_ready"), t + 1)
                for i in range(TOPK // 8):
                    if steps:
                        dve.wait_ge(S("top_step"), steps)
                    v.max(best, w_).then_inc(S("top_step"), 1)
                    dve.wait_ge(S("top_step"), steps + 1)
                    v.match_replace(w_, best, w_, TAKEN).then_inc(S("top_step"), 1)
                    steps += 2
                dve.wait_ge(S("top_step"), steps)
                ts(score[:, t, 0:n], w_, 2.0 * FILL, HIDE, ALU.is_gt, ALU.mult).then_inc(S("hide_made"), 1)
            wait_read(dve, "gc0", "gc1", "gc2", "gc3")
            for j in range(4):
                o = wait_full(dve, f"ya{j}")
                m3 = slab[:, 3, 512 * j:512 * j + 512]
                read(tt(m3, o[:], m3, ALU.mult), f"ya{j}")
            for t in range(TT):
                n = P * (t + 1)
                dve.wait_ge(S("bias_landed"), 16 * (t + 1))
                dve.wait_ge(S("hide_ready"), t + 1)
                if t:
                    for k in range(2):
                        wait_full(dve, f"pt0_0_{k}")
                for j in range(4):
                    o = wait_full(dve, f"log{t}_{j}")
                    dst = lgt[:, 2 * j:2 * j + 2, 0:n]
                    bias = slab[:, 2, 512 * j:512 * j + 512].rearrange("p (m s) -> p m s", m=2)[:, :, ::-1][:, :, 0:n]
                    read(stt(dst, o[:].rearrange("p (m s) -> p m s", m=2)[:, :, 0:n], HD ** -0.5, bias,
                             ALU.mult, ALU.add), f"log{t}_{j}")
                    wait_read(dve, f"log{t}_{j}")
                    tt(dst, dst, score[:, t:t + 1, 0:n].broadcast_to([P, 2, n]), ALU.add
                       ).then_inc(S("logits_ready"), 1)
                dve.wait_ge(S("logits_ready"), 4 * (t + 1))
                v.tensor_reduce(small[:, 128:136], lgt[:, :, 0:n], AX_X, ALU.max).then_inc(S("rowmax"), 1)
                dve.wait_ge(S("rowmax"), t + 1)
                ts(small[:, 128:136], small[:, 128:136], -1.0, None, ALU.mult).then_inc(S("rowmax_ready"), 1)
                dve.wait_ge(S("exp_ready"), t + 1)
                v.reciprocal(small[:, 136:144], small[:, 136:144]).then_inc(S("rowsum"), 1)
                dve.wait_ge(S("rowsum"), t + 1)
                tt(lgt[:, :, 0:n], lgt[:, :, 0:n],
                   small[:, 136:144].rearrange("p (h a) -> p h a", a=1).broadcast_to([P, NH, n]), ALU.mult
                   ).then_inc(S("probs_ready"), 1)
            dve.wait_ge(S("att_high"), 1)
            low_part(slab[:, 6, :], slab[:, 9, :], slab[:, 6, :]).then_inc(S("att_low"), 1)
            wait_read(dve, "gd0", "gd1", "gd2", "gd3")
            for j in range(4):
                o = wait_full(dve, f"yb{j}")
                g1 = slab[:, 1, 512 * j:512 * j + 512]
                m3 = slab[:, 3, 512 * j:512 * j + 512]
                read(tt(g1, o[:], g1, ALU.mult), f"yb{j}")
                wait_read(dve, f"yb{j}", f"ya{j}")
                tt(m3, m3, g1, ALU.add).then_inc(S("merged2_ready"), 1)
                dve.wait_ge(S("merged2_high"), j + 1)
                low_part(m3, slab[:, 7, 512 * j:512 * j + 512], m3).then_inc(S("merged2_low"), 1)

            def residual(pre):
                for u in range(2):
                    for t in range(TT):
                        o = wait_full(dve, f"{pre}{u}_{t}")
                        xs = tok(10)[:, t, 512 * u:512 * u + 512]
                        read(tt(xs, xs, o[:], ALU.add), f"{pre}{u}_{t}")

            residual("mo")
            rms_apply(4, TT, 54)
            low_turned([f"x3t{j}" for j in range(4)], "ffn_norm", 4)
            def hidden_low(i):
                dve.wait_ge(S("hid_high"), i + 1)
                tt(r32(hid_parts[1][:, 4 * i:4 * i + 4, :]), half(5, i % 2), r32(hT[:, 4 * i:4 * i + 4, :]),
                   ALU.subtract).then_inc(S("hid_low"), 1)

            for i in range(6):
                wait_read(dve, f"fg{i}_0", f"fg{i}_1")
                if i == 0:
                    wait_read(dve, "x3t3")
                if i >= 2:
                    dve.wait_ge(S("hid_low"), i - 1)
                causal_conv(half(4, i % 2), half(5, i % 2), "ffn_w", FFN_W, "ffn_b",
                            [(c, c, 4 * i + c) for c in range(4)], "ffn_tap", 4 * FFN_W * i)
                if i:
                    hidden_low(i - 1)
                dve.wait_ge(S("fgelu_ready"), i + 1)
                for j in range(2):
                    o = wait_full(dve, f"fu{i}_{j}")
                    hj = half(5, i % 2)[:, 2 * j:2 * j + 2, :].rearrange("p a t -> p (a t)")
                    read(tt(hj, o[:], hj, ALU.mult), f"fu{i}_{j}")
            hidden_low(5)
            residual("dn")
            rms_apply(4, 2 * TT, 62)
            low_turned([f"x4t{j}" for j in range(4)], "ple_norm", 8)
            for u in range(2):
                for t in range(TT):
                    o = wait_full(dve, f"pp{u}_{t}")
                    read(v.tensor_copy(tok(5)[:, t, 512 * u:512 * u + 512], o[:]), f"pp{u}_{t}")
            for u in range(2):
                for t in range(TT):
                    wait_read(dve, f"pg{u}_{t}", f"pp{u}_{t}")
                    gate = tok(4)[:, t, 512 * u:512 * u + 512]
                    tt(gate, gate, tok(5)[:, t, 512 * u:512 * u + 512], ALU.mult).then_inc(S("ple_step"), 1)
                    dve.wait_ge(S("ple_step"), 2 * u + t + 1)
                    xs = tok(10)[:, t, 512 * u:512 * u + 512]
                    ins = tt(xs, xs, gate, ALU.add)
                    if u:
                        ins.then_inc(S("out_ready"), 1)


def _bucket_rows():
    dist = np.maximum(np.arange(511) - (T - 1), 0)
    exact = NB // 2
    far = exact + (np.log(np.maximum(dist, 1).astype(np.float32) / exact) / np.float32(np.log(MAXD / exact))
                   * (NB - exact)).astype(np.int32)
    bucket = np.where(dist < exact, dist, np.minimum(far, NB - 1))
    return (np.arange(NB)[:, None] == bucket[None, :]).astype(np.float32)


def _unit(w):
    return w.reshape(-1, P, w.shape[1]).transpose(1, 0, 2).reshape(P, -1)


def _layout(i):
    f = {k: np.asarray(v) for k, v in i.items()}
    w_in, b_in = f["w_in"][0], f["b_in"][0]
    at = np.cumsum([0, D, D, 512, 512, D, D, RANK, D, D])
    ca, cg, q, k, vv, r, fl, ga, gb = (w_in[:, at[j]:at[j + 1]] for j in range(9))
    bca, bcg, bq, bk, bv, br, bfl, bga, bgb = (b_in[at[j]:at[j + 1]] for j in range(9))

    def two(w):
        return [w[:, 0:512], w[:, 512:1024]]

    first = [cg[:, :512], ca[:, :512], cg[:, 512:], ca[:, 512:], k] + two(vv) + [q] + two(r) + two(ga) + two(gb)
    first += two(f["w_conv_out"][0]) + two(f["w_gla_out"][0]) + two(f["w_out"][0])
    units1 = np.stack([_unit(w) for w in first])

    w2 = f["w_in_2"][0]
    at = np.cumsum([0, D, D, D, 256, 256, 512, 64, 8, D, D])
    lx, lg, q2, k2, v2, qi, ki, wi, gc, gd = (w2[:, at[j]:at[j + 1]] for j in range(10))
    up = f["w_up_2"][0]
    down = f["w_down_2"][0]
    second = two(lx) + two(lg) + [np.concatenate([k2, v2], 1), qi]
    units2 = [_unit(w) for w in second]
    units2.append(np.concatenate([f["lru_wa_2"][0], f["lru_wx_2"][0]]).transpose(1, 0, 2).reshape(P, -1))
    units2 += [_unit(w) for w in two(q2) + two(gc) + two(f["w_lru_br_2"][0]) + two(gd) + two(f["w_attn_br_2"][0])
               + two(f["w_out_2"][0])]
    for j in range(6):
        units2 += [_unit(up[:, 512 * j:512 * j + 512]), _unit(up[:, FF + 512 * j:FF + 512 * j + 512])]
    for u in range(2):
        for j in range(3):
            units2.append(_unit(down[D * j:D * j + D, 512 * u:512 * u + 512]))
    units2.append(_unit(f["w_ple_proj_2"][0]))
    units2 += [_unit(w) for w in two(f["w_ple_gate_2"][0])]
    full2 = np.zeros((len(units2), P, UNIT), np.float32)
    for j, w in enumerate(units2):
        full2[j, :, :w.shape[1]] = w

    def per_channel(x):
        return x.reshape(-1, P).T

    cols = np.zeros((P, NCOLS), np.float32)

    def put(name, x):
        cols[:x.shape[0], COLS[name]:COLS[name] + x.shape[1]] = x

    for name, x in (("b_conv_a", bca), ("b_conv_g", bcg), ("b_q", bq), ("b_k", bk), ("b_r", br), ("b_ga", bga),
                    ("b_gb", bgb), ("conv_b", f["conv_b"]), ("cln_g", f["conv_ln_g"]), ("cln_b", f["conv_ln_b"]),
                    ("b_co", f["b_conv_out"]), ("b_gate", f["b_gate_up"]), ("gla_g", f["gla_norm_g"]),
                    ("mix_norm", f["mix_norm_2"]), ("lru_b", f["lru_conv_b_2"]), ("lru_ba", f["lru_ba_2"]),
                    ("lru_bx", f["lru_bx_2"]), ("lam", f["lru_lambda_2"]), ("q_norm", f["q_norm_2"]),
                    ("k_norm", f["k_norm_2"]), ("ffn_norm", f["ffn_norm_2"]), ("ffn_b", f["ffn_conv_b_2"]),
                    ("ple_norm", f["ple_norm_2"])):
        put(name, per_channel(x))
    put("b_flr", bfl[:, None])
    for name, x in (("conv_w", f["conv_w"]), ("lru_w", f["lru_conv_w_2"]), ("ffn_w", f["ffn_conv_w_2"])):
        put(name, x[0].reshape(x.shape[1], -1, P).transpose(2, 1, 0).reshape(P, -1))

    route = np.concatenate([f["w_router_group"][0], f["w_router_expert"][0]], 1)
    return {
        "xT": np.ascontiguousarray(_unit(f["x"][0].T)), "x": f["x"],
        "cols": cols, "units1": units1, "units2": full2,
        "w1": f["w1"][0], "w3": f["w3"][0], "w2": f["w2"][0],
        "w_flr": np.ascontiguousarray(_unit(fl).reshape(P, DC, RANK)), "w_gate_up": f["w_gate_up"][0],
        "b_v": bv, "b_out": f["b_out"][0], "ln1_g": f["ln1_g"][0], "ln1_b": f["ln1_b"][0],
        "ln2_g": f["ln2_g"][0], "ln2_b": f["ln2_b"][0],
        "w_route": np.ascontiguousarray(_unit(route).reshape(P, DC, NG + NE)),
        "b_route": np.concatenate([f["b_router_group"][0], f["b_router_expert"][0]]),
        "w_kiwi": np.ascontiguousarray(_unit(np.concatenate([ki, ki, wi], 1))),
        "rel_bias": f["rel_bias_2"], "buckets": _bucket_rows(),
        "pT": np.ascontiguousarray(_unit(f["p_2"][0, 0].T)),
    }


def kernel(**inputs):
    import concourse.bacc as bacc
    from concourse.bass_utils import run_bass_kernel_spmd

    nc = bacc.Bacc("TRN2", target_bir_lowering=False, num_devices=1)
    arrays, aps = {}, {}
    for name, x in _layout(inputs).items():
        x = np.ascontiguousarray(x)
        arrays[f"in_{name}"] = x
        aps[name] = nc.dram_tensor(f"in_{name}", x.shape, mybir.dt.from_np(x.dtype), kind="ExternalInput").ap()
    out = nc.dram_tensor("out", (1, T, D), F32, kind="ExternalOutput").ap()
    build(nc, aps, out)
    return run_bass_kernel_spmd(nc, [arrays], core_ids=[0]).results[0]["out"]
```

```python
from contextlib import ExitStack

import numpy as np

import concourse.bass as bass
from concourse import mybir

ALU = mybir.AluOpType
ACT = mybir.ActivationFunctionType
F32 = mybir.dt.float32
F32R = mybir.dt.float32r
I32 = mybir.dt.int32
U32 = mybir.dt.uint32
AX_X = mybir.AxisListType.X

P = 128
T = 256
TT = T // P
D = 1024
DC = D // P
UNIT = 4096
RING = 6
V_LAGS = (4, 12)
GLU_LAG, GATE_LAG = 18, 29
STREAM = 4
ALPHA = 2.0 ** 0.25

CONV_W = 31
CHUNK = 64
NCH = T // CHUNK
H1, HK, HV = 4, 128, 256
RANK = 16
TAU = 16.0

NG, EPG = 8, 8
NE = NG * EPG
SMALL_LOADS = 7
CONSTS = 10
CAP = 32
ROUNDS = T // CAP
META = NE + 2

NH, NKV, HD = 8, 2, 128
QPK = NH // NKV
IH, ID = 8, 64
TOPK = 64
NB, MAXD = 32, 128
LRU_W = 4
FF = 3072
FFC = FF // P
FFN_W = 3
PLE = 256
FILL = -1.0e38
TAKEN = -3.0e38
HIDE = -1.0e30

COLS = {}
_n = 0
for _name, _w in (("b_conv_a", 8), ("b_conv_g", 8), ("b_q", 4), ("b_k", 4), ("b_r", 8), ("b_flr", 1),
                  ("b_ga", 8), ("b_gb", 8), ("conv_w", 8 * CONV_W), ("conv_b", 8), ("cln_g", 8), ("cln_b", 8),
                  ("b_co", 8), ("b_gate", 4), ("gla_g", 8), ("mix_norm", 8), ("lru_w", 8 * LRU_W),
                  ("lru_b", 8), ("lru_ba", 8), ("lru_bx", 8), ("lam", 8), ("q_norm", 1), ("k_norm", 1),
                  ("ffn_norm", 8), ("ffn_w", FFC * FFN_W), ("ffn_b", FFC), ("ple_norm", 8)):
    COLS[_name] = _n
    _n += _w
NCOLS = _n

def _tasks():
    names = []
    names += ["g0", "g1", "a0", "a1", "g2", "g3", "a2", "a3", "k0", "k1", "fl", "z0", "z1"]
    names += [f"v{u}_{t}" for u in range(2) for t in range(2)] + ["q0", "q1"]
    names += [f"r{j}" for j in range(4)] + [f"ga{j}" for j in range(4)]
    names += ["csum", "kdt0", "kdt1"] + [f"kv{i}" for i in range(8)] + ["gb0", "gb1", "csq"]
    names += [f"o{h}" for h in range(4)] + ["gb2", "gb3", "osum0", "osum1"]
    names += [f"yc{j}" for j in range(4)] + [f"yg{j}" for j in range(4)]
    names += [f"mix{u}_{t}" for t in range(2) for u in range(2)]
    names += ["x1t0", "x1t1", "lg", "x1t2", "x1t3", "pos"]
    first = list(names)
    n2 = [f"x2t{j}" for j in range(4)] + ["kiwi_k", "kiwi_w", "relb"]
    n2 += [f"lx{j}" for j in range(4)] + [f"lg_{j}" for j in range(4)]
    n2 += ["kk", "vv", "qi0", "qi1"] + [f"dots{t}_{j}" for t in range(2) for j in range(4)]
    n2 += [f"lr{j}" for j in range(4)] + [f"li{j}" for j in range(4)]
    n2 += ["ksum"] + [f"qq{j}" for j in range(4)]
    n2 += ["gc0", "gc1"] + [f"qsum{j}" for j in range(4)] + ["gc2", "gc3", "ya0", "ya1"]
    for t in range(2):
        n2 += [f"log{t}_{j}" for j in range(4)]
    n2 += ["ya2", "ya3"]
    for t in range(2):
        n2 += [f"pt{t}_{s}_{k}" for s in range(t + 1) for k in range(2)] + [f"pv{t}_{k}" for k in range(2)]
        n2 += [f"gd{2 * t}", f"gd{2 * t + 1}"]
    n2 += [f"yb{j}" for j in range(4)] + [f"mo{u}_{t}" for t in range(2) for u in range(2)]
    n2 += [f"x3t{j}" for j in range(4)]
    for i in range(6):
        n2 += [f"fg{i}_0", f"fg{i}_1", f"fu{i}_0", f"fu{i}_1"]
    n2 += [f"dn{u}_{t}" for u in range(2) for t in range(2)]
    n2 += [f"pp{u}_{t}" for u in range(2) for t in range(2)]
    n2 += [f"x4t{j}" for j in range(4)]
    n2 += [f"pg{u}_{t}" for t in range(2) for u in range(2)]
    return first, n2


TASKS1, TASKS2 = _tasks()
TASK = {name: i for i, name in enumerate(TASKS1 + TASKS2)}

UNITS1 = ["g1", "a1", "g3", "a3", "k1", "v0_1", "v1_1", "q1", "r1", "r3", "ga1", "ga3", "gb1", "gb3",
          "yc1", "yc3", "yg1", "yg3", "mix0_1", "mix1_1"]
UNITS2 = (["lx1", "lx3", "lg_1", "lg_3", "vv", "qi1", "li3", "qq1", "qq3", "gc1", "gc3", "ya1", "ya3",
           "gd1", "gd3", "yb1", "yb3", "mo0_1", "mo1_1"]
          + [f"f{x}{i}_1" for i in range(6) for x in "gu"]
          + ["dn0_1/1", "dn0_1/2", "dn0_1", "dn1_1/1", "dn1_1/2", "dn1_1", "pp1_1", "pg0_1", "pg1_1"])
UNITS = (UNITS1, UNITS2)
SPLIT = (UNITS1[1:], [n for n in UNITS2 if n not in ("li3", "pp1_1")])
assert len(UNITS1) % STREAM == 0


def by_rows(name):
    return name[:2] in ("v0", "v1", "dn", "pg", "mo") or name[:3] == "mix"


def build(nc, a, out):
    with ExitStack() as ctx:
        def sb(name, shape, dt=F32):
            return ctx.enter_context(nc.sbuf_tensor(name, shape, dt))

        sems = {}

        def S(name):
            if name not in sems:
                sems[name] = ctx.enter_context(nc.semaphore(name))
            return sems[name]

        banks = [ctx.enter_context(nc.psum_tensor(f"bank{i}", [P, 512], F32)) for i in range(8)]
        shapes = {"ring": [P, RING, UNIT], "slab": [P, 11, 2048], "rows": [P, 3, D]}
        with ExitStack() as names:
            parts = {name: names.enter_context(nc.sbuf_tensor(f"{name}_parts", shape, F32R))
                     for name, shape in shapes.items()}
        ring, slab, rows = (sb(name, shape) for name, shape in shapes.items())
        cols = sb("cols", [P, NCOLS])
        w_flr = sb("w_flr", [P, DC, RANK])
        w_route = sb("w_route", [P, DC, NG + NE])
        b_route = sb("b_route", [P, NG + NE])
        ident = sb("ident", [P, P])
        alphas = sb("alphas", [P, P])
        ones = sb("ones", [P, P])
        before = sb("before", [P, P])
        stack = sb("stack", [P, CAP])
        slots = sb("slots", [P, P])
        slots_i = sb("slots_i", [P, P], I32)
        numbers = sb("numbers", [P, NE])
        numbers_i = sb("numbers_i", [P, NE], I32)
        eps_ln = sb("eps_ln", [P, 1])
        eps_rms = sb("eps_rms", [P, 1])
        small = sb("small", [P, 192])
        meta = sb("meta", [P, META, 4])
        g_top = sb("g_top", [P, TT, 8])
        g_idx = sb("g_idx", [P, TT, 8], U32)
        e_top = sb("e_top", [P, TT, 8])
        e_idx = sb("e_idx", [P, TT, 8], U32)
        over = sb("over", [P, 1], I32)
        bias_dram = nc.dram_tensor("bias_scratch", (NH, 512), F32, kind="Internal").ap()

        def col(name, i=0):
            return cols[:, COLS[name] + i:COLS[name] + i + 1]

        def chan(s):
            return slab[:, s, :].rearrange("p (c t) -> p c t", c=DC)

        def tok(s):
            return slab[:, s, :].rearrange("p (t d) -> p t d", t=TT)

        def half(s, h):
            return slab[:, s, 1024 * h:1024 * h + 1024].rearrange("p (c t) -> p c t", c=4)

        spare = [slab[:, s:s + 2, :].rearrange("p a b -> p (a b)") for s in (9, 6)]
        xg = slab[:, 1, 0:DC * CAP].rearrange("p (c s) -> p c s", c=DC)
        g_sb = slab[:, 1, 512:1024]
        u_sb = slab[:, 1, 1024:1536]
        silu_sb = slab[:, 1, 1536:1664].rearrange("p (c s) -> p c s", c=4)
        h_sb = slab[:, 1, 1664:1792].rearrange("p (c s) -> p c s", c=4)
        y_sb = tok(2)
        spread = slab[:, 3, 0:512].rearrange("p (a t) -> p a t", a=2)
        sel = slab[:, 3, 512:640].rearrange("p (a t s) -> p a t s", a=2, t=TT)
        selw = slab[:, 3, 1024:1536].rearrange("p (a t s) -> p a t s", a=2, t=TT)
        meta_f = slab[:, 3, 640:648].rearrange("p (a b) -> p a b", a=2)
        zeros = slab[:, 4, 0:512]
        logit = slab[:, 5, 0:TT * 72].rearrange("p (t n) -> p t n", t=TT)
        mask = slab[:, 5, 256:256 + TT * NE].rearrange("p (t n) -> p t n", t=TT)
        mask_a = slab[:, 5, 384:384 + TT * NE].rearrange("p (t n) -> p t n", t=TT)
        mask_b = slab[:, 5, 512:512 + TT * NE].rearrange("p (t n) -> p t n", t=TT)
        picked = slab[:, 5, 640:640 + TT * 64].rearrange("p (t i g) -> p t i g", t=TT, i=EPG)
        e_log = slab[:, 5, 768:768 + TT * 8].rearrange("p (t n) -> p t n", t=TT)
        onehot = slab[:, 5, 784:784 + TT * 8].rearrange("p (t n) -> p t n", t=TT)
        e_exp = slab[:, 5, 800:800 + TT * 8].rearrange("p (t n) -> p t n", t=TT)
        kT = slab[:, 7, 0:512].rearrange("p (h t) -> p h t", h=NKV)
        v2 = slab[:, 7, 512:1024].rearrange("p (t n) -> p t n", t=TT)
        qiT = slab[:, 7, 1024:2048].rearrange("p (c t) -> p c t", c=4)
        kiT = slab[:, 8, 0:256]
        score = slab[:, 8, 256:768].rearrange("p (t s) -> p t s", t=TT)
        work = slab[:, 8, 768:1280].rearrange("p (t s) -> p t s", t=TT)
        k_sq = slab[:, 8, 1280:1792]
        wih = slab[:, 8, 1792:1808].rearrange("p (t h) -> p t h", t=TT)
        best = slab[:, 8, 1808:1816]
        rel = [slab[:, s, :] for s in (6, 9)]
        lgt = slab[:, 4, :].rearrange("p (h s) -> p h s", h=NH)
        prob_t = slab[:, 5, :].rearrange("p (s h t) -> p s h t", s=TT, h=NH)
        hT = slab[:, 1:4, :].rearrange("p a (c t) -> p (a c) t", c=DC)
        turn_ = [banks[(TASK["pos"] + 1 + i) % 8] for i in range(8)]
        acc = [turn_[0:2], turn_[2:4]]
        gate_bank, up_bank, y_bank, gather_bank = turn_[4:8]

        def states(n, h):
            s, at = ((10, 1024), (4, 0), (4, 1024), (7, 1024))[n]
            return slab[:, s, at + HV * h:at + HV * h + HV]

        mean = slab[:, 10, 768:1024]
        conv_root = slab[:, 10, 0:T]
        kiwi_high = slab[:, 4, 512:512 + DC * 136]
        slotted = slab[:, 5, 896:1024]

        def indexer_head(j, m):
            return 4 * (j // 2) + j % 2 + 2 * m

        def bank(task):
            return banks[TASK[task] % 8]

        def take_bank(task):
            if TASK[task] >= 8:
                nc.tensor.wait_ge(S(f"bank_read{TASK[task] % 8}"), TASK[task] // 8)
            return bank(task)

        def full(ins, task):
            ins.then_inc(S(f"bank_full{TASK[task] % 8}"), 1)

        def wait_full(eng, task):
            eng.wait_ge(S(f"bank_full{TASK[task] % 8}"), TASK[task] // 8 + 1)
            return bank(task)

        def read(ins, task):
            ins.then_inc(S(f"bank_read{TASK[task] % 8}"), 1)

        def wait_read(eng, *tasks):
            for task in tasks:
                eng.wait_ge(S(f"bank_read{TASK[task] % 8}"), TASK[task] // 8 + 1)

        def expert_slot(q, w):
            return 3 * q + w

        def wait_used(eng, name):
            if "/" in name:
                eng.wait_ge(S("down_used"), 2 * int(name[2]) + int(name[-1]))
            else:
                wait_full(eng, name)

        def wait_landed(eng, part, name):
            n = UNITS[part].index(name)
            eng.wait_ge(S(f"unit_landed{n % STREAM}"), 16 * (part * (len(UNITS1) // STREAM) + n // STREAM + 1))

        def split_count(part, name):
            return 2 * (part * len(SPLIT[0]) + SPLIT[part].index(name)) + part

        KIWI_COUNT = 2 * len(SPLIT[0])

        def halves(part, name):
            slot_, high = ring[:, UNITS[part].index(name) % STREAM, :], ring[:, STREAM + SPLIT[part].index(name) % 2, :]
            if by_rows(name):
                return [tuple(x[:, 2048 * h:2048 * h + 2048] for x in (slot_, high)) for h in range(2)]
            return [tuple(x.rearrange("p (c n) -> p c n", c=DC)[:, :, 256 * h:256 * h + 256] for x in (slot_, high))
                    for h in range(2)]

        def r32(ap):
            return bass.AP(parts[ap.tensor.name], ap.offset, ap.ap)

        xt_parts = (chan(8), chan(9))
        conv_parts = (chan(4), chan(3))
        gla_parts = (chan(5), chan(10))
        merged_parts = (chan(8), chan(1))
        xn_parts = (chan(0), rows[:, 0:2, :].rearrange("p a (c t) -> p (a c) t", c=4))
        lru_parts = (chan(5), chan(1))
        att_parts = (chan(9), chan(6))
        merged2_parts = (chan(7), chan(3))
        hid_parts = (hT, slab[:, 6:9, :].rearrange("p a (c t) -> p (a c) t", c=DC))

        block = ctx.enter_context(nc.Block())

        @block.sync
        def _(sp):
            sp.dma_start(slab[:, 0, :], a["xT"]).then_inc(S("xt_landed"), 16)
            for n, name in enumerate(UNITS1):
                if n >= STREAM:
                    wait_used(sp, UNITS1[n - STREAM])
                if name == "yg1":
                    wait_full(sp, "csq")
                    sp.dma_start(tok(2), a["x"].rearrange("o (t p) d -> p (o t) d", p=P)).then_inc(S("x_landed"), 16)
                    wait_read(sp, "v0_1", "v1_1")
                    sp.dma_start(rows[:, 0, :], a["ln1_b"].partition_broadcast(P)).then_inc(S("ln1b_landed"), 16)
                if n == 0:
                    for h, name_ in enumerate(("first_half_landed", "unit_landed0")):
                        cut = slice(256 * h, 256 * h + 256)
                        sp.dma_start(ring[:, 0, :].rearrange("p (c n) -> p c n", c=DC)[:, :, cut],
                                     a["units1"][0].rearrange("p (c n) -> p c n", c=DC)[:, :, cut]
                                     ).then_inc(S(name_), 16)
                else:
                    sp.dma_start(ring[:, n % STREAM, :], a["units1"][n]).then_inc(S(f"unit_landed{n % STREAM}"), 16)
                if n == 0:
                    sp.dma_start(cols[:], a["cols"]).then_inc(S("cols_landed"), 16)

            def expert_unit(e, q, w):
                name = ("w1", "w3", "w2")[w]
                src = a[name][bass.ds(e, 1) if not isinstance(e, int) else slice(e, e + 1)]
                src = src.rearrange("e (p c) n -> p (e c n)", p=P)
                sp.dma_start(ring[:, expert_slot(q, w), :], src).then_inc(S(f"expert_landed{3 * q + w}"), 16)

            used = ("gate_full", "up_full", "y1_full")

            def expert_pair(it, r):
                for q in range(2):
                    for w in range(3):
                        sp.wait_ge(S(used[w]), r * NE + 2 * it + q - 1)
                        expert_unit(2 * it + q, q, w)

            def expert_early(e, q, w):
                s = expert_slot(q, w)
                wait_used(sp, UNITS1[s - STREAM] if s < STREAM else [n for n in SPLIT[0] if SPLIT[0].index(n) % 2 == s - STREAM][-1])
                expert_unit(e, q, w)

            expert_early(0, 0, 0)
            expert_early(0, 0, 1)
            wait_used(sp, "yg3")
            sp.dma_start(spare[0], a["w1"][2].rearrange("(p c) n -> p (c n)", p=P)).then_inc(S("spare_w1_landed"), 16)
            sp.wait_ge(S("merged_ready"), 4)
            sp.dma_start(spare[1], a["w3"][2].rearrange("(p c) n -> p (c n)", p=P)).then_inc(S("spare_w3_landed"), 16)
            expert_early(0, 0, 2)
            for w in range(3):
                expert_early(1, 1, w)
            for e, w, n in ((4, 0, 1), (4, 1, 1), (2, 2, 1), (3, 0, 2), (3, 1, 2), (3, 2, 2),
                            (4, 2, 3), (5, 0, 4), (5, 1, 4), (5, 2, 4)):
                sp.wait_ge(S(used[w]), n)
                expert_unit(e, e % 2, w)
            with sp.Fori(3, NE // 2) as it:
                expert_pair(it, 0)
            wait_read(sp, "pos")
            more = sp.value_load(over[0:1, 0:1], min_val=0, max_val=1)
            with sp.If(more > 0):
                with sp.Fori(1, ROUNDS) as r:
                    with sp.Fori(0, NE // 2) as it:
                        expert_pair(it, r)
                for w in range(3):
                    sp.wait_ge(S(used[w]), ROUNDS * NE)
            for n, _task in enumerate(UNITS2):
                if n < STREAM:
                    sp.wait_ge(S(used[n % 3]), NE - 1 + n // 3)
                else:
                    wait_used(sp, UNITS2[n - STREAM])
                s = n % STREAM
                sp.dma_start(ring[:, s, :], a["units2"][n]).then_inc(S(f"unit_landed{s}"), 16)
            for i in range(2 * TT):
                t, cut = i // 2, slice(512 * (i % 2), 512 * (i % 2) + 512)
                sp.wait_ge(S("out_ready"), i + 1)
                sp.dma_start(out.rearrange("o (t p) d -> p (o t) d", p=P)[:, t, cut], tok(10)[:, t, cut]
                             ).then_inc(S("out_stored"), 16)
            sp.wait_ge(S("out_stored"), 16 * 2 * TT)

        @block.gpsimd
        def _(pool):
            g = nc.gpsimd
            pool.dma_start(w_flr[:], a["w_flr"]).then_inc(S("small_landed"), 16)
            pool.dma_start(slab[0:RANK, 10, 0:512], a["w_gate_up"]).then_inc(S("small_landed"), 16)
            pool.dma_start(rows[:, 0, :], a["b_v"].partition_broadcast(P)).then_inc(S("small_landed"), 16)
            pool.dma_start(rows[:, 1, :], a["b_out"].partition_broadcast(P)).then_inc(S("small_landed"), 16)
            pool.dma_start(rows[:, 2, :], a["ln1_g"].partition_broadcast(P)).then_inc(S("small_landed"), 16)
            pool.dma_start(w_route[:], a["w_route"]).then_inc(S("small_landed"), 16)
            pool.dma_start(b_route[:], a["b_route"].partition_broadcast(P)).then_inc(S("small_landed"), 16)
            g.memset(ident[:], 0.0).then_inc(S("consts_begun"), 1)
            g.memset(alphas[:], 0.0).then_inc(S("consts_begun"), 1)
            g.memset(before[:], 1.0).then_inc(S("consts_begun"), 1)
            g.memset(stack[:], 0.0).then_inc(S("consts_begun"), 1)
            g.memset(slab[:, 10, 1024:2048], 1.0).then_inc(S("consts_begun"), 1)
            g.iota(slots_i[:].rearrange("p (a b) -> p a b", a=4), pattern=[[0, 4], [1, CAP]], base=0,
                   channel_multiplier=0).then_inc(S("consts_begun"), 1)
            g.iota(numbers_i[:], pattern=[[1, NE]], base=0, channel_multiplier=0).then_inc(S("consts_begun"), 1)
            pool.wait_ge(S("consts_begun"), 7)
            for j in range(4):
                if j:
                    pool.wait_ge(S("stacked"), j)
                g.affine_select(out=stack[:], in_=stack[:], compare_op=ALU.not_equal, fill=1.0, base=-CAP * j,
                                pattern=[[-1, CAP]], channel_multiplier=1).then_inc(S("stacked"), 1)
            g.memset(slab[:, 10, 1024:2048:CHUNK], 0.0).then_inc(S("consts_ready"), 1)
            g.affine_select(out=ident[:], in_=ident[:], compare_op=ALU.not_equal, fill=1.0, base=0,
                            pattern=[[-1, P]], channel_multiplier=1).then_inc(S("consts_ready"), 1)
            g.affine_select(out=alphas[:], in_=alphas[:], compare_op=ALU.not_equal, fill=ALPHA, base=0,
                            pattern=[[-1, P]], channel_multiplier=1).then_inc(S("consts_ready"), 1)
            g.affine_select(out=before[:], in_=before[:], compare_op=ALU.is_gt, fill=0.0, base=0,
                            pattern=[[1, P]], channel_multiplier=-1).then_inc(S("consts_ready"), 1)
            g.tensor_copy(slots[:], slots_i[:]).then_inc(S("consts_ready"), 1)
            g.tensor_copy(numbers[:], numbers_i[:]).then_inc(S("consts_ready"), 1)
            g.memset(ones[:], 1.0).then_inc(S("consts_ready"), 1)
            g.memset(eps_ln[:], 1e-5).then_inc(S("consts_ready"), 1)
            g.memset(eps_rms[:], 1e-6).then_inc(S("consts_ready"), 1)
            g.memset(meta[:], -1.0).then_inc(S("consts_ready"), 1)
            pool.wait_ge(S("consts_ready"), CONSTS)

            def weights_low(part, *names):
                for name in names:
                    for h, (w, high) in enumerate(halves(part, name)):
                        pool.wait_ge(S("high_ready"), split_count(part, name) + h + 1)
                        g.tensor_tensor(r32(w), w, r32(high), ALU.subtract).then_inc(S("low_ready"), 1)

            weights_low(0, *SPLIT[0])
            pool.wait_ge(S("x1_ready"), TT)
            pool.dma_start(rows[:, 1, :], a["ln2_g"].partition_broadcast(P)).then_inc(S("ln2_landed"), 16)
            pool.dma_start(rows[:, 2, :], a["ln2_b"].partition_broadcast(P)).then_inc(S("ln2_landed"), 16)
            pool.wait_ge(S("gate_full"), 3)
            pool.wait_ge(S("up_full"), 3)
            pool.dma_start(slab[:, 6, 0:DC * 136], a["w_kiwi"]).then_inc(S("small2_landed"), 16)
            pool.dma_start(slab[0:NB, 9, 0:NH], a["rel_bias"]).then_inc(S("small2_landed"), 16)
            pool.dma_start(slab[0:NB, 9, 16:16 + 511], a["buckets"]).then_inc(S("small2_landed"), 16)
            pool.wait_ge(S("high_ready"), KIWI_COUNT + 1)
            kiwi = slab[:, 6, 0:DC * 136]
            g.tensor_tensor(r32(kiwi), kiwi, r32(kiwi_high), ALU.subtract).then_inc(S("low_ready"), 1)
            weights_low(1, "lx1", "lx3")
            pool.wait_ge(S("x2_ready"), TT)
            pool.dma_start(rows[:, 2, 0:512], a["pT"]).then_inc(S("p_landed"), 16)
            weights_low(1, "lg_1", "lg_3", "vv", "qi1", "qq1")
            for t in range(TT):
                pool.wait_ge(S("score_ready"), t + 1)
                g.affine_select(out=work[:, t, 0:P * (t + 1)], in_=score[:, t, 0:P * (t + 1)],
                                compare_op=ALU.is_ge, fill=FILL, base=P * t, pattern=[[-1, P * (t + 1)]],
                                channel_multiplier=1).then_inc(S("work_ready"), 1)
            for t, names in enumerate((("qq3", "gc1", "gc3"), ("ya1", "ya3"))):
                weights_low(1, *names)
                pool.wait_ge(S("hide_made"), t + 1)
                g.affine_select(out=score[:, t, 0:P * (t + 1)], in_=score[:, t, 0:P * (t + 1)],
                                compare_op=ALU.is_ge, fill=HIDE, base=P * t, pattern=[[-1, P * (t + 1)]],
                                channel_multiplier=1).then_inc(S("hide_ready"), 1)
            weights_low(1, *SPLIT[1][SPLIT[1].index("gd1"):])

        @block.tensor
        def _(pe):
            mm = nc.tensor.matmul
            units = [0, 0]

            def unit(part=0, cols_=512):
                name = UNITS[part][units[part]]
                s = units[part] % STREAM
                units[part] += 1
                w = ring[:, s, :].rearrange("p (c n) -> p c n", n=cols_)
                if name not in SPLIT[part]:
                    wait_landed(pe, part, name)
                    return w
                high = ring[:, STREAM + SPLIT[part].index(name) % 2, :].rearrange("p (c n) -> p c n", n=cols_)
                return high, w, split_count(part, name)

            def products(out_, w, x, swap, wcol, xcol, half_, start=True, stop=True,
                         arrive=None):
                def one(wp, xp, first, last):
                    l, r = (xp, wp) if swap else (wp, xp)
                    return mm(out_, l, r, start=start and first, stop=stop and last)

                if not isinstance(w, tuple):
                    for c in range(DC):
                        ins = one(w[:, c, wcol], x[:, c, xcol], c == 0, c == DC - 1)
                    return ins
                high, low, count = w
                for c in range(DC):
                    if arrive and c in arrive:
                        arrive[c]()
                    if half_ is not None and c == 0:
                        pe.wait_ge(S("high_ready"), count + half_ + 1)
                    elif half_ is None and c % 4 == 0:
                        pe.wait_ge(S("high_ready"), count + c // 4 + 1)
                    one(r32(high[:, c, wcol]), r32(x[0][:, c, xcol]), c == 0, False)
                    one(r32(high[:, c, wcol]), r32(x[1][:, c, xcol]), False, False)
                for c in range(DC):
                    if half_ is not None and c == 0:
                        pe.wait_ge(S("low_ready"), count + half_ + 1)
                    elif half_ is None and c % 4 == 0:
                        pe.wait_ge(S("low_ready"), count + c // 4 + 1)
                    ins = one(r32(low[:, c, wcol]), r32(x[0][:, c, xcol]), False, c == DC - 1)
                return ins

            def chan_major(w, x, tasks, arrive=None):
                for i, task in enumerate(tasks):
                    o = take_bank(task)
                    for m in range(2):
                        f = P * (2 * i + m)
                        last = products(o[:, T * m:T * m + T], w, x, False, slice(f, f + P), slice(0, T), i,
                                        arrive=None if i + m else arrive)
                    full(last, task)

            def token_major(w, x, tasks):
                for t, task in enumerate(tasks):
                    o = take_bank(task)
                    full(products(o[:], w, x, True, slice(0, 512), slice(P * t, P * t + P), None), task)

            def tile_by_tile(ws, x, pre, arrive=None):
                for t in range(TT):
                    for u, w in enumerate(ws):
                        o = take_bank(f"{pre}{u}_{t}")
                        last = products(o[:], w, x, True, slice(0, 512), slice(P * t, P * t + P), None,
                                        arrive=None if t + u else arrive)
                        full(last, f"{pre}{u}_{t}")

            def as_counted(name):
                return {2 * j: lambda j=j: pe.wait_ge(S(name), j + 1) for j in range(4)}

            def as_turned(x):
                return {4 * k: lambda k=k: wait_read(pe, f"{x}t{k}", f"{x}t{2 + k}") for k in range(2)}

            def turn(src, tasks, ready, done=0, tiles=(0, 1)):
                for t in tiles:
                    pe.wait_ge(S(ready), done + t + 1)
                    for k in range(2):
                        o = take_bank(tasks[2 * t + k])
                        for i in range(4):
                            c = 4 * k + i
                            last = nc.tensor.transpose(o[:, P * i:P * i + P], src[:, t, P * c:P * c + P], ident[:])
                        full(last, tasks[2 * t + k])

            xT = chan(0)
            pe.wait_ge(S("xt_landed"), 16)
            pe.wait_ge(S("first_half_landed"), 16)
            w = ring[:, 0, :].rearrange("p (c n) -> p c n", c=DC)
            chan_major(w, xT, ["g0"])
            w = unit()[:, :, 256:512]
            chan_major(w, xT, ["g1"])
            xTs = xt_parts
            pe.wait_ge(S("xt_high"), 1)
            pe.wait_ge(S("xt_low"), 1)
            chan_major(unit(), xTs, ["a0", "a1"])
            chan_major(unit(), xTs, ["g2", "g3"])
            chan_major(unit(), xTs, ["a2", "a3"])
            chan_major(unit(), xTs, ["k0", "k1"])
            pe.wait_ge(S("small_landed"), 16 * SMALL_LOADS)
            o = take_bank("fl")
            for c in range(DC):
                last = mm(o[0:RANK, 0:T], w_flr[:, c, :], xT[:, c, :], start=c == 0, stop=c == DC - 1)
            full(last, "fl")
            pe.wait_ge(S("small_landed"), 16 * SMALL_LOADS)
            wait_read(pe, "fl")
            for j in range(2):
                o = take_bank(f"z{j}")
                for m in range(2):
                    f = P * (2 * j + m)
                    last = mm(o[:, T * m:T * m + T], slab[0:RANK, 10, f:f + P], slab[0:RANK, 10, 512:512 + T],
                              start=True, stop=True)
                full(last, f"z{j}")
            token_major(unit(), xTs, ["v0_0", "v0_1"])
            token_major(unit(), xTs, ["v1_0", "v1_1"])
            chan_major(unit(), xTs, ["q0", "q1"])
            chan_major(unit(), xTs, ["r0", "r1"])
            chan_major(unit(), xTs, ["r2", "r3"])
            chan_major(unit(), xTs, ["ga0", "ga1"])
            chan_major(unit(), xTs, ["ga2", "ga3"])
            pe.wait_ge(S("consts_ready"), CONSTS)
            o = take_bank("csum")
            for c in range(DC):
                if c % 4 == 0:
                    pe.wait_ge(S("conv_tap"), 4 * CONV_W * (c // 4 + 1))
                last = mm(o[:, 0:T], ones[:], chan(3)[:, c, :], start=c == 0, stop=c == DC - 1)
            full(last, "csum")
            pe.wait_ge(S("consts_ready"), CONSTS)
            pe.wait_ge(S("kdec_ready"), 1)
            for t in range(TT):
                o = take_bank(f"kdt{t}")
                for h in range(H1):
                    last = nc.tensor.transpose(o[:, P * h:P * h + P], half(5, 0)[:, h, P * t:P * t + P], ident[:])
                full(last, f"kdt{t}")
            wait_read(pe, "kdt0", "kdt1", "v0_0", "v0_1", "v1_0", "v1_1")
            for n in range(NCH):
                b = CHUNK * (n % 2)
                for hp in range(2):
                    task = f"kv{2 * n + hp}"
                    o = take_bank(task)
                    for m in range(2):
                        h = 2 * hp + m
                        last = mm(o[:, HV * m:HV * m + HV],
                                  slab[b:b + CHUNK, 5, 1024 + 512 * (n // 2) + P * h:1024 + 512 * (n // 2) + P * h + P],
                                  tok(6)[b:b + CHUNK, n // 2, HV * h:HV * h + HV], start=True, stop=True)
                    full(last, task)
            chan_major(unit(), xTs, ["gb0", "gb1"])
            o = take_bank("csq")
            pe.wait_ge(S("csq_ready"), 1)
            for c in range(DC):
                last = mm(o[:, 0:T], ones[:], chan(2)[:, c, :], start=c == 0, stop=c == DC - 1)
            full(last, "csq")
            wait_read(pe, "q0", "q1")
            wait_read(pe, *[f"kv{i}" for i in range(8)])
            for h in range(H1):
                o = take_bank(f"o{h}")
                for m in range(2):
                    for n in range(NCH):
                        st = states(n, h)[:, P * m:P * m + P]
                        last = mm(o[:, T * m + CHUNK * n:T * m + CHUNK * n + CHUNK], st,
                                  half(7, 0)[:, h, CHUNK * n:CHUNK * n + CHUNK], start=True, stop=True)
                full(last, f"o{h}")
            chan_major(unit(), xTs, ["gb2", "gb3"])
            for j in range(2):
                pe.wait_ge(S("osq_ready"), 2 * j + 2)
                o = take_bank(f"osum{j}")
                for m in range(2):
                    h = 2 * j + m
                    for k in range(2):
                        last = mm(o[:, T * m:T * m + T], ones[:], chan(5)[:, 2 * h + k, :], start=k == 0, stop=k == 1)
                full(last, f"osum{j}")
            pe.wait_ge(S("conv_low"), 1)
            chan_major(unit(), conv_parts, ["yc0", "yc1"])
            chan_major(unit(), conv_parts, ["yc2", "yc3"])
            pe.wait_ge(S("gla_low"), 1)
            chan_major(unit(), gla_parts, ["yg0", "yg1"])
            chan_major(unit(), gla_parts, ["yg2", "yg3"])
            tile_by_tile([unit(), unit()], merged_parts, "mix", arrive=as_counted("merged_low"))
            pe.wait_ge(S("small_landed"), 16 * SMALL_LOADS)
            for t in range(TT):
                turn(tok(0), [f"x1t{j}" for j in range(4)], "x1_ready", tiles=(t,))
                wait_read(pe, f"x1t{2 * t}", f"x1t{2 * t + 1}")
                if t == 0:
                    o = take_bank("lg")
                for c in range(DC):
                    last = mm(o[:, 128 * t:128 * t + 72], chan(1)[:, c, P * t:P * t + P], w_route[:, c, :],
                              start=c == 0, stop=c == DC - 1)
            full(last, "lg")
            wait_read(pe, *TASKS1[-8:-4])
            pe.wait_ge(S("consts_ready"), CONSTS)
            for t in range(TT):
                for hf in range(2):
                    mm(acc[t][hf][:], alphas[:], tok(0)[:, t, 512 * hf:512 * hf + 512], start=True, stop=False)
            pe.wait_ge(S("mask_ready"), 1)
            pe.wait_ge(S("consts_ready"), CONSTS)
            o = take_bank("pos")
            mm(o[:, 0:64], before[:], mask[:, 0, :], start=True, stop=True)
            mm(o[:, 64:128], before[:], mask[:, 1, :], start=True, stop=False)
            mm(o[:, 64:128], ones[:], mask[:, 0, :], start=False, stop=True)
            mm(o[:, 128:192], ones[:], mask[:, 0, :], start=True, stop=False)
            full(mm(o[:, 128:192], ones[:], mask[:, 1, :], start=False, stop=True), "pos")
            wait_read(pe, "pos", "lg")
            pe.wait_ge(S("x1_ready"), TT)

            def gather(f, par, r):
                pe.wait_ge(S("sel_ready"), (r * META + f + 1) * TT)
                for c in range(DC):
                    for t in range(TT):
                        last = mm(gather_bank[:, CAP * c:CAP * c + CAP], tok(0)[:, t, c::DC], sel[:, par, t, :],
                                  start=t == 0, stop=t == 1)
                last.then_inc(S("xg_full"), 1)

            def combine(par, ends=False, again=False):
                for t in range(TT):
                    for hf in range(2):
                        last = mm(acc[t][hf][:], spread[:, par, P * t:P * t + P],
                                  y_sb[:, par, 512 * hf:512 * hf + 512], start=False, stop=ends,
                                  skip_group_check=again)
                last.then_inc(S("combined"), 1)

            def expert(e, q, it, r, in_spare=False):
                n = r * NE + e
                for w, (b, name) in enumerate(((gate_bank, "gate_full"), (up_bank, "up_full"))):
                    wt = ring[:, expert_slot(q, w), :]
                    if in_spare:
                        pe.wait_ge(S(("spare_w1_landed", "spare_w3_landed")[w]), 16)
                        wt = spare[w]
                    else:
                        pe.wait_ge(S(f"expert_landed{3 * q + w}"), 16 if isinstance(e, int) and e < 2
                                   else 16 * (r * (NE // 2) + it + q))
                    if w == 0:
                        pe.wait_ge(S("xg_copied"), r * (NE + 1) + e + 1)
                    else:
                        pe.wait_ge(S("y1_copied"), r * (NE + 1) + e + 1)
                    wt = wt.rearrange("p (c n) -> p c n", c=DC)
                    for c in range(DC):
                        j = c % 4
                        last = mm(b[CAP * j:CAP * j + CAP, :], xg[:, c, :], wt[:, c, :],
                                  start=c < 4, stop=c >= 4, tile_position=(0, CAP * j))
                    last.then_inc(S(name), 1)
                gather(e + 1, 1 - q, r)
                pe.wait_ge(S("selw_ready"), (r * META + e + 1) * TT)
                pe.wait_ge(S("y0_copied"), r * (NE + 1) + e + 1)
                for t in range(TT):
                    last = nc.tensor.transpose(y_bank[:, P * t:P * t + P], selw[:, q, t, :], ident[:])
                last.then_inc(S("spread_full"), 1)
                pe.wait_ge(S("g_copied"), n + 1)
                pe.wait_ge(S("u_copied"), n + 1)
                for src, o in ((g_sb, 0), (u_sb, 128)):
                    for m in range(4):
                        last = mm(gate_bank[:, o + CAP * m:o + CAP * m + CAP], src[:, m::4], stack[:],
                                  start=True, stop=True)
                last.then_inc(S("hidden_full"), 1)
                pe.wait_ge(S("spread_copied"), r * (NE + 1) + e + 1)
                if not (isinstance(e, int) and e == 0):
                    combine(1 - q, again=not isinstance(r, int))
                pe.wait_ge(S("h_ready"), n + 1)
                pe.wait_ge(S(f"expert_landed{3 * q + 2}"), 16 * (r * (NE // 2) + it + 1))
                wt = ring[:, expert_slot(q, 2), :].rearrange("p (c n) -> p c n", c=4)
                pe.wait_ge(S("spread_copied"), r * (NE + 1) + e + 2)
                for hf, (b, name) in enumerate(((y_bank, "y0_full"), (up_bank, "y1_full"))):
                    for m in range(4):
                        last = mm(b[CAP * m:CAP * m + CAP, :], h_sb[:, m, :],
                                  wt[:, m, 512 * hf:512 * hf + 512], start=True, stop=True,
                                  tile_position=(0, CAP * m))
                    last.then_inc(S(name), 1)

            def last_combine(r):
                pe.wait_ge(S("y0_copied"), (r + 1) * (NE + 1))
                pe.wait_ge(S("y1_copied"), (r + 1) * (NE + 1))
                pe.wait_ge(S("spread_copied"), (r + 1) * (NE + 1))
                combine(1, ends=True, again=not isinstance(r, int))

            pe.wait_ge(S("consts_ready"), CONSTS)
            gather(0, 0, 0)
            for e in range(4):
                expert(e, e % 2, e // 2, 0, in_spare=e == 2)
            with pe.Fori(2, NE // 2) as it:
                for q in range(2):
                    expert(2 * it + q, q, it, 0)
            last_combine(0)
            more = pe.value_load(over[0:1, 0:1], min_val=0, max_val=1)
            with pe.If(more > 0):
                with pe.Fori(1, ROUNDS) as r:
                    pe.wait_ge(S("xg_copied"), r * (NE + 1))
                    gather(0, 0, r)
                    with pe.Fori(0, NE // 2) as it:
                        for q in range(2):
                            expert(2 * it + q, q, it, r)
                    last_combine(r)
            turn(tok(1), [f"x2t{j}" for j in range(4)], "xn_ready")
            xn = xn_parts
            pe.wait_ge(S("small2_landed"), 48)
            kiwi_parts = (kiwi_high.rearrange("p (c n) -> p c n", c=DC),
                          slab[:, 6, 0:DC * 136].rearrange("p (c n) -> p c n", c=DC), KIWI_COUNT)
            o = take_bank("kiwi_k")
            full(products(o[:, 0:T], kiwi_parts, xn, False, slice(0, P), slice(0, T), 0,
                          arrive=as_turned("x2")), "kiwi_k")
            o = take_bank("kiwi_w")
            for t in range(TT):
                last = products(o[:, 8 * t:8 * t + 8], kiwi_parts, xn, True, slice(P, P + 8), slice(P * t, P * t + P), 0)
            full(last, "kiwi_w")
            o = take_bank("relb")
            full(mm(o[0:NH, 0:511], slab[0:NB, 9, 0:NH], slab[0:NB, 9, 16:16 + 511], start=True, stop=True), "relb")
            chan_major(unit(1), xn, ["lx0", "lx1"])
            chan_major(unit(1), xn, ["lx2", "lx3"])
            chan_major(unit(1), xn, ["lg_0", "lg_1"])
            chan_major(unit(1), xn, ["lg_2", "lg_3"])
            w = unit(1)
            chan_major(w, xn, ["kk"])
            o = take_bank("vv")
            for t in range(TT):
                last = products(o[:, T * t:T * t + T], w, xn, True, slice(256, 512), slice(P * t, P * t + P), 1)
            full(last, "vv")
            chan_major(unit(1), xn, ["qi0", "qi1"])
            wait_read(pe, "kiwi_k", "qi0", "qi1")
            for t in range(TT):
                n = P * (t + 1)
                for j in range(4):
                    o = take_bank(f"dots{t}_{j}")
                    for m in range(2):
                        h = indexer_head(j, m)
                        b = ID * (h % 2)
                        last = mm(o[:, T * m:T * m + n], qiT[b:b + ID, h // 2, P * t:P * t + P], kiT[b:b + ID, 0:n],
                                  start=True, stop=True)
                    full(last, f"dots{t}_{j}")
            w = unit(1, 128)
            for x, pre in ((0, "lr"), (1, "li")):
                for j in range(4):
                    o = take_bank(f"{pre}{j}")
                    for m in range(2):
                        c = 2 * j + m
                        if x == 0:
                            pe.wait_ge(S("lru_tap"), 2 * LRU_W * (j + 1))
                        last = mm(o[:, T * m:T * m + T], w[:, 8 * x + c, :], chan(2)[:, c, :], start=True, stop=True)
                    full(last, f"{pre}{j}")
            o = take_bank("ksum")
            pe.wait_ge(S("k_sq_ready"), 1)
            full(mm(o[:, 0:512], ones[:], k_sq, start=True, stop=True), "ksum")
            chan_major(unit(1), xn, ["qq0", "qq1"])
            chan_major(unit(1), xn, ["qq2", "qq3"])
            chan_major(unit(1), xn, ["gc0", "gc1"])
            for j in range(4):
                o = take_bank(f"qsum{j}")
                pe.wait_ge(S("q_sq_ready"), j + 1)
                full(mm(o[:, 0:512], ones[:], slab[:, 6, 512 * j:512 * j + 512], start=True, stop=True), f"qsum{j}")
            chan_major(unit(1), xn, ["gc2", "gc3"])
            pe.wait_ge(S("lru_low"), 1)
            chan_major(unit(1), lru_parts, ["ya0", "ya1"])
            pe.wait_ge(S("k_ready"), 1)
            pe.wait_ge(S("q_ready"), 4)
            for t in range(TT):
                n = P * (t + 1)
                for j in range(4):
                    o = take_bank(f"log{t}_{j}")
                    for m in range(2):
                        h = 2 * j + m
                        last = mm(o[:, T * m:T * m + n], chan(9)[:, h, P * t:P * t + P], kT[:, h // QPK, 0:n],
                                  start=True, stop=True)
                    full(last, f"log{t}_{j}")
            chan_major(unit(1), lru_parts, ["ya2", "ya3"])
            for t in range(TT):
                pe.wait_ge(S("probs_ready"), t + 1)
                for s in range(t + 1):
                    for k in range(2):
                        o = take_bank(f"pt{t}_{s}_{k}")
                        for m in range(4):
                            last = nc.tensor.transpose(o[:, P * m:P * m + P], lgt[:, 4 * k + m, P * s:P * s + P],
                                                       ident[:])
                        full(last, f"pt{t}_{s}_{k}")
                wait_read(pe, *[f"pt{t}_{s}_{k}" for s in range(t + 1) for k in range(2)])
                for k in range(2):
                    o = take_bank(f"pv{t}_{k}")
                    for s in range(t + 1):
                        last = mm(o[:, 0:512], v2[:, s, HD * k:HD * k + HD],
                                  prob_t[:, s, 4 * k:4 * k + 4, :].rearrange("p h t -> p (h t)"),
                                  start=s == 0, stop=s == t)
                    full(last, f"pv{t}_{k}")
                chan_major(unit(1), xn, [f"gd{2 * t}", f"gd{2 * t + 1}"])
            pe.wait_ge(S("att_low"), 2)
            chan_major(unit(1), att_parts, ["yb0", "yb1"])
            chan_major(unit(1), att_parts, ["yb2", "yb3"])
            tile_by_tile([unit(1), unit(1)], merged2_parts, "mo", arrive=as_counted("merged2_low"))
            turn(tok(4), [f"x3t{j}" for j in range(4)], "xn_ready", TT)
            for i in range(6):
                chan_major(unit(1), xn, [f"fg{i}_0", f"fg{i}_1"], arrive=None if i else as_turned("x3"))
                chan_major(unit(1), xn, [f"fu{i}_0", f"fu{i}_1"])
            for u in range(2):
                o = [take_bank(f"dn{u}_{t}") for t in range(TT)]
                for k in range(3):
                    if u == 0:
                        pe.wait_ge(S("hid_low"), 2 * k + 2)
                    w = unit(1)
                    x = [part[:, DC * k:DC * k + DC, :] for part in hid_parts]
                    for t in range(TT):
                        last = products(o[t][:], w, x, True, slice(0, 512), slice(P * t, P * t + P), None,
                                        start=k == 0, stop=k == 2)
                        if k == 2:
                            full(last, f"dn{u}_{t}")
                    if k < 2:
                        last.then_inc(S("down_used"), 1)
            pe.wait_ge(S("p_landed"), 16)
            w = unit(1, 1024)
            pT = rows[:, 2, 0:512].rearrange("p (c t) -> p c t", c=2)
            for u in range(2):
                for t in range(TT):
                    o = take_bank(f"pp{u}_{t}")
                    for c in range(2):
                        last = mm(o[:], pT[:, c, P * t:P * t + P], w[:, c, 512 * u:512 * u + 512],
                                  start=c == 0, stop=c == 1)
                    full(last, f"pp{u}_{t}")
            turn(tok(4), [f"x4t{j}" for j in range(4)], "xn_ready", 2 * TT)
            tile_by_tile([unit(1), unit(1)], xn, "pg", arrive=as_turned("x4"))

        @block.scalar
        def _(act):
            A = nc.scalar.activation

            def per_chunk(tasks, dst, func, bias=None, scale=1.0, first=0):
                for i, task in enumerate(tasks):
                    o = wait_full(act, task)
                    for m in range(2):
                        c = first + 2 * i + m
                        b = col(bias, c) if bias else 0.0
                        ins = A(dst[:, c, :], o[:, T * m:T * m + T], func, bias=b, scale=scale)
                    read(ins, task)

            def weights_high(part, *names):
                for name in names:
                    k = SPLIT[part].index(name)
                    wait_landed(act, part, name)
                    if k >= 2:
                        wait_used(act, SPLIT[part][k - 2])
                    for w, high in halves(part, name):
                        A(r32(high), w, ACT.Copy).then_inc(S("high_ready"), 1)

            act.wait_ge(S("xt_landed"), 16)
            A(r32(slab[:, 8, :]), slab[:, 0, :], ACT.Copy).then_inc(S("xt_high"), 1)
            act.wait_ge(S("cols_landed"), 16)
            per_chunk(["g0"], chan(1), ACT.Sigmoid, "b_conv_g")
            weights_high(0, "a1")
            per_chunk(["g1"], chan(1), ACT.Sigmoid, "b_conv_g", first=2)
            weights_high(0, "g3", "a3")
            per_chunk(["g2", "g3"], chan(1), ACT.Sigmoid, "b_conv_g", first=4)
            weights_high(0, "k1", "v0_1")
            per_chunk(["k0", "k1"], half(4, 0), ACT.Identity, "b_k")
            o = wait_full(act, "fl")
            read(A(slab[0:RANK, 10, 512:512 + T], o[0:RANK, 0:T], ACT.Identity,
                   bias=cols[0:RANK, COLS["b_flr"]:COLS["b_flr"] + 1]), "fl")
            weights_high(0, "v1_1")
            per_chunk(["z0", "z1"], half(5, 0), ACT.Identity, "b_gate")
            la = half(7, 1)
            act.wait_ge(S("negabs_ready"), 1)
            A(la, la, ACT.Exp).then_inc(S("gate_exp"), 1)
            act.wait_ge(S("gate_exp"), 1)
            A(la, la, ACT.Ln, bias=1.0).then_inc(S("gate_ln"), 1)
            weights_high(0, "q1", "r1")
            act.wait_ge(S("toend_ready"), 1)
            A(la, la, ACT.Exp, scale=1.0 / TAU).then_inc(S("decay_ready"), 1)
            A(small[:, 0:16].rearrange("p (h n a) -> p h n a", h=H1, a=1), half(4, 1).rearrange("p h (n t) -> p h n t", t=CHUNK)[:, :, :, CHUNK - 1:CHUNK],
              ACT.Exp, scale=1.0 / TAU).then_inc(S("decay_ready"), 1)
            per_chunk(["q0", "q1"], half(7, 0), ACT.Identity, "b_q")
            weights_high(0, "r3")
            wait_full(act, "fl")
            per_chunk(["r0", "r1"], chan(0), ACT.Silu, "b_r")
            weights_high(0, "ga1")
            per_chunk(["r2", "r3"], chan(0), ACT.Silu, "b_r", first=4)
            weights_high(0, "ga3")
            wait_read(act, "a0", "a1", "a2", "a3")
            per_chunk(["ga0", "ga1"], chan(1), ACT.Sigmoid, "b_ga")
            weights_high(0, "gb1")
            per_chunk(["ga2", "ga3"], chan(1), ACT.Sigmoid, "b_ga", first=4)
            weights_high(0, "gb3")
            act.wait_ge(S("centered"), DC)
            A(chan(2), chan(3), ACT.Square).then_inc(S("csq_ready"), 1)
            wait_full(act, "kv7")
            per_chunk(["gb0", "gb1"], chan(6), ACT.Sigmoid, "b_gb")
            act.wait_ge(S("consts_ready"), CONSTS)
            o = wait_full(act, "csq")
            read(A(conv_root, o[:, 0:T], ACT.Sqrt, bias=eps_ln[:], scale=1.0 / D), "csq")
            weights_high(0, "yc1")
            act.wait_ge(S("conv_normed"), DC)
            for h in range(H1):
                if h == 2:
                    wait_full(act, "o3")
                o = wait_full(act, f"o{h}")
                dst = chan(10)[:, 2 * h:2 * h + 2, :].rearrange("p a t -> p (a t)")
                read(A(dst, o[:, 0:512], ACT.Copy, scale=HK ** -0.5), f"o{h}")
                wait_read(act, f"o{h}")
                A(chan(5)[:, 2 * h:2 * h + 2, :].rearrange("p a t -> p (a t)"), dst, ACT.Square
                  ).then_inc(S("osq_ready"), 1)
            for c in range(DC):
                act.wait_ge(S("conv_normed"), c + 1)
                ins = A(chan(3)[:, c, :], chan(3)[:, c, :], ACT.Silu, bias=col("cln_b", c), scale=col("cln_g", c))
            ins.then_inc(S("conv_act_ready"), 1)
            act.wait_ge(S("conv_act_ready"), 1)
            A(r32(slab[:, 4, :]), slab[:, 3, :], ACT.Copy).then_inc(S("conv_high"), 1)
            per_chunk(["gb2", "gb3"], chan(6), ACT.Sigmoid, "b_gb", first=4)
            weights_high(0, "yc3")
            for j in range(2):
                o = wait_full(act, f"osum{j}")
                read(A(slab[:, 7, 1024 + 512 * j:1024 + 512 * j + 512], o[:, 0:512], ACT.Sqrt,
                       bias=eps_rms[:], scale=1.0 / HV), f"osum{j}")
            weights_high(0, "yg1")
            act.wait_ge(S("gla_ready"), 1)
            A(r32(slab[:, 5, :]), slab[:, 10, :], ACT.Copy).then_inc(S("gla_high"), 1)
            weights_high(0, "yg3", "mix0_1")
            wait_full(act, "gb3")
            for j in range(4):
                act.wait_ge(S("merged_ready"), j + 1)
                A(r32(slab[:, 8, 512 * j:512 * j + 512]), slab[:, 1, 512 * j:512 * j + 512], ACT.Copy
                  ).then_inc(S("merged_high"), 1)
            weights_high(0, "mix1_1")
            for t in range(TT):
                act.wait_ge(S("ln_stats"), t + 1)
                A(small[:, 20 + t:21 + t], small[:, 17 + 2 * t:18 + 2 * t], ACT.Sqrt, bias=eps_ln[:]
                  ).then_inc(S("ln_std"), 1)
            for j in range(4):
                t, k = divmod(j, 2)
                o = wait_full(act, f"x1t{j}")
                read(A(chan(1)[:, 4 * k:4 * k + 4, P * t:P * t + P], o[:].rearrange("p (c n) -> p c n", c=4), ACT.Copy),
                     f"x1t{j}")
            act.wait_ge(S("gtop_ready"), TT)
            for t in range(TT):
                A(e_exp[:, t, :], logit[:, t, 0:NG], ACT.Exp, bias=small[:, 30 + t:31 + t],
                  accum_out=small[:, 32 + t:33 + t]).then_inc(S("gsum_ready"), 1)
            act.wait_ge(S("ediff_ready"), 1)
            A(small[:, 36:38], small[:, 34:36], ACT.Exp).then_inc(S("ratio_ready"), 1)

            def take_xg(n):
                act.wait_ge(S("xg_full"), n)
                A(slab[:, 1, 0:DC * CAP], gather_bank[:, 0:DC * CAP], ACT.Copy).then_inc(S("xg_copied"), 1)

            def expert(e, q, r):
                n = r * NE + e
                act.wait_ge(S("gate_full"), n + 1)
                A(g_sb, gate_bank[:], ACT.Copy).then_inc(S("g_copied"), 1)
                take_xg(r * (NE + 1) + e + 2)
                act.wait_ge(S("hidden_full"), n + 1)
                A(slab[:, 1, 1536:1664], gate_bank[:, 0:128], ACT.Silu).then_inc(S("silu_ready"), 1)
                act.wait_ge(S("y0_full"), n + 1)
                A(y_sb[:, q, 0:512], y_bank[:], ACT.Copy).then_inc(S("y0_copied"), 1)

            wait_read(act, "lg")
            wait_read(act, "pos")
            act.wait_ge(S("meta_ready"), 1)
            act.wait_ge(S("zeros_ready"), 1)
            A(y_sb[:, 1, 0:512], zeros, ACT.Copy).then_inc(S("y0_copied"), 1)
            take_xg(1)
            with act.Fori(0, NE // 2) as it:
                for q in range(2):
                    expert(2 * it + q, q, 0)
            more = act.value_load(over[0:1, 0:1], min_val=0, max_val=1)
            with act.If(more > 0):
                with act.Fori(1, ROUNDS) as r:
                    act.wait_ge(S("combined"), r * (NE + 1) - 1)
                    A(y_sb[:, 1, 0:512], zeros, ACT.Copy).then_inc(S("y0_copied"), 1)
                    take_xg(r * (NE + 1) + 1)
                    with act.Fori(0, NE // 2) as it:
                        for q in range(2):
                            expert(2 * it + q, q, r)
                act.wait_ge(S("y1_full"), ROUNDS * NE)
            act.wait_ge(S("up_full"), NE)
            act.wait_ge(S("y1_full"), NE)
            act.wait_ge(S("small2_landed"), 48)
            A(r32(kiwi_high), slab[:, 6, 0:DC * 136], ACT.Copy).then_inc(S("high_ready"), 1)
            weights_high(1, "lx1")
            for t in range(TT):
                act.wait_ge(S("ln_stats"), TT + t + 1)
                A(small[:, 46 + t:47 + t], small[:, 43 + 2 * t:44 + 2 * t], ACT.Sqrt, bias=eps_ln[:]
                  ).then_inc(S("ln_std"), 1)

            def rms_tile(t, dst, done, at):
                A(tok(dst)[:, t, :], tok(10)[:, t, :], ACT.Square, accum_out=small[:, at + t:at + t + 1]
                  ).then_inc(S("rms_sum"), 1)
                act.wait_ge(S("rms_sum"), done + t + 1)
                A(small[:, at + 2 + t:at + 3 + t], small[:, at + t:at + t + 1], ACT.Sqrt, bias=eps_rms[:],
                  scale=1.0 / D).then_inc(S("rms_root"), 1)
                act.wait_ge(S("rms_inverse"), done + t + 1)
                A(tok(dst)[:, t, :], tok(10)[:, t, :], ACT.Copy, scale=small[:, at + 2 + t:at + 3 + t]
                  ).then_inc(S("xn_ready"), 1)

            for t in range(TT):
                act.wait_ge(S("x2_ready"), t + 1)
                rms_tile(t, 1, 0, 50)

            def take_turned(tasks, gain):
                for i, task in enumerate(tasks):
                    o = wait_full(act, task)
                    t, k = divmod(i, 2)
                    for m in range(4):
                        ins = A(r32(chan(0)[:, 4 * k + m, P * t:P * t + P]), o[:, P * m:P * m + P], ACT.Copy,
                                scale=col(gain, 4 * k + m))
                    ins.then_inc(S("xn_high"), 1)

            take_turned([f"x2t{j}" for j in range(4)], "mix_norm")
            act.wait_ge(S("lam_negabs"), 1)
            A(small[:, 80:88], small[:, 72:80], ACT.Exp).then_inc(S("lam_exp"), 1)
            weights_high(1, "lx3")
            o = wait_full(act, "kiwi_k")
            read(A(kiT, o[:, 0:T], ACT.Copy), "kiwi_k")
            o = wait_full(act, "kiwi_w")
            read(A(slab[:, 8, 1792:1808], o[:, 0:16], ACT.Copy, scale=IH ** -0.5), "kiwi_w")
            o = wait_full(act, "relb")
            read(A(slab[0:NH, 9, 1024:1024 + 511], o[0:NH, 0:511], ACT.Copy), "relb")
            wait_read(act, "relb")
            act.dma_start(bias_dram[:, 0:511], slab[0:NH, 9, 1024:1024 + 511]).then_inc(S("relb_stored"), 16)

            def load_bias(t):
                src = bass.AP(bias_dram.tensor, bias_dram.offset + P * t, [[1, P], [512, NH], [1, T]])
                act.dma_start(slab[:, 2, :].rearrange("p (h j) -> p h j", h=NH), src
                              ).then_inc(S("bias_landed"), 16)

            per_chunk(["lx0", "lx1"], chan(1), ACT.Copy)
            weights_high(1, "lg_1")
            per_chunk(["lx2", "lx3"], chan(1), ACT.Copy, first=4)
            weights_high(1, "lg_3")
            per_chunk(["lg_0", "lg_1"], chan(3), ACT.Gelu_apprx_tanh)
            weights_high(1, "vv")
            per_chunk(["lg_2", "lg_3"], chan(3), ACT.Gelu_apprx_tanh, first=4)
            weights_high(1, "qi1")
            o = wait_full(act, "kk")
            read(A(slab[:, 7, 0:512], o[:, 0:512], ACT.Copy), "kk")
            wait_read(act, "kk")
            A(k_sq, slab[:, 7, 0:512], ACT.Square).then_inc(S("k_sq_ready"), 1)
            o = wait_full(act, "vv")
            read(A(slab[:, 7, 512:1024], o[:, 0:512], ACT.Copy), "vv")
            weights_high(1, "qq1")
            for j in range(2):
                o = wait_full(act, f"qi{j}")
                read(A(slab[:, 7, 1024 + 512 * j:1536 + 512 * j], o[:, 0:512], ACT.Copy), f"qi{j}")
            weights_high(1, "qq3")
            act.wait_ge(S("relb_stored"), 16)
            for t in range(TT):
                n = P * (t + 1)
                for j in range(4):
                    o = wait_full(act, f"dots{t}_{j}")
                    read(A(rel[t][:, 512 * j:512 * j + 512].rearrange("p (m s) -> p m s", m=2)[:, :, 0:n],
                           o[:].rearrange("p (m s) -> p m s", m=2)[:, :, 0:n], ACT.Relu, scale=ID ** -0.5),
                         f"dots{t}_{j}")
            per_chunk([f"lr{j}" for j in range(4)], chan(4), ACT.Sigmoid, "lru_ba")
            per_chunk([f"li{j}" for j in range(4)], chan(5), ACT.Sigmoid, "lru_bx")
            wait_read(act, "lr0", "lr1", "lr2", "lr3")
            act.wait_ge(S("rate_ready"), 1)
            act.wait_ge(S("score_ready"), 1)
            for c in range(DC):
                ins = A(chan(6)[:, c, :], chan(4)[:, c, :], ACT.Tanh, scale=small[:, 112 + c:113 + c])
            ins.then_inc(S("tanh_ready"), 1)
            for c in range(DC):
                ins = A(chan(4)[:, c, :], chan(4)[:, c, :], ACT.Exp, scale=small[:, 112 + c:113 + c])
            ins.then_inc(S("a_ready"), 1)
            act.wait_ge(S("score_ready"), 2)
            for j in range(4):
                o = wait_full(act, f"qq{j}")
                read(A(slab[:, 9, 512 * j:512 * j + 512], o[:, 0:512], ACT.Copy), f"qq{j}")
                if j == 0:
                    act.wait_ge(S("ua_used"), 1)
                    load_bias(0)
                    act.wait_ge(S("mult2_ready"), 1)
                    A(slab[:, 6, :], slab[:, 6, :], ACT.Sqrt, scale=-1.0).then_inc(S("mult_ready"), 1)
                    o = wait_full(act, "ksum")
                    read(A(k_sq, o[:, 0:512], ACT.Sqrt, bias=eps_rms[:], scale=1.0 / HD), "ksum")
                if j % 2:
                    weights_high(1, ("gc1", "gc3")[j // 2])
            act.wait_ge(S("u_ready"), 1)
            for j in range(4):
                wait_read(act, f"qq{j}")
                A(slab[:, 6, 512 * j:512 * j + 512], slab[:, 9, 512 * j:512 * j + 512], ACT.Square
                  ).then_inc(S("q_sq_ready"), 1)
            act.wait_ge(S("ya_ready"), 1)
            A(r32(slab[:, 5, :]), slab[:, 1, :], ACT.Copy).then_inc(S("lru_high"), 1)
            per_chunk(["gc0", "gc1"], chan(3), ACT.Sigmoid)
            weights_high(1, "ya1")
            for j in range(4):
                o = wait_full(act, f"qsum{j}")
                read(A(slab[:, 6, 512 * j:512 * j + 512], o[:, 0:512], ACT.Sqrt, bias=eps_rms[:], scale=1.0 / HD),
                     f"qsum{j}")
            per_chunk(["gc2", "gc3"], chan(3), ACT.Sigmoid, first=4)
            weights_high(1, "ya3")
            for t in range(TT):
                n = P * (t + 1)
                act.wait_ge(S("rowmax_ready"), t + 1)
                if t == 0:
                    load_bias(1)
                for h in range(NH):
                    ins = A(lgt[:, h, 0:n], lgt[:, h, 0:n], ACT.Exp, bias=small[:, 128 + h:129 + h],
                            accum_out=small[:, 136 + h:137 + h])
                ins.then_inc(S("exp_ready"), 1)
                if t == 0:
                    weights_high(1, "gd1")
                else:
                    wait_full(act, "ya3")
                    per_chunk(["gd0", "gd1"], chan(1), ACT.Sigmoid)
                    wait_full(act, "pv0_1")
                for s in range(t + 1):
                    for k in range(2):
                        o = wait_full(act, f"pt{t}_{s}_{k}")
                        read(A(prob_t[:, s, 4 * k:4 * k + 4, :].rearrange("p h t -> p (h t)"), o[:, 0:512],
                               ACT.Copy), f"pt{t}_{s}_{k}")
                for k in range(2):
                    o = wait_full(act, f"pv{t}_{k}")
                    read(A(chan(6)[:, 4 * k:4 * k + 4, P * t:P * t + P],
                           o[:].rearrange("p (h t) -> p h t", h=4), ACT.Copy), f"pv{t}_{k}")
                if t == 0:
                    weights_high(1, "gd3")
            wait_read(act, "pv0_0", "pv0_1", "pv1_0", "pv1_1")
            for h in range(2):
                A(r32(slab[:, 9, 1024 * h:1024 * h + 1024]), slab[:, 6, 1024 * h:1024 * h + 1024], ACT.Copy
                  ).then_inc(S("att_high"), 1)
            weights_high(1, "yb1")
            per_chunk(["gd2", "gd3"], chan(1), ACT.Sigmoid, first=4)
            weights_high(1, "yb3")
            wait_full(act, "yb1")
            weights_high(1, "mo0_1")
            for j in range(4):
                act.wait_ge(S("merged2_ready"), j + 1)
                A(r32(slab[:, 7, 512 * j:512 * j + 512]), slab[:, 3, 512 * j:512 * j + 512], ACT.Copy
                  ).then_inc(S("merged2_high"), 1)
            weights_high(1, "mo1_1")
            weights_high(1, "fg0_1")
            for t in range(TT):
                wait_read(act, f"mo0_{t}", f"mo1_{t}")
                rms_tile(t, 4, TT, 54)
            take_turned([f"x3t{j}" for j in range(4)], "ffn_norm")
            weights_high(1, "fu0_1")
            down = ["dn0_1/1", "dn0_1/2", "dn0_1", "dn1_1/1", "dn1_1/2", "dn1_1"]
            for i in range(6):
                for j in range(2):
                    o = wait_full(act, f"fg{i}_{j}")
                    if i >= 2:
                        act.wait_ge(S("ffn_tap"), 4 * FFN_W * (i - 1))
                    read(A(half(4, i % 2)[:, 2 * j:2 * j + 2, :].rearrange("p a t -> p (a t)"), o[:, 0:512],
                           ACT.Copy), f"fg{i}_{j}")
                weights_high(1, f"fg{i + 1}_1" if i < 5 else down[0])
                act.wait_ge(S("ffn_tap"), 4 * FFN_W * (i + 1))
                A(half(5, i % 2), half(5, i % 2), ACT.Gelu_apprx_tanh).then_inc(S("fgelu_ready"), 1)
                weights_high(1, f"fu{i + 1}_1" if i < 5 else down[1])
                wait_read(act, f"fu{i}_0", f"fu{i}_1")
                A(r32(hT[:, 4 * i:4 * i + 4, :]), half(5, i % 2), ACT.Copy).then_inc(S("hid_high"), 1)
            weights_high(1, *down[2:])
            weights_high(1, "pg0_1", "pg1_1")
            for t in range(TT):
                wait_read(act, f"dn0_{t}", f"dn1_{t}")
                rms_tile(t, 4, 2 * TT, 62)
            take_turned([f"x4t{j}" for j in range(4)], "ple_norm")
            for t in range(TT):
                for u in range(2):
                    o = wait_full(act, f"pg{u}_{t}")
                    read(A(tok(4)[:, t, 512 * u:512 * u + 512], o[:], ACT.Sigmoid), f"pg{u}_{t}")

        @block.vector
        def _(dve):
            v = nc.vector
            stt, ts, tt = v.scalar_tensor_tensor, v.tensor_scalar, v.tensor_tensor

            def glu_input(js):
                for j in js:
                    wait_read(dve, f"g{j}")
                    o = wait_full(dve, f"a{j}")
                    for m in range(2):
                        c = 2 * j + m
                        ins = stt(chan(2)[:, c, :], o[:, T * m:T * m + T], col("b_conv_a", c), chan(1)[:, c, :],
                                  ALU.add, ALU.mult)
                    read(ins, f"a{j}")
                wait_read(dve, *[f"a{j}" for j in js])

            def causal_conv(src, dst, w, width, bias, chunks, done, base, between=None):
                n = 0
                for j in reversed(range(width)):
                    lag = width - 1 - j
                    for i, (cs, cd, cw) in enumerate(chunks):
                        wc = col(w, width * cw + j)
                        if lag == 0:
                            ins = ts(dst[:, cd, :], src[:, cs, :], wc, col(bias, cw), ALU.mult, ALU.add)
                        else:
                            dve.wait_ge(S(done), base + n - len(chunks) + 1)
                            ins = stt(dst[:, cd, lag:T], src[:, cs, 0:T - lag], wc, dst[:, cd, lag:T],
                                      ALU.mult, ALU.add)
                        n += 1
                        ins.then_inc(S(done), 1)
                    if between and lag in between:
                        between[lag]()
                dve.wait_ge(S(done), base + n)
                return base + n

            def low_part(full_, high, low):
                return tt(r32(low), full_, r32(high), ALU.subtract)

            dve.wait_ge(S("xt_high"), 1)
            low_part(slab[:, 0, :], slab[:, 8, :], slab[:, 9, :]).then_inc(S("xt_low"), 1)

            def take_v(u):
                dve.wait_ge(S("small_landed"), 16 * SMALL_LOADS)
                for t in range(TT):
                    o = wait_full(dve, f"v{u}_{t}")
                    read(tt(tok(6)[:, t, 512 * u:512 * u + 512], o[:], rows[:, 0, 512 * u:512 * u + 512], ALU.add),
                         f"v{u}_{t}")

            dve.wait_ge(S("cols_landed"), 16)
            glu_input([0, 1])
            z, la = half(5, 0), half(7, 1)

            def gate_negabs():
                wait_read(dve, "z0", "z1")
                stt(la, z, -1.0, z, ALU.mult, ALU.min).then_inc(S("negabs_ready"), 1)

            n = causal_conv(chan(2), chan(3), "conv_w", CONV_W, "conv_b", [(c, c, c) for c in range(4)],
                            "conv_tap", 0, between={GLU_LAG: lambda: glu_input([2, 3]), GATE_LAG: gate_negabs})
            dve.wait_ge(S("gate_ln"), 1)
            stt(z, z, 0.0, la, ALU.min, ALU.subtract).then_inc(S("gate_step"), 1)
            dve.wait_ge(S("gate_step"), 1)
            dve.wait_ge(S("consts_ready"), CONSTS)
            v.tensor_tensor_scan(slab[:, 4, 1024:2048], slab[:, 10, 1024:2048], slab[:, 5, 0:1024], 0.0,
                                 ALU.mult, ALU.add).then_inc(S("gate_step"), 1)
            dve.wait_ge(S("gate_step"), 2)
            cum = slab[:, 4, 1024:2048].rearrange("p (n t) -> p n t", t=CHUNK)
            tt(slab[:, 7, 1024:2048].rearrange("p (n t) -> p n t", t=CHUNK),
               cum[:, :, CHUNK - 1:CHUNK].broadcast_to([P, 16, CHUNK]), cum, ALU.subtract
               ).then_inc(S("toend_ready"), 1)
            causal_conv(chan(2), chan(3), "conv_w", CONV_W, "conv_b", [(c, c, c) for c in range(4, 8)],
                        "conv_tap", n, between={V_LAGS[0]: lambda: take_v(0), V_LAGS[1]: lambda: take_v(1)})
            dve.wait_ge(S("decay_ready"), 1)
            wait_read(dve, "k0", "k1")
            tt(half(5, 0), half(4, 0), la, ALU.mult).then_inc(S("kdec_ready"), 1)
            o = wait_full(dve, "csum")
            read(ts(mean, o[:, 0:T], -1.0 / D, None, ALU.mult), "csum")
            for t in range(TT):
                o = wait_full(dve, f"kdt{t}")
                read(v.tensor_copy(slab[:, 5, 1024 + 512 * t:1536 + 512 * t], o[:]), f"kdt{t}")
            wait_read(dve, "csum")
            for c in range(DC):
                tt(chan(3)[:, c, :], chan(3)[:, c, :], mean, ALU.add).then_inc(S("centered"), 1)
            dve.wait_ge(S("decay_ready"), 2)
            for n in range(NCH):
                for hp in range(2):
                    o = wait_full(dve, f"kv{2 * n + hp}")
                    if n:
                        wait_read(dve, f"kv{2 * n - 2 + hp}")
                    for m in range(2):
                        h = 2 * hp + m
                        if n == 0:
                            ins = v.tensor_copy(states(n, h), o[:, HV * m:HV * m + HV])
                        else:
                            ins = stt(states(n, h), states(n - 1, h), small[:, 4 * h + n:4 * h + n + 1],
                                      o[:, HV * m:HV * m + HV], ALU.mult, ALU.add)
                    read(ins, f"kv{2 * n + hp}")
            wait_read(dve, "csq")
            v.reciprocal(mean, conv_root).then_inc(S("conv_rstd"), 1)
            dve.wait_ge(S("conv_rstd"), 1)
            for c in range(DC):
                tt(chan(3)[:, c, :], chan(3)[:, c, :], mean, ALU.mult).then_inc(S("conv_normed"), 1)
            dve.wait_ge(S("conv_high"), 1)
            low_part(slab[:, 3, :], slab[:, 4, :], slab[:, 3, :]).then_inc(S("conv_low"), 1)
            for j in range(2):
                wait_read(dve, f"osum{j}")
            v.reciprocal(slab[:, 7, 1024:2048], slab[:, 7, 1024:2048]).then_inc(S("o_step"), 1)
            dve.wait_ge(S("o_step"), 1)
            for c in range(DC):
                ins = stt(chan(10)[:, c, :], chan(10)[:, c, :], col("gla_g", c), half(7, 1)[:, c // 2, :],
                          ALU.mult, ALU.mult)
            ins.then_inc(S("o_step"), 1)
            dve.wait_ge(S("o_step"), 2)
            wait_read(dve, "r0", "r1", "r2", "r3")
            tt(slab[:, 10, :], slab[:, 10, :], slab[:, 0, :], ALU.mult).then_inc(S("gla_ready"), 1)
            dve.wait_ge(S("gla_high"), 1)
            low_part(slab[:, 10, :], slab[:, 5, :], slab[:, 10, :]).then_inc(S("gla_low"), 1)
            wait_read(dve, "ga0", "ga1", "ga2", "ga3", "gb0", "gb1", "gb2", "gb3")
            for j in range(4):
                o = wait_full(dve, f"yc{j}")
                for m in range(2):
                    c = 2 * j + m
                    ins = stt(chan(1)[:, c, :], o[:, T * m:T * m + T], col("b_co", c), chan(1)[:, c, :],
                              ALU.add, ALU.mult)
                read(ins, f"yc{j}")
            for j in range(4):
                o = wait_full(dve, f"yg{j}")
                gb = slab[:, 6, 512 * j:512 * j + 512]
                mj = slab[:, 1, 512 * j:512 * j + 512]
                read(tt(gb, o[:], gb, ALU.mult), f"yg{j}")
                wait_read(dve, f"yg{j}", f"yc{j}")
                tt(mj, mj, gb, ALU.add).then_inc(S("merged_ready"), 1)
            for j in range(4):
                mj = slab[:, 1, 512 * j:512 * j + 512]
                dve.wait_ge(S("merged_high"), j + 1)
                low_part(mj, slab[:, 8, 512 * j:512 * j + 512], mj).then_inc(S("merged_low"), 1)
            dve.wait_ge(S("x_landed"), 16)
            dve.wait_ge(S("small_landed"), 16 * SMALL_LOADS)
            x = tok(2)
            for t in range(TT):
                stt(x[:, t, :], x[:, t, :], ALPHA, rows[:, 1, :], ALU.mult, ALU.add).then_inc(S("x_scaled"), 1)
            dve.wait_ge(S("x_scaled"), TT)

            def layer_norm(src, dst, t, g, b, at, std_at, done):
                k = done + t
                st = small[:, 160 + 12 * t:172 + 12 * t].rearrange("p (a b) -> p a b", a=2)
                for u in range(2):
                    v.bn_stats(st[:, u, :], src[u]).then_inc(S("ln_bn"), 1)
                dve.wait_ge(S("ln_bn"), 2 * k + 2)
                v.bn_aggr(small[:, at + 2 * t:at + 2 * t + 2], st).then_inc(S("ln_stats"), 1)
                dve.wait_ge(S("ln_stats"), k + 1)
                for u in range(2):
                    cut = slice(512 * u, 512 * u + 512)
                    stt(dst[:, t, cut], src[u], small[:, at + 2 * t:at + 2 * t + 1], g[:, cut], ALU.subtract, ALU.mult
                        ).then_inc(S("ln_a"), 1)
                dve.wait_ge(S("ln_std"), k + 1)
                rs = small[:, std_at + 2 + t:std_at + 3 + t]
                v.reciprocal(rs, small[:, std_at + t:std_at + t + 1]).then_inc(S("ln_rstd"), 1)
                dve.wait_ge(S("ln_rstd"), k + 1)
                dve.wait_ge(S("ln_a"), 2 * k + 2)
                return stt(dst[:, t, :], dst[:, t, :], rs, b, ALU.mult, ALU.add)

            dve.wait_ge(S("small_landed"), 16 * SMALL_LOADS)
            dve.wait_ge(S("ln1b_landed"), 16)
            for t in range(TT):
                for u in range(2):
                    o = wait_full(dve, f"mix{u}_{t}")
                    xs = x[:, t, 512 * u:512 * u + 512]
                    read(tt(xs, xs, o[:], ALU.add), f"mix{u}_{t}")
                wait_read(dve, f"mix0_{t}", f"mix1_{t}")
                layer_norm([x[:, t, 0:512], x[:, t, 512:1024]], tok(0), t, rows[:, 2, :], rows[:, 0, :], 16, 20, 0).then_inc(S("x1_ready"), 1)
            dve.wait_ge(S("x1_ready"), TT)
            v.memset(zeros, 0.0).then_inc(S("zeros_ready"), 1)
            dve.wait_ge(S("small_landed"), 16 * SMALL_LOADS)
            o = wait_full(dve, "lg")
            for t in range(TT):
                ins = tt(logit[:, t, :], o[:, 128 * t:128 * t + 72], b_route[:], ALU.add)
            read(ins, "lg")
            wait_read(dve, "lg")
            dve.wait_ge(S("consts_ready"), CONSTS)
            for t in range(TT):
                v.max(g_top[:, t, :], logit[:, t, 0:NG]).then_inc(S("route_step"), 1)
            dve.wait_ge(S("route_step"), 2)
            for t in range(TT):
                v.max_index(g_idx[:, t, :], g_top[:, t, :], logit[:, t, 0:NG]).then_inc(S("route_step"), 1)
            for t in range(TT):
                ts(small[:, 30 + t:31 + t], g_top[:, t, 0:1], -1.0, None, ALU.mult).then_inc(S("gtop_ready"), 1)
            dve.wait_ge(S("route_step"), 4)
            gi = small[:, 38:40]
            v.tensor_copy(gi, g_idx[:, :, 0:1].rearrange("p t a -> p (t a)")).then_inc(S("route_step"), 1)
            dve.wait_ge(S("route_step"), 5)
            for t in range(TT):
                ts(onehot[:, t, :], numbers[:, 0:NG], gi[:, t:t + 1], None, ALU.is_equal).then_inc(S("route_step"), 1)
            dve.wait_ge(S("route_step"), 7)
            for t in range(TT):
                tt(picked[:, t, :, :], logit[:, t, NG:].rearrange("p (g i) -> p i g", g=NG),
                   onehot[:, t:t + 1, :].broadcast_to([P, EPG, NG]), ALU.mult).then_inc(S("route_step"), 1)
            dve.wait_ge(S("route_step"), 9)
            for t in range(TT):
                v.tensor_reduce(e_log[:, t, :], picked[:, t, :, :], AX_X, ALU.add).then_inc(S("route_step"), 1)
            dve.wait_ge(S("route_step"), 11)
            for t in range(TT):
                v.max(e_top[:, t, :], e_log[:, t, :]).then_inc(S("route_step"), 1)
            dve.wait_ge(S("route_step"), 13)
            for t in range(TT):
                v.max_index(e_idx[:, t, :], e_top[:, t, :], e_log[:, t, :]).then_inc(S("route_step"), 1)
            tt(small[:, 34:36], e_top[:, :, 1:2].rearrange("p t a -> p (t a)"),
               e_top[:, :, 0:1].rearrange("p t a -> p (t a)"), ALU.subtract).then_inc(S("ediff_ready"), 1)
            dve.wait_ge(S("route_step"), 15)
            ef = small[:, 156:160]
            v.tensor_copy(ef.rearrange("p (t a) -> p t a", t=TT), e_idx[:, :, 0:2]).then_inc(S("route_step"), 1)
            dve.wait_ge(S("route_step"), 16)
            for t in range(TT):
                stt(small[:, 184 + 2 * t:186 + 2 * t], gi[:, t:t + 1].broadcast_to([P, 2]), float(EPG),
                    ef[:, 2 * t:2 * t + 2], ALU.mult, ALU.add).then_inc(S("route_step"), 1)
            dve.wait_ge(S("route_step"), 18)
            for t in range(TT):
                ts(mask_a[:, t, :], numbers[:], small[:, 184 + 2 * t:185 + 2 * t], None, ALU.is_equal
                   ).then_inc(S("route_step"), 1)
                ts(mask_b[:, t, :], numbers[:], small[:, 185 + 2 * t:186 + 2 * t], None, ALU.is_equal
                   ).then_inc(S("route_step"), 1)
            dve.wait_ge(S("route_step"), 22)
            tt(mask, mask_a, mask_b, ALU.add).then_inc(S("mask_ready"), 1)
            dve.wait_ge(S("ratio_ready"), 1)
            dve.wait_ge(S("gsum_ready"), TT)
            den, w0, w1 = small[:, 188:190], small[:, 190:192], small[:, 24:26]
            stt(den, small[:, 36:38], 1.0, small[:, 32:34], ALU.add, ALU.mult).then_inc(S("route_step"), 1)
            dve.wait_ge(S("route_step"), 23)
            v.reciprocal(w0, den).then_inc(S("route_step"), 1)
            dve.wait_ge(S("route_step"), 24)
            tt(w1, w0, small[:, 36:38], ALU.mult).then_inc(S("route_step"), 1)
            dve.wait_ge(S("route_step"), 25)
            dve.wait_ge(S("consts_ready"), CONSTS)
            for t in range(TT):
                ts(mask_a[:, t, :], mask_a[:, t, :], w0[:, t:t + 1], None, ALU.mult).then_inc(S("route_step"), 1)
            dve.wait_ge(S("route_step"), 27)
            for t in range(TT):
                wt = meta[:, 0:NE, 2 + t:3 + t].rearrange("p n a -> p (n a)")
                stt(wt, mask_b[:, t, :], w1[:, t:t + 1], mask_a[:, t, :], ALU.mult, ALU.add
                    ).then_inc(S("route_step"), 1)
            o = wait_full(dve, "pos")
            stt(slotted, o[:, 0:128], 1.0, mask.rearrange("p t n -> p (t n)"), ALU.add, ALU.mult
                ).then_inc(S("route_step"), 1)
            v.tensor_reduce(small[:, 26:27], o[:, 128:192], AX_X, ALU.max).then_inc(S("route_step"), 1)
            dve.wait_ge(S("route_step"), 31)
            read(ts(over[:], small[:, 26:27], float(CAP), None, ALU.is_gt), "pos")
            v.memset(spread[:, 1, :], 0.0).then_inc(S("spread_copied"), 1)
            v.memset(y_sb[:, 1, 512:1024], 0.0).then_inc(S("y1_copied"), 1)
            dve.wait_ge(S("route_step"), 31)
            ts(meta[:, 0:NE, 0:2].rearrange("p n t -> p t n"), slotted.rearrange("p (t n) -> p t n", t=TT),
               -1.0, None, ALU.add).then_inc(S("meta_ready"), 1)

            def select(f, par, r):
                m = meta[:, bass.ds(f, 1), :] if not isinstance(f, int) else meta[:, f:f + 1, :]
                v.tensor_copy(meta_f[:, par, :], m.rearrange("p a b -> p (a b)")).then_inc(S("metaf_ready"), 1)
                dve.wait_ge(S("metaf_ready"), r * META + f + 1)
                for t in range(TT):
                    ts(sel[:, par, t, :], slots[:, 0:CAP], meta_f[:, par, t:t + 1], None,
                       ALU.is_equal).then_inc(S("sel_ready"), 1)
                for t in range(TT):
                    ts(selw[:, par, t, :], slots[:], meta_f[:, par, t:t + 1], meta_f[:, par, 2 + t:3 + t],
                       ALU.is_equal, ALU.mult).then_inc(S("selw_ready"), 1)

            def expert(e, q, r):
                n = r * NE + e
                dve.wait_ge(S("up_full"), n + 1)
                v.tensor_copy(u_sb, up_bank[:]).then_inc(S("u_copied"), 1)
                dve.wait_ge(S("spread_full"), n + 1)
                v.tensor_copy(spread[:, q, :], y_bank[:, 0:256]).then_inc(S("spread_copied"), 1)
                dve.wait_ge(S("silu_ready"), n + 1)
                tt(slab[:, 1, 1664:1792], slab[:, 1, 1536:1664], gate_bank[:, 128:256], ALU.mult
                   ).then_inc(S("h_ready"), 1)
                dve.wait_ge(S("y1_full"), n + 1)
                v.tensor_copy(y_sb[:, q, 512:1024], up_bank[:]).then_inc(S("y1_copied"), 1)
                select(e + 2, q, r)

            dve.wait_ge(S("meta_ready"), 1)
            dve.wait_ge(S("consts_ready"), CONSTS)
            for f in range(2):
                select(f, f, 0)
            with dve.Fori(0, NE // 2) as it:
                for q in range(2):
                    expert(2 * it + q, q, 0)
            more = dve.value_load(over[0:1, 0:1], min_val=0, max_val=1)
            with dve.If(more > 0):
                with dve.Fori(1, ROUNDS) as r:
                    dve.wait_ge(S("combined"), r * (NE + 1) - 1)
                    ts(meta[:, :, 0:TT], meta[:, :, 0:TT], -float(CAP), None, ALU.add).then_inc(S("meta_moved"), 1)
                    dve.wait_ge(S("meta_moved"), r)
                    for f in range(2):
                        select(f, f, r)
                    v.memset(spread[:, 1, :], 0.0).then_inc(S("spread_copied"), 1)
                    v.memset(y_sb[:, 1, 512:1024], 0.0).then_inc(S("y1_copied"), 1)
                    with dve.Fori(0, NE // 2) as it:
                        for q in range(2):
                            expert(2 * it + q, q, r)
                dve.wait_ge(S("combined"), ROUNDS * (NE + 1) - 1)
            dve.wait_ge(S("combined"), NE)
            dve.wait_ge(S("ln2_landed"), 32)
            for t in range(TT):
                layer_norm([acc[t][hf][:] for hf in range(2)], tok(10), t, rows[:, 1, :], rows[:, 2, :], 42, 46, TT
                           ).then_inc(S("x2_ready"), 1)

            def rms_inverses(done, at):
                for t in range(TT):
                    dve.wait_ge(S("rms_root"), done + t + 1)
                    rs = small[:, at + 2 + t:at + 3 + t]
                    v.reciprocal(rs, rs).then_inc(S("rms_inverse"), 1)

            def low_turned(tasks, gain, done):
                for i, task in enumerate(tasks):
                    o = wait_full(dve, task)
                    dve.wait_ge(S("xn_high"), done + i + 1)
                    t, k = divmod(i, 2)
                    for m in range(4):
                        c = 4 * k + m
                        ins = stt(r32(xn_parts[1][:, c, P * t:P * t + P]), o[:, P * m:P * m + P], col(gain, c),
                                  r32(xn_parts[0][:, c, P * t:P * t + P]), ALU.mult, ALU.subtract)
                    read(ins, task)

            rms_inverses(0, 50)
            low_turned([f"x2t{j}" for j in range(4)], "mix_norm", 0)
            lam = cols[:, COLS["lam"]:COLS["lam"] + 8]
            stt(small[:, 72:80], lam, -1.0, lam, ALU.mult, ALU.min).then_inc(S("lam_negabs"), 1)
            dve.wait_ge(S("lam_exp"), 1)
            e_, d_, s_, s2, pl = (small[:, 80 + 8 * i:88 + 8 * i] for i in range(5))
            ts(d_, e_, 2.0, None, ALU.add).then_inc(S("rate_step"), 1)
            dve.wait_ge(S("rate_step"), 1)
            v.reciprocal(d_, d_).then_inc(S("rate_step"), 1)
            dve.wait_ge(S("rate_step"), 2)
            tt(s_, e_, d_, ALU.mult).then_inc(S("rate_step"), 1)
            dve.wait_ge(S("rate_step"), 3)
            tt(s2, s_, s_, ALU.mult).then_inc(S("rate_step"), 1)
            dve.wait_ge(S("rate_step"), 4)
            ts(pl, s2, 1.0 / 17, 1.0 / 15, ALU.mult, ALU.add).then_inc(S("rate_step"), 1)
            n = 5
            for k in (13, 11, 9, 7, 5, 3, 1):
                dve.wait_ge(S("rate_step"), n)
                tt(pl, pl, s2, ALU.mult).then_inc(S("rate_step"), 1)
                dve.wait_ge(S("rate_step"), n + 1)
                ts(pl, pl, 1.0 / k, None, ALU.add).then_inc(S("rate_step"), 1)
                n += 2
            dve.wait_ge(S("rate_step"), n)
            tt(pl, pl, s_, ALU.mult).then_inc(S("rate_step"), 1)
            ts(d_, lam, -1.0, 0.0, ALU.mult, ALU.max).then_inc(S("rate_step"), 1)
            dve.wait_ge(S("rate_step"), n + 2)
            stt(pl, pl, 2.0, d_, ALU.mult, ALU.add).then_inc(S("rate_step"), 1)
            dve.wait_ge(S("rate_step"), n + 3)
            ts(pl, pl, -8.0, None, ALU.mult).then_inc(S("rate_ready"), 1)
            for j in range(4):
                wait_read(dve, f"lx{j}")
                causal_conv(chan(1), chan(2), "lru_w", LRU_W, "lru_b", [(2 * j + m,) * 3 for m in range(2)],
                            "lru_tap", 2 * LRU_W * j)
            wait_read(dve, "kiwi_w")
            steps = 0
            for t in range(TT):
                n = P * (t + 1)
                rel_t = rel[t].rearrange("p (h s) -> p h s", h=IH)
                for h in range(IH):
                    if h % 2 == 0:
                        wait_read(dve, f"dots{t}_{h // 2}")
                    w = indexer_head(h // 2, h % 2)
                    sc = score[:, t, 0:n]
                    if h == 0:
                        ins = ts(sc, rel_t[:, h, 0:n], wih[:, t, w:w + 1], None, ALU.mult)
                    else:
                        dve.wait_ge(S("score_step"), steps)
                        ins = stt(sc, rel_t[:, h, 0:n], wih[:, t, w:w + 1], sc, ALU.mult, ALU.add)
                    if h < IH - 1:
                        ins.then_inc(S("score_step"), 1)
                        steps += 1
                    else:
                        ins.then_inc(S("score_ready"), 1)
            def best_keys(t):
                n = P * (t + 1)
                steps = 2 * t * (TOPK // 8)
                w_ = work[:, t, 0:n]
                dve.wait_ge(S("work_ready"), t + 1)
                for i in range(TOPK // 8):
                    if steps:
                        dve.wait_ge(S("top_step"), steps)
                    v.max(best, w_).then_inc(S("top_step"), 1)
                    dve.wait_ge(S("top_step"), steps + 1)
                    v.match_replace(w_, best, w_, TAKEN).then_inc(S("top_step"), 1)
                    steps += 2
                dve.wait_ge(S("top_step"), steps)
                ts(score[:, t, 0:n], w_, 2.0 * FILL, HIDE, ALU.is_gt, ALU.mult).then_inc(S("hide_made"), 1)
            best_keys(0)
            wait_read(dve, "li0", "li1", "li2", "li3")
            tt(slab[:, 5, :], slab[:, 5, :], slab[:, 2, :], ALU.mult).then_inc(S("ua_used"), 1)
            dve.wait_ge(S("a_ready"), 1)
            tt(slab[:, 1, :], slab[:, 4, :], slab[:, 4, :], ALU.mult).then_inc(S("a_step"), 1)
            dve.wait_ge(S("a_step"), 1)
            stt(slab[:, 6, :], slab[:, 1, :], 1.0, slab[:, 6, :], ALU.add, ALU.mult).then_inc(S("mult2_ready"), 1)
            dve.wait_ge(S("a_step"), 1)
            v.memset(chan(4)[:, :, 0:1], 0.0).then_inc(S("a_step"), 1)
            best_keys(1)
            dve.wait_ge(S("mult_ready"), 1)
            dve.wait_ge(S("ua_used"), 1)
            tt(slab[:, 5, :], slab[:, 5, :], slab[:, 6, :], ALU.mult).then_inc(S("u_ready"), 1)
            dve.wait_ge(S("u_ready"), 1)
            dve.wait_ge(S("a_step"), 2)
            v.tensor_tensor_scan(slab[:, 1, :], slab[:, 4, :], slab[:, 5, :], 0.0, ALU.mult, ALU.add
                                 ).then_inc(S("lru_done"), 1)
            dve.wait_ge(S("lru_done"), 1)
            wait_read(dve, "lg_0", "lg_1", "lg_2", "lg_3")
            tt(slab[:, 1, :], slab[:, 1, :], slab[:, 3, :], ALU.mult).then_inc(S("ya_ready"), 1)
            dve.wait_ge(S("lru_high"), 1)
            low_part(slab[:, 1, :], slab[:, 5, :], slab[:, 1, :]).then_inc(S("lru_low"), 1)
            wait_read(dve, "ksum")
            v.reciprocal(k_sq, k_sq).then_inc(S("qk_step"), 1)
            dve.wait_ge(S("qk_step"), 1)
            stt(slab[:, 7, 0:512], slab[:, 7, 0:512], col("k_norm"), k_sq, ALU.mult, ALU.mult
                ).then_inc(S("k_ready"), 1)
            for j in range(4):
                wait_read(dve, f"qsum{j}")
                r6 = slab[:, 6, 512 * j:512 * j + 512]
                q9 = slab[:, 9, 512 * j:512 * j + 512]
                v.reciprocal(r6, r6).then_inc(S("qk_step"), 1)
                dve.wait_ge(S("qk_step"), j + 2)
                stt(q9, q9, col("q_norm"), r6, ALU.mult, ALU.mult).then_inc(S("q_ready"), 1)
            def take_lru(js):
                for j in js:
                    wait_read(dve, f"gc{j}")
                    o = wait_full(dve, f"ya{j}")
                    m3 = slab[:, 3, 512 * j:512 * j + 512]
                    read(tt(m3, o[:], m3, ALU.mult), f"ya{j}")

            take_lru([0, 1])
            for t in range(TT):
                n = P * (t + 1)
                dve.wait_ge(S("bias_landed"), 16 * (t + 1))
                dve.wait_ge(S("hide_ready"), t + 1)
                if t:
                    for k in range(2):
                        wait_full(dve, f"pt0_0_{k}")
                for j in range(4):
                    o = wait_full(dve, f"log{t}_{j}")
                    dst = lgt[:, 2 * j:2 * j + 2, 0:n]
                    bias = slab[:, 2, 512 * j:512 * j + 512].rearrange("p (m s) -> p m s", m=2)[:, :, ::-1][:, :, 0:n]
                    read(stt(dst, o[:].rearrange("p (m s) -> p m s", m=2)[:, :, 0:n], HD ** -0.5, bias,
                             ALU.mult, ALU.add), f"log{t}_{j}")
                    wait_read(dve, f"log{t}_{j}")
                    tt(dst, dst, score[:, t:t + 1, 0:n].broadcast_to([P, 2, n]), ALU.add
                       ).then_inc(S("logits_ready"), 1)
                dve.wait_ge(S("logits_ready"), 4 * (t + 1))
                v.tensor_reduce(small[:, 128:136], lgt[:, :, 0:n], AX_X, ALU.max).then_inc(S("rowmax"), 1)
                dve.wait_ge(S("rowmax"), t + 1)
                ts(small[:, 128:136], small[:, 128:136], -1.0, None, ALU.mult).then_inc(S("rowmax_ready"), 1)
                if t:
                    take_lru([2, 3])
                dve.wait_ge(S("exp_ready"), t + 1)
                v.reciprocal(small[:, 136:144], small[:, 136:144]).then_inc(S("rowsum"), 1)
                dve.wait_ge(S("rowsum"), t + 1)
                tt(lgt[:, :, 0:n], lgt[:, :, 0:n],
                   small[:, 136:144].rearrange("p (h a) -> p h a", a=1).broadcast_to([P, NH, n]), ALU.mult
                   ).then_inc(S("probs_ready"), 1)
            for h in range(2):
                dve.wait_ge(S("att_high"), h + 1)
                s6 = slab[:, 6, 1024 * h:1024 * h + 1024]
                low_part(s6, slab[:, 9, 1024 * h:1024 * h + 1024], s6).then_inc(S("att_low"), 1)
            wait_read(dve, "gd0", "gd1", "gd2", "gd3")
            for j in range(4):
                o = wait_full(dve, f"yb{j}")
                g1 = slab[:, 1, 512 * j:512 * j + 512]
                m3 = slab[:, 3, 512 * j:512 * j + 512]
                read(tt(g1, o[:], g1, ALU.mult), f"yb{j}")
                wait_read(dve, f"yb{j}", f"ya{j}")
                tt(m3, m3, g1, ALU.add).then_inc(S("merged2_ready"), 1)
            for j in range(4):
                m3 = slab[:, 3, 512 * j:512 * j + 512]
                dve.wait_ge(S("merged2_high"), j + 1)
                low_part(m3, slab[:, 7, 512 * j:512 * j + 512], m3).then_inc(S("merged2_low"), 1)

            def residual(pre, by_tile):
                for i in range(2):
                    for j in range(2):
                        u, t = (j, i) if by_tile else (i, j)
                        o = wait_full(dve, f"{pre}{u}_{t}")
                        xs = tok(10)[:, t, 512 * u:512 * u + 512]
                        read(tt(xs, xs, o[:], ALU.add), f"{pre}{u}_{t}")

            residual("mo", True)
            rms_inverses(TT, 54)
            low_turned([f"x3t{j}" for j in range(4)], "ffn_norm", 4)
            def hidden_low(i):
                dve.wait_ge(S("hid_high"), i + 1)
                tt(r32(hid_parts[1][:, 4 * i:4 * i + 4, :]), half(5, i % 2), r32(hT[:, 4 * i:4 * i + 4, :]),
                   ALU.subtract).then_inc(S("hid_low"), 1)

            for i in range(6):
                wait_read(dve, f"fg{i}_0", f"fg{i}_1")
                if i == 0:
                    wait_read(dve, "x3t3")
                if i >= 2:
                    dve.wait_ge(S("hid_low"), i - 1)
                causal_conv(half(4, i % 2), half(5, i % 2), "ffn_w", FFN_W, "ffn_b",
                            [(c, c, 4 * i + c) for c in range(4)], "ffn_tap", 4 * FFN_W * i)
                if i:
                    hidden_low(i - 1)
                dve.wait_ge(S("fgelu_ready"), i + 1)
                for j in range(2):
                    o = wait_full(dve, f"fu{i}_{j}")
                    hj = half(5, i % 2)[:, 2 * j:2 * j + 2, :].rearrange("p a t -> p (a t)")
                    read(tt(hj, o[:], hj, ALU.mult), f"fu{i}_{j}")
            hidden_low(5)
            residual("dn", False)
            rms_inverses(2 * TT, 62)
            low_turned([f"x4t{j}" for j in range(4)], "ple_norm", 8)
            for u in range(2):
                for t in range(TT):
                    o = wait_full(dve, f"pp{u}_{t}")
                    read(v.tensor_copy(tok(5)[:, t, 512 * u:512 * u + 512], o[:]), f"pp{u}_{t}")
            for t in range(TT):
                for u in range(2):
                    wait_read(dve, f"pg{u}_{t}", f"pp{u}_{t}")
                    gate = tok(4)[:, t, 512 * u:512 * u + 512]
                    tt(gate, gate, tok(5)[:, t, 512 * u:512 * u + 512], ALU.mult).then_inc(S("ple_step"), 1)
                    dve.wait_ge(S("ple_step"), 2 * t + u + 1)
                    xs = tok(10)[:, t, 512 * u:512 * u + 512]
                    tt(xs, xs, gate, ALU.add).then_inc(S("out_ready"), 1)


def _bucket_rows():
    dist = np.maximum(np.arange(511) - (T - 1), 0)
    exact = NB // 2
    far = exact + (np.log(np.maximum(dist, 1).astype(np.float32) / exact) / np.float32(np.log(MAXD / exact))
                   * (NB - exact)).astype(np.int32)
    bucket = np.where(dist < exact, dist, np.minimum(far, NB - 1))
    return (np.arange(NB)[:, None] == bucket[None, :]).astype(np.float32)


def _unit(w):
    return w.reshape(-1, P, w.shape[1]).transpose(1, 0, 2).reshape(P, -1)


def _layout(i):
    f = {k: np.asarray(v) for k, v in i.items()}
    w_in, b_in = f["w_in"][0], f["b_in"][0]
    at = np.cumsum([0, D, D, 512, 512, D, D, RANK, D, D])
    ca, cg, q, k, vv, r, fl, ga, gb = (w_in[:, at[j]:at[j + 1]] for j in range(9))
    bca, bcg, bq, bk, bv, br, bfl, bga, bgb = (b_in[at[j]:at[j + 1]] for j in range(9))

    def two(w):
        return [w[:, 0:512], w[:, 512:1024]]

    first = [cg[:, :512], ca[:, :512], cg[:, 512:], ca[:, 512:], k] + two(vv) + [q] + two(r) + two(ga) + two(gb)
    first += two(f["w_conv_out"][0]) + two(f["w_gla_out"][0]) + two(f["w_out"][0])
    units1 = np.stack([_unit(w) for w in first])

    w2 = f["w_in_2"][0]
    at = np.cumsum([0, D, D, D, 256, 256, 512, 64, 8, D, D])
    lx, lg, q2, k2, v2, qi, ki, wi, gc, gd = (w2[:, at[j]:at[j + 1]] for j in range(10))
    up = f["w_up_2"][0]
    down = f["w_down_2"][0]
    second = two(lx) + two(lg) + [np.concatenate([k2, v2], 1), qi]
    units2 = [_unit(w) for w in second]
    units2.append(np.concatenate([f["lru_wa_2"][0], f["lru_wx_2"][0]]).transpose(1, 0, 2).reshape(P, -1))
    units2 += [_unit(w) for w in two(q2) + two(gc) + two(f["w_lru_br_2"][0]) + two(gd) + two(f["w_attn_br_2"][0])
               + two(f["w_out_2"][0])]
    for j in range(6):
        units2 += [_unit(up[:, 512 * j:512 * j + 512]), _unit(up[:, FF + 512 * j:FF + 512 * j + 512])]
    for u in range(2):
        for j in range(3):
            units2.append(_unit(down[D * j:D * j + D, 512 * u:512 * u + 512]))
    units2.append(_unit(f["w_ple_proj_2"][0]))
    units2 += [_unit(w) for w in two(f["w_ple_gate_2"][0])]
    full2 = np.zeros((len(units2), P, UNIT), np.float32)
    for j, w in enumerate(units2):
        full2[j, :, :w.shape[1]] = w

    def per_channel(x):
        return x.reshape(-1, P).T

    cols = np.zeros((P, NCOLS), np.float32)

    def put(name, x):
        cols[:x.shape[0], COLS[name]:COLS[name] + x.shape[1]] = x

    for name, x in (("b_conv_a", bca), ("b_conv_g", bcg), ("b_q", bq), ("b_k", bk), ("b_r", br), ("b_ga", bga),
                    ("b_gb", bgb), ("conv_b", f["conv_b"]), ("cln_g", f["conv_ln_g"]), ("cln_b", f["conv_ln_b"]),
                    ("b_co", f["b_conv_out"]), ("b_gate", f["b_gate_up"]), ("gla_g", f["gla_norm_g"]),
                    ("mix_norm", f["mix_norm_2"]), ("lru_b", f["lru_conv_b_2"]), ("lru_ba", f["lru_ba_2"]),
                    ("lru_bx", f["lru_bx_2"]), ("lam", f["lru_lambda_2"]), ("q_norm", f["q_norm_2"]),
                    ("k_norm", f["k_norm_2"]), ("ffn_norm", f["ffn_norm_2"]), ("ffn_b", f["ffn_conv_b_2"]),
                    ("ple_norm", f["ple_norm_2"])):
        put(name, per_channel(x))
    put("b_flr", bfl[:, None])
    for name, x in (("conv_w", f["conv_w"]), ("lru_w", f["lru_conv_w_2"]), ("ffn_w", f["ffn_conv_w_2"])):
        put(name, x[0].reshape(x.shape[1], -1, P).transpose(2, 1, 0).reshape(P, -1))

    route = np.concatenate([f["w_router_group"][0], f["w_router_expert"][0]], 1)
    return {
        "xT": np.ascontiguousarray(_unit(f["x"][0].T)), "x": f["x"],
        "cols": cols, "units1": units1, "units2": full2,
        "w1": f["w1"][0], "w3": f["w3"][0], "w2": f["w2"][0],
        "w_flr": np.ascontiguousarray(_unit(fl).reshape(P, DC, RANK)), "w_gate_up": f["w_gate_up"][0],
        "b_v": bv, "b_out": f["b_out"][0], "ln1_g": f["ln1_g"][0], "ln1_b": f["ln1_b"][0],
        "ln2_g": f["ln2_g"][0], "ln2_b": f["ln2_b"][0],
        "w_route": np.ascontiguousarray(_unit(route).reshape(P, DC, NG + NE)),
        "b_route": np.concatenate([f["b_router_group"][0], f["b_router_expert"][0]]),
        "w_kiwi": np.ascontiguousarray(_unit(np.concatenate([ki, ki, wi], 1))),
        "rel_bias": f["rel_bias_2"], "buckets": _bucket_rows(),
        "pT": np.ascontiguousarray(_unit(f["p_2"][0, 0].T)),
    }


def kernel(**inputs):
    import concourse.bacc as bacc
    from concourse.bass_utils import run_bass_kernel_spmd

    nc = bacc.Bacc("TRN2", target_bir_lowering=False, num_devices=1)
    arrays, aps = {}, {}
    for name, x in _layout(inputs).items():
        x = np.ascontiguousarray(x)
        arrays[f"in_{name}"] = x
        aps[name] = nc.dram_tensor(f"in_{name}", x.shape, mybir.dt.from_np(x.dtype), kind="ExternalInput").ap()
    out = nc.dram_tensor("out", (1, T, D), F32, kind="ExternalOutput").ap()
    build(nc, aps, out)
    return run_bass_kernel_spmd(nc, [arrays], core_ids=[0]).results[0]["out"]
```
